# Optimizing a Trainium2 kernel written in Bass

```python
import math
import jax
import jax.numpy as jnp
from jax import lax
import numpy as np

D_MODEL = 1024
BATCH = 1
SEQ = 256
DEPTH = 2
DEC_BATCH = 8
DEC_SEQ = 1
PAST_LEN = 2048
PAGE_SIZE = 128

F32 = jnp.float32
EPS = 1e-6
CHUNK = 128
N_EVEN = (DEPTH + 1) // 2
N_ODD = DEPTH // 2
D_FF = 2816
SSD_D_INNER = 2 * D_MODEL
SSD_HEAD_DIM = 64
SSD_HEADS = SSD_D_INNER // SSD_HEAD_DIM
SSD_GROUPS = 4
SSD_D_STATE = 128
SSD_CONV = 4
SSD_CONV_CH = SSD_D_INNER + 2 * SSD_GROUPS * SSD_D_STATE
RET_HEADS = 4
RET_QK = D_MODEL
RET_V = 2 * D_MODEL
RET_DK = RET_QK // RET_HEADS
RET_DV = RET_V // RET_HEADS
ROPE_BASE = 10000.0
AB_SIZES = (SSD_D_INNER, SSD_CONV_CH, SSD_HEADS, RET_QK, RET_QK, RET_V, RET_V)
IN_AB = sum(AB_SIZES)
M_HEADS = 4
M_QK = D_MODEL // 2
M_V = D_MODEL
M_DK = M_QK // M_HEADS
M_DV = M_V // M_HEADS
C_SIZES = (M_QK, M_QK, M_V, M_HEADS, M_HEADS, M_V)
IN_C = sum(C_SIZES)
MEM_LEN = 256
X_HEADS = 4
X_HEAD_DIM = D_MODEL // X_HEADS

kernel_name = 'hybrid_ssd_retention_mlstm_macaron_step'

def _split(a, sizes):
    return jnp.split(a, np.cumsum(sizes)[:-1].tolist(), axis=-1)

def _to_chunks(a, c):
    b, l = a.shape[:2]
    return jnp.moveaxis(a.reshape(b, l // c, c, *a.shape[2:]), 1, 0)

def _from_chunks(a):
    n, b, c = a.shape[:3]
    return jnp.moveaxis(a, 0, 1).reshape(b, n * c, *a.shape[3:])

def group_rms(x, groups):
    shp = x.shape
    xf = x.astype(F32).reshape(*shp[:-1], groups, shp[-1] // groups)
    xf = xf * lax.rsqrt(jnp.mean(xf * xf, axis=-1, keepdims=True) + EPS)
    return xf.reshape(shp).astype(x.dtype)

def rmsnorm(x, g):
    return group_rms(x, 1) * g

def swiglu(x, w_in, w_out):
    g, u = jnp.split(x @ w_in, 2, axis=-1)
    return (jax.nn.silu(g) * u) @ w_out

def rotary(x, pos):
    half = x.shape[-1] // 2
    inv = jnp.exp(-math.log(ROPE_BASE) * jnp.arange(half, dtype=F32) / half)
    ang = pos.astype(F32)[:, None] * inv
    cos = jnp.cos(ang)[None, :, None, :]
    sin = jnp.sin(ang)[None, :, None, :]
    xf = x.astype(F32)
    x1, x2 = xf[..., :half], xf[..., half:]
    return jnp.concatenate([x1 * cos - x2 * sin, x1 * sin + x2 * cos], axis=-1).astype(x.dtype)

def causal_conv(u, buf, w, b):
    l = u.shape[1]
    full = jnp.concatenate([buf.astype(u.dtype), u], axis=1)
    out = b + sum(full[:, j:j + l] * w[j] for j in range(SSD_CONV))
    return out, full[:, l:]

def ssd_scan(x, dt, a, bm, cm, h0):
    bsz, l, nh, hp = x.shape
    g = SSD_GROUPS
    r = nh // g
    ns = bm.shape[-1]
    c = math.gcd(l, CHUNK)
    dt = dt.astype(F32)
    da = (dt * a.astype(F32)).reshape(bsz, l, g, r)
    xdt = x.astype(F32).reshape(bsz, l, g, r, hp) * dt.reshape(bsz, l, g, r)[..., None]
    mask = jnp.tril(jnp.ones((c, c), bool))[None, :, :, None, None]

    def step(h, inp):
        xc, dac, bc, cc = inp
        cs = jnp.cumsum(dac, axis=1)
        seg = cs[:, :, None] - cs[:, None, :]
        decay = jnp.exp(jnp.where(mask, seg, -jnp.inf))
        att = jnp.einsum('btgn,bsgn->btsg', cc, bc)[..., None] * decay
        y = jnp.einsum('btsgr,bsgrp->btgrp', att, xc)
        y = y + jnp.einsum('btgn,bgrpn->btgrp', cc, h) * jnp.exp(cs)[..., None]
        last = cs[:, -1]
        w = jnp.exp(last[:, None] - cs)
        h = h * jnp.exp(last)[..., None, None] + jnp.einsum('bsgr,bsgrp,bsgn->bgrpn', w, xc, bc)
        return h, y

    h_init = h0.astype(F32).reshape(bsz, g, r, hp, ns)
    hT, ys = lax.scan(step, h_init, (_to_chunks(xdt, c), _to_chunks(da, c),
                                     _to_chunks(bm.astype(F32), c), _to_chunks(cm.astype(F32), c)))
    y = _from_chunks(ys).reshape(bsz, l, nh, hp)
    return y.astype(x.dtype), hT.reshape(bsz, nh, hp, ns).astype(h0.dtype)

def retention_scan(q, k, v, s0):
    bsz, l, nh, dk = q.shape
    c = math.gcd(l, CHUNK)
    lg = jnp.log1p(-jnp.exp2(-5.0 - jnp.arange(nh, dtype=F32)))
    idx = jnp.arange(c, dtype=F32)
    diff = idx[:, None] - idx[None, :]
    decay = jnp.exp(jnp.where((diff >= 0)[..., None], diff[..., None] * lg, -jnp.inf))
    inner = jnp.exp((idx[:, None] + 1.0) * lg)
    tail = jnp.exp((c - 1.0 - idx)[:, None] * lg)
    carry_decay = jnp.exp(c * lg)

    def step(s, inp):
        qc, kc, vc = inp
        att = jnp.einsum('bthd,bshd->btsh', qc, kc) * decay
        y = jnp.einsum('btsh,bshe->bthe', att, vc) + jnp.einsum('bthd,bhde->bthe', qc, s) * inner[:, :, None]
        s = s * carry_decay[:, None, None] + jnp.einsum('bshd,sh,bshe->bhde', kc, tail, vc)
        return s, y

    sT, ys = lax.scan(step, s0.astype(F32), (_to_chunks(q.astype(F32), c), _to_chunks(k.astype(F32), c),
                                            _to_chunks(v.astype(F32), c)))
    return _from_chunks(ys).astype(v.dtype), sT.astype(s0.dtype)

def mlstm_scan(q, k, v, i_pre, f_pre, c0, n0, m0):
    bsz, l, nh, dk = q.shape
    c = math.gcd(l, CHUNK)
    mask = jnp.tril(jnp.ones((c, c), bool))[None, :, :, None]
    logf = jax.nn.log_sigmoid(f_pre.astype(F32))

    def step(carry, inp):
        cmat, nvec, m = carry
        qc, kc, vc, ic, lfc = inp
        b = jnp.cumsum(lfc, axis=1)
        g = ic - b
        mt = b + jnp.maximum(m[:, None], lax.cummax(g, axis=1))
        w = jnp.exp(jnp.where(mask, g[:, None] + (b - mt)[:, :, None], -jnp.inf))
        a = jnp.einsum('bthd,bshd->btsh', qc, kc) * w
        inter = jnp.exp(b + m[:, None] - mt)
        num = jnp.einsum('btsh,bshe->bthe', a, vc) + jnp.einsum('bthd,bhde->bthe', qc, cmat) * inter[..., None]
        den = a.sum(axis=2) + jnp.einsum('bthd,bhd->bth', qc, nvec) * inter
        hc = num / jnp.maximum(jnp.abs(den), jnp.exp(-mt))[..., None]
        m_new = mt[:, -1]
        wl = jnp.exp(g + (b[:, -1] - m_new)[:, None])
        dp = jnp.exp(b[:, -1] + m - m_new)
        cmat = cmat * dp[..., None, None] + jnp.einsum('bsh,bshd,bshe->bhde', wl, kc, vc)
        nvec = nvec * dp[..., None] + jnp.einsum('bsh,bshd->bhd', wl, kc)
        return (cmat, nvec, m_new), hc

    init = (c0.astype(F32), n0.astype(F32), m0.astype(F32))
    (cT, nT, mT), hs = lax.scan(step, init, (_to_chunks(q.astype(F32), c), _to_chunks(k.astype(F32), c),
                                             _to_chunks(v.astype(F32), c), _to_chunks(i_pre.astype(F32), c),
                                             _to_chunks(logf, c)))
    return (_from_chunks(hs).astype(v.dtype), cT.astype(c0.dtype), nT.astype(n0.dtype), mT.astype(m0.dtype))

def mixer_ab(h, pos, conv_buf, ssm_h, ret_s, w_in, conv_w, conv_b, dt_bias, a_log, d_skip, ssd_norm, w_out):
    bsz, l, _ = h.shape
    z, xbc, dt_raw, rq, rk, rv, rg = _split(h @ w_in, AB_SIZES)
    xbc, conv_buf = causal_conv(xbc, conv_buf, conv_w, conv_b)
    xbc = jax.nn.silu(xbc)
    xs, bm, cm = _split(xbc, (SSD_D_INNER, SSD_GROUPS * SSD_D_STATE, SSD_GROUPS * SSD_D_STATE))
    xs = xs.reshape(bsz, l, SSD_HEADS, SSD_HEAD_DIM)
    dt = jax.nn.softplus((dt_raw + dt_bias).astype(F32))
    a = -jnp.exp(a_log.astype(F32))
    y, ssm_h = ssd_scan(xs, dt, a, bm.reshape(bsz, l, SSD_GROUPS, SSD_D_STATE),
                        cm.reshape(bsz, l, SSD_GROUPS, SSD_D_STATE), ssm_h)
    y = (y + xs * d_skip[:, None]).reshape(bsz, l, SSD_D_INNER) * jax.nn.silu(z)
    y = group_rms(y, SSD_GROUPS) * ssd_norm
    q = rotary(rq.reshape(bsz, l, RET_HEADS, RET_DK), pos)
    k = rotary(rk.reshape(bsz, l, RET_HEADS, RET_DK), pos) * (RET_DK ** -0.5)
    v = rv.reshape(bsz, l, RET_HEADS, RET_DV)
    r, ret_s = retention_scan(q, k, v, ret_s)
    r = jax.nn.silu(rg) * group_rms(r.reshape(bsz, l, RET_V), RET_HEADS)
    return jnp.concatenate([y, r], axis=-1) @ w_out, conv_buf, ssm_h, ret_s

def mixer_c(h, c0, n0, m0, w_in, i_bias, f_bias, norm_g, w_out):
    bsz, l, _ = h.shape
    q, k, v, ig, fg, o = _split(h @ w_in, C_SIZES)
    q = q.reshape(bsz, l, M_HEADS, M_DK)
    k = k.reshape(bsz, l, M_HEADS, M_DK) * (M_DK ** -0.5)
    v = v.reshape(bsz, l, M_HEADS, M_DV)
    hh, c0, n0, m0 = mlstm_scan(q, k, v, ig + i_bias, fg + f_bias, c0, n0, m0)
    hh = group_rms(hh.reshape(bsz, l, M_V), M_HEADS) * norm_g
    return (jax.nn.sigmoid(o) * hh) @ w_out, c0, n0, m0

def mem_kv(mem, norm_g, w_kv):
    bsz = mem.shape[0]
    k, v = jnp.split(rmsnorm(mem, norm_g) @ w_kv, 2, axis=-1)
    return (k.reshape(bsz, MEM_LEN, X_HEADS, X_HEAD_DIM), v.reshape(bsz, MEM_LEN, X_HEADS, X_HEAD_DIM))

def cross_attn(h, k, v, w_q, w_o):
    bsz, l, _ = h.shape
    q = (h @ w_q).reshape(bsz, l, X_HEADS, X_HEAD_DIM)
    s = jnp.einsum('blhd,bmhd->bhlm', q, k.astype(q.dtype)).astype(F32) * (X_HEAD_DIM ** -0.5)
    p = jax.nn.softmax(s, axis=-1).astype(h.dtype)
    o = jnp.einsum('bhlm,bmhd->blhd', p, v.astype(h.dtype)).reshape(bsz, l, D_MODEL)
    return o @ w_o

def trunk(x, pos, mem_k, mem_v, conv_buf, ssm_h, ret_s, mc, mn, mm, p):
    conv_new, ssm_new, ret_new, mc_new, mn_new, mm_new = [], [], [], [], [], []
    for layer in range(DEPTH):
        x = x + 0.5 * swiglu(rmsnorm(x, p['norm_ffn1'][layer]), p['w_ffn1_in'][layer], p['w_ffn1_out'][layer])
        hn = rmsnorm(x, p['norm_mix'][layer])
        e = layer // 2
        if layer % 2 == 0:
            out, cb, sh, rs = mixer_ab(hn, pos, conv_buf[e], ssm_h[e], ret_s[e], p['w_in_ab'][e],
                                       p['ssd_conv_w'][e], p['ssd_conv_b'][e], p['ssd_dt_bias'][e],
                                       p['ssd_a_log'][e], p['ssd_d'][e], p['ssd_norm'][e], p['w_out_ab'][e])
            conv_new.append(cb)
            ssm_new.append(sh)
            ret_new.append(rs)
        else:
            out, c1, n1, m1 = mixer_c(hn, mc[e], mn[e], mm[e], p['w_in_c'][e], p['mlstm_i_bias'][e],
                                      p['mlstm_f_bias'][e], p['mlstm_norm'][e], p['w_out_c'][e])
            mc_new.append(c1)
            mn_new.append(n1)
            mm_new.append(m1)
        x = x + out
        x = x + cross_attn(rmsnorm(x, p['norm_xattn'][layer]), mem_k[layer], mem_v[layer],
                           p['w_xq'][layer], p['w_xo'][layer])
        x = x + 0.5 * swiglu(rmsnorm(x, p['norm_ffn2'][layer]), p['w_ffn2_in'][layer], p['w_ffn2_out'][layer])
    return (rmsnorm(x, p['norm_final']), jnp.stack(conv_new), jnp.stack(ssm_new), jnp.stack(ret_new),
            jnp.stack(mc_new), jnp.stack(mn_new), jnp.stack(mm_new))

def setup_inputs(seed: int = 0) -> dict:
    key = jax.random.key(seed)
    keys = iter(jax.random.split(key, 48))

    def nrm(shape, scale):
        return jax.random.normal(next(keys), shape, F32) * scale

    def gain(shape):
        return 1.0 + nrm(shape, 0.02)

    dt0 = jnp.exp(jax.random.uniform(next(keys), (N_EVEN, SSD_HEADS), F32,
                                     minval=math.log(1e-3), maxval=math.log(1e-1)))
    return {
        'x_prompt': nrm((BATCH, SEQ, D_MODEL), 1.0),
        'x_sample': nrm((DEC_BATCH, DEC_SEQ, D_MODEL), 1.0),
        'cache_mem_k': nrm((DEPTH, DEC_BATCH, MEM_LEN, X_HEADS, X_HEAD_DIM), 1.0),
        'cache_mem_v': nrm((DEPTH, DEC_BATCH, MEM_LEN, X_HEADS, X_HEAD_DIM), 1.0),
        'state_conv': nrm((N_EVEN, DEC_BATCH, SSD_CONV - 1, SSD_CONV_CH), 1.0),
        'state_ssm': nrm((N_EVEN, DEC_BATCH, SSD_HEADS, SSD_HEAD_DIM, SSD_D_STATE), 0.3),
        'state_ret': nrm((N_EVEN, DEC_BATCH, RET_HEADS, RET_DK, RET_DV), 1.0),
        'state_mlstm_c': nrm((N_ODD, DEC_BATCH, M_HEADS, M_DK, M_DV), 0.3),
        'state_mlstm_n': nrm((N_ODD, DEC_BATCH, M_HEADS, M_DK), 0.3),
        'state_mlstm_m': nrm((N_ODD, DEC_BATCH, M_HEADS), 1.0),
        'mem_prompt': nrm((BATCH, MEM_LEN, D_MODEL), 1.0),
        'norm_ffn1': gain((DEPTH, D_MODEL)),
        'w_ffn1_in': nrm((DEPTH, D_MODEL, 2 * D_FF), D_MODEL ** -0.5),
        'w_ffn1_out': nrm((DEPTH, D_FF, D_MODEL), D_FF ** -0.5),
        'norm_mix': gain((DEPTH, D_MODEL)),
        'w_in_ab': nrm((N_EVEN, D_MODEL, IN_AB), D_MODEL ** -0.5),
        'ssd_conv_w': nrm((N_EVEN, SSD_CONV, SSD_CONV_CH), SSD_CONV ** -0.5),
        'ssd_conv_b': nrm((N_EVEN, SSD_CONV_CH), 0.02),
        'ssd_dt_bias': dt0 + jnp.log(-jnp.expm1(-dt0)),
        'ssd_a_log': jnp.log(jax.random.uniform(next(keys), (N_EVEN, SSD_HEADS), F32, minval=1.0, maxval=16.0)),
        'ssd_d': 1.0 + nrm((N_EVEN, SSD_HEADS), 0.1),
        'ssd_norm': gain((N_EVEN, SSD_D_INNER)),
        'w_out_ab': nrm((N_EVEN, SSD_D_INNER + RET_V, D_MODEL), (SSD_D_INNER + RET_V) ** -0.5),
        'w_in_c': nrm((N_ODD, D_MODEL, IN_C), D_MODEL ** -0.5),
        'mlstm_i_bias': nrm((N_ODD, M_HEADS), 0.5),
        'mlstm_f_bias': jnp.linspace(3.0, 6.0, M_HEADS, dtype=F32)[None] + nrm((N_ODD, M_HEADS), 0.1),
        'mlstm_norm': gain((N_ODD, M_V)),
        'w_out_c': nrm((N_ODD, M_V, D_MODEL), M_V ** -0.5),
        'norm_xattn': gain((DEPTH, D_MODEL)),
        'norm_mem': gain((DEPTH, D_MODEL)),
        'w_xq': nrm((DEPTH, D_MODEL, D_MODEL), D_MODEL ** -0.5),
        'w_xkv': nrm((DEPTH, D_MODEL, 2 * D_MODEL), D_MODEL ** -0.5),
        'w_xo': nrm((DEPTH, D_MODEL, D_MODEL), D_MODEL ** -0.5),
        'norm_ffn2': gain((DEPTH, D_MODEL)),
        'w_ffn2_in': nrm((DEPTH, D_MODEL, 2 * D_FF), D_MODEL ** -0.5),
        'w_ffn2_out': nrm((DEPTH, D_FF, D_MODEL), D_FF ** -0.5),
        'norm_final': gain((D_MODEL,)),
    }

def reference(x_prompt, x_sample, cache_mem_k, cache_mem_v, state_conv, state_ssm, state_ret,
              state_mlstm_c, state_mlstm_n, state_mlstm_m, mem_prompt,
              norm_ffn1, w_ffn1_in, w_ffn1_out, norm_mix, w_in_ab, ssd_conv_w, ssd_conv_b,
              ssd_dt_bias, ssd_a_log, ssd_d, ssd_norm, w_out_ab, w_in_c, mlstm_i_bias, mlstm_f_bias,
              mlstm_norm, w_out_c, norm_xattn, norm_mem, w_xq, w_xkv, w_xo, norm_ffn2, w_ffn2_in,
              w_ffn2_out, norm_final):
    p = dict(norm_ffn1=norm_ffn1, w_ffn1_in=w_ffn1_in, w_ffn1_out=w_ffn1_out, norm_mix=norm_mix,
             w_in_ab=w_in_ab, ssd_conv_w=ssd_conv_w, ssd_conv_b=ssd_conv_b, ssd_dt_bias=ssd_dt_bias,
             ssd_a_log=ssd_a_log, ssd_d=ssd_d, ssd_norm=ssd_norm, w_out_ab=w_out_ab, w_in_c=w_in_c,
             mlstm_i_bias=mlstm_i_bias, mlstm_f_bias=mlstm_f_bias, mlstm_norm=mlstm_norm, w_out_c=w_out_c,
             norm_xattn=norm_xattn, w_xq=w_xq, w_xo=w_xo, norm_ffn2=norm_ffn2, w_ffn2_in=w_ffn2_in,
             w_ffn2_out=w_ffn2_out, norm_final=norm_final)
    dt = x_prompt.dtype
    kv = [mem_kv(mem_prompt, norm_mem[layer], w_xkv[layer]) for layer in range(DEPTH)]
    mem_k_prompt = jnp.stack([pair[0] for pair in kv])
    mem_v_prompt = jnp.stack([pair[1] for pair in kv])
    (y_prompt, conv_p, ssm_p, ret_p, mc_p, mn_p, mm_p) = trunk(
        x_prompt, jnp.arange(SEQ), mem_k_prompt, mem_v_prompt,
        jnp.zeros((N_EVEN, BATCH, SSD_CONV - 1, SSD_CONV_CH), dt),
        jnp.zeros((N_EVEN, BATCH, SSD_HEADS, SSD_HEAD_DIM, SSD_D_STATE), dt),
        jnp.zeros((N_EVEN, BATCH, RET_HEADS, RET_DK, RET_DV), dt),
        jnp.zeros((N_ODD, BATCH, M_HEADS, M_DK, M_DV), dt),
        jnp.zeros((N_ODD, BATCH, M_HEADS, M_DK), dt),
        jnp.zeros((N_ODD, BATCH, M_HEADS), dt), p)
    (y_sample, conv_s, ssm_s, ret_s, mc_s, mn_s, mm_s) = trunk(
        x_sample, PAST_LEN + jnp.arange(DEC_SEQ), cache_mem_k, cache_mem_v,
        state_conv, state_ssm, state_ret, state_mlstm_c, state_mlstm_n, state_mlstm_m, p)
    return (y_prompt, y_sample, mem_k_prompt, mem_v_prompt, conv_p, conv_s, ssm_p, ssm_s,
            ret_p, ret_s, mc_p, mc_s, mn_p, mn_s, mm_p, mm_s)


_drawn_inputs = setup_inputs


def setup_inputs(seed=0):
    import zlib

    import numpy as np

    out = dict(_drawn_inputs(seed))
    spreads = {}
    factors = {'ssd_norm': 2.702,
     'mlstm_norm': 31.429,
     'norm_xattn': 8.0,
     'norm_mem': 2.848,
     'norm_ffn2': 5.152,
     'norm_final': 2.68}
    for name, (base, spread) in spreads.items():
        noise = np.random.default_rng([zlib.crc32(name.encode()), seed]).standard_normal(out[name].shape)
        drawn = base * np.exp(spread * noise) if base else spread * noise
        out[name] = jnp.asarray(drawn.astype(out[name].dtype))
    for name, factor in factors.items():
        out[name] = (out[name] * factor).astype(out[name].dtype)
    return out
```

```python
from contextlib import ExitStack

import numpy as np
import concourse.bass as bass
from concourse import mybir

F32 = mybir.dt.float32
F32R = mybir.dt.float32r
ALU = mybir.AluOpType
ACT = mybir.ActivationFunctionType
AX = mybir.AxisListType.X

P = 128
D = 1024
KD = D // P
NP = 256
NS = 8
T = NP + NS
FF = 2816
KF = FF // P
EPS = 1e-6
SSD_HEADS, SSD_P, SSD_G, SSD_N = 32, 64, 4, 128
SSD_IN = SSD_HEADS * SSD_P
CONV_CH = SSD_IN + 2 * SSD_G * SSD_N
CT = CONV_CH // P
RH, RDK, RDV = 4, 256, 512
MH, MDK, MDV = 4, 128, 256
XH, XD, MEM = 4, 256, 256
SLOTS = 4
CHUNK = 2048


def build(nc, A, O, stop=None):
    with ExitStack() as ctx:
        sem_of = lambda name: ctx.enter_context(nc.semaphore(name))
        base = (nc.sbuf_base + 63) // 64 * 64
        top = [base]

        def place(name, shape, dt=F32, at=None):
            n = int(np.prod(shape[1:])) * 4
            if at is None:
                at = top[0]
                top[0] += (n + 31) // 32 * 32
            return nc.alloc_sbuf_tensor_at(name, shape, dt, offset=at)

        raw = place("raw", [P, SLOTS, CHUNK])
        whi = place("whi", [P, 2, CHUNK], F32R)
        wlo = place("wlo", [P, 2, CHUNK], F32R)
        x = place("x", [P, KD, T])
        xnh = place("xnh", [P, KD, T], F32R)
        xnl = place("xnl", [P, KD, T], F32R)
        ident = place("ident", [P, P])
        ones = place("ones", [P, P])
        mask = place("mask", [P, 3 * P])
        g1 = place("g1", [P, 112])
        g2 = place("g2", [P, 120])
        tab_at = top[0]
        rot = place("rot", [P, 4, T])
        rstd4 = place("rstd4", [P, 4, T], at=tab_at)
        dtab = place("dtab", [P, RH, NP])
        tail = place("tail", [P, 2 * RH])
        cols = place("cols", [P, 64])
        dcol = cols[:, 0:16]
        norm_at = top[0]
        sq = place("sq", [P, 2, T])
        ms = place("ms", [P, T])
        rstd1 = place("rstd1", [P, 1, T])
        xt = place("xt", [P, 3, T])
        gate_at = top[0]
        sg = place("sg", [P, 2, T])
        ht = place("ht", [P, 2, T])
        REG = top[0]
        END = nc.sbuf_usable_end
        room = END - REG
        print("region", REG, room) if stop else None

        psum = ctx.enter_context(nc.psum_tensor("psum", [P, 8, 512], F32))
        SSB = 4

        landed = [sem_of(f"landed{i}") for i in range(SLOTS)]
        hi_done = sem_of("hi_done")
        lo_done = sem_of("lo_done")
        chunk_done = sem_of("chunk_done")
        bank_free = sem_of("bank_free")
        seeded = sem_of("seeded")
        h_hi = sem_of("h_hi")
        gate_ready = sem_of("gate_ready")
        h_ready = sem_of("h_ready")
        sq_ready = sem_of("sq_ready")
        ss_done = sem_of("ss_done")
        ms_done = sem_of("ms_done")
        sd_done = sem_of("sd_done")
        rstd_done = sem_of("rstd_done")
        xt_done = sem_of("xt_done")
        xh_done = sem_of("xh_done")
        xn_ready = sem_of("xn_ready")
        tp_done = sem_of("tp_done")
        tpa = sem_of("tpa")
        tpd = sem_of("tpd")
        consts = sem_of("consts")
        ones_set = sem_of("ones_set")
        stored = {"sp": sem_of("stored_sp"), "pool": sem_of("stored_pool")}
        order = {"act": sem_of("act_order"), "dve": sem_of("dve_order"), "pool": sem_of("pool_order")}
        count = {"act": 0, "dve": 0, "pool": 0}
        stores = {"sp": 0, "pool": 0}
        tot = dict(chunk=0, use=0, ffn=0, gate=0, stores=0, sq=0, grp=0, app=0, tp=0)

        def link(eng, which, ins):
            count[which] += 1
            ins.then_inc(order[which], 1)
            eng.wait_ge(order[which], count[which])

        def store(eng, which, out, src):
            stores[which] += 16
            eng.dma_start(out, src).then_inc(stored[which], 16)

        stages = []

        class Stage:
            def sp(S, e): pass
            def pe(S, e): pass
            def act(S, e): pass
            def dve(S, e): pass
            def pool(S, e): pass

        def walk(eng, n, fn, last=0):
            g = (n - last) // 4
            if g >= 2:
                with eng.Fori(0, g) as i:
                    for r in range(4):
                        fn(i, r)
            else:
                g = 0
            for l in range(4 * g, n - last):
                fn(0, l)

        linears = []
        pending = []

        class Linear(Stage):

            def __init__(S, W, n, kt, tiles, parts, rhs, ready=None, act=None, dve=None, cpu=1, cols=T, turned=False, per=0):
                S.W, S.n, S.kt, S.tiles, S.parts, S.rhs = W, n, kt, tiles, parts, rhs
                S.ready, S.eact, S.edve, S.cpu, S.cols, S.turned, S.per = ready, act, dve, cpu, cols, turned, per
                S.c0, S.use0 = tot["chunk"], tot["use"]
                tot["chunk"] += n
                tot["use"] += n // cpu
                S.next = None
                if linears:
                    linears[-1].next = S
                linears.append(S)
                stages.append(S)

            def uses_end(S):
                return S.use0 + S.n // S.cpu

            def sp(S, e):
                def load(i, r):
                    slot = (S.c0 + r) % SLOTS
                    e.wait_ge(lo_done, i * 4 + (S.c0 + r + 1))
                    for dst, src in S.parts(raw[:, slot, :], i, r):
                        e.dma_start(dst, src).then_inc(landed[slot], 16)
                walk(e, S.n, load)

            def split_hi(S, e, i, r):
                c = S.c0 + r
                e.wait_ge(landed[c % SLOTS], i * 32 + 32 * (c // SLOTS + 1))
                if r > 0 or S.c0 > 0:
                    e.wait_ge(chunk_done, i * 4 + c)
                m = S.kt * S.tiles * P
                nc.scalar.activation(whi[:, c % 2, 0:m], raw[:, c % SLOTS, 0:m], ACT.Copy).then_inc(hi_done, 1)

            def split_lo(S, e, i, r):
                c = S.c0 + r
                m = S.kt * S.tiles * P
                e.wait_ge(hi_done, i * 4 + (c + 1))
                nc.vector.tensor_tensor(wlo[:, c % 2, 0:m], raw[:, c % SLOTS, 0:m], whi[:, c % 2, 0:m].bitcast(F32),
                                        ALU.subtract).then_inc(lo_done, 1)

            def pe(S, e):
                if S.ready:
                    S.ready(e)
                def mul(i, r):
                    c, half, par = S.c0 + r, r % S.cpu, (S.use0 + r // S.cpu) % 2
                    e.wait_ge(lo_done, i * 4 + (c + 1 + SLOTS))
                    if half == 0:
                        e.wait_ge(bank_free, i * (4 // S.cpu) + (S.use0 + r // S.cpu + 1))
                    wh = whi[:, c % 2, 0:S.kt * S.tiles * P].rearrange("p (k n) -> p k n", k=S.kt)
                    wl = wlo[:, c % 2, 0:S.kt * S.tiles * P].rearrange("p (k n) -> p k n", k=S.kt)
                    hi, lo = S.rhs[half] if isinstance(S.rhs, list) else S.rhs
                    for t in range(S.tiles):
                        out = psum[:, 2 * par + t, 0:S.cols]
                        for k in range(S.kt):
                            kk = k if isinstance(S.rhs, list) else half * S.kt + k
                            first, final = half == 0 and k == 0, half == S.cpu - 1 and k == S.kt - 1
                            if S.turned:
                                ah, al = hi[:, kk, t * P:(t + 1) * P], lo[:, kk, t * P:(t + 1) * P]
                                e.matmul(out, ah, wh[:, k, :], start=first, stop=False)
                                e.matmul(out, ah, wl[:, k, :], start=False, stop=False)
                                m = e.matmul(out, al, wh[:, k, :], start=False, stop=final)
                            else:
                                a, b = wh[:, k, t * P:(t + 1) * P], wl[:, k, t * P:(t + 1) * P]
                                e.matmul(out, a, hi[:, kk, 0:S.cols], start=first, stop=False)
                                e.matmul(out, a, lo[:, kk, 0:S.cols], start=False, stop=False)
                                m = e.matmul(out, b, hi[:, kk, 0:S.cols], start=False, stop=final)
                    m.then_inc(chunk_done, 1)
                walk(e, S.n, mul)

            def evict(S, e, fn, which, i, r):
                if fn is None or r % S.cpu != S.cpu - 1:
                    return
                e.wait_ge(chunk_done, i * 4 + (S.c0 + r + 2))
                u = r // S.cpu
                fn(e, i * (4 // S.cpu) + u, (S.use0 + u) % 2, i * (4 // S.cpu) + (S.use0 + u))

            def both(S, e, split, fn, which):
                if S is linears[0]:
                    split(S, e, 0, 0)

                def step(i, r):
                    split(S, e, i, r + 1)
                    S.evict(e, fn, which, i, r)
                walk(e, S.n, step, last=1)
                if S.next:
                    split(S.next, e, 0, 0)
                S.evict(e, fn, which, 0, S.n - 1)

            def act(S, e):
                S.both(e, Linear.split_hi, S.eact, "act")

            def dve(S, e):
                S.base = count["dve"]
                S.both(e, Linear.split_lo, S.edve, "dve")
                count["dve"] = S.base + S.per * (S.n // S.cpu)

            def chain(S, e, l):
                n = [0]

                def go(ins):
                    n[0] += 1
                    assert n[0] <= S.per
                    ins.then_inc(order["dve"], 1)
                    e.wait_ge(order["dve"], l * S.per + (S.base + n[0]))
                return go

        def by_cols(W, col0, w=256, kt=KD):
            def parts(dst, i, r):
                v = dst[:, 0:kt * w].rearrange("p (k n) -> p k n", k=kt)
                src = W.rearrange("(k p) n -> p k n", p=P)
                h = kt // 2
                at = i * (4 * w) + (r * w + col0)
                for a, b in ((0, h), (h, kt)):
                    yield v[:, a:b, :], src[:, a:b, bass.ds(at, w)]
            return parts

        def two_cols(W, col0, col1):
            def parts(dst, i, r):
                v = dst[:, 0:KD * 256].rearrange("p (k two n) -> p k two n", k=KD, two=2)
                src = W.rearrange("(k p) n -> p k n", p=P)
                for q, c in ((0, col0), (1, col1)):
                    yield v[:, :, q, :], src[:, :, bass.ds(i * 512 + (r * P + c), P)]
            return parts

        def by_rows(W, kt):
            def parts(dst, i, r):
                v = dst[:, 0:kt * P].rearrange("p (k n) -> p k n", k=kt)
                src = W[(r % 2) * kt * P:(r % 2 + 1) * kt * P, :].rearrange("(k p) n -> p k n", p=P)
                h = kt // 2
                for a, b in ((0, h), (h, kt)):
                    yield v[:, a:b, :], src[:, a:b, bass.ds(i * 256 + (r // 2) * P, P)]
            return parts

        def add_to_x(scale, tiles):
            def dve(e, l, par, use):
                ps = psum[:, 2 * par:2 * par + tiles, 0:T]
                xs = x[:, bass.ds(l * tiles, tiles), :]
                e.scalar_tensor_tensor(out=xs, in0=ps, scalar=scale, in1=xs, op0=ALU.mult, op1=ALU.add).then_inc(bank_free, 1)
            return dve

        def copy_out(dst, scale=1.0, n=T):
            def dve(e, l, par, use):
                e.tensor_scalar(dst[:, bass.ds(l * 2, 2), :], psum[:, 2 * par:2 * par + 2, 0:n], scale, None,
                                ALU.mult).then_inc(bank_free, 1)
            return dve

        class Stat(Stage):

            def __init__(S, src, groups, g, out, wait=None, n=T):
                S.src, S.groups, S.g, S.out, S.wait, S.n = src, groups, g, out, wait, n
                S.q0, S.g0 = tot["sq"], tot["grp"]
                tot["sq"] += groups * g
                tot["grp"] += groups
                stages.append(S)

            def act(S, e):
                for t in range(S.groups * S.g):
                    if S.wait:
                        S.wait(e, t)
                    if S.q0 + t >= 2:
                        e.wait_ge(ss_done, S.q0 + t - 1)
                    nc.scalar.activation(sq[:, t % 2, 0:S.n], S.src[:, t, 0:S.n], ACT.Square).then_inc(sq_ready, 1)
                    if t % S.g == S.g - 1:
                        G = t // S.g
                        e.wait_ge(ms_done, S.g0 + G + 1)
                        nc.scalar.activation(S.out[:, G, 0:S.n], ms[:, 0:S.n], ACT.Sqrt).then_inc(sd_done, 1)

            def pe(S, e):
                for t in range(S.groups * S.g):
                    G = S.g0 + t // S.g
                    if t % S.g == 0 and G > 0:
                        e.wait_ge(ms_done, G)
                    if t == 0:
                        e.wait_ge(ones_set, 1)
                    e.wait_ge(sq_ready, S.q0 + t + 1)
                    e.matmul(psum[:, SSB, 0:S.n], ones[:, :], sq[:, t % 2, 0:S.n], start=t % S.g == 0,
                             stop=t % S.g == S.g - 1).then_inc(ss_done, 1)

            def dve(S, e):
                for G in range(S.groups):
                    e.wait_ge(ss_done, S.q0 + (G + 1) * S.g)
                    if S.g0 + G > 0:
                        e.wait_ge(sd_done, S.g0 + G)
                    e.tensor_scalar(ms[:, 0:S.n], psum[:, SSB, 0:S.n], 1.0 / (S.g * P), EPS, ALU.mult, ALU.add).then_inc(ms_done, 1)
                    e.wait_ge(sd_done, S.g0 + G + 1)
                    e.reciprocal(S.out[:, G, 0:S.n], S.out[:, G, 0:S.n]).then_inc(rstd_done, 1)

        class Apply(Stage):

            def __init__(S, src, groups, g, rs, gcol, hi, lo, n=T, wait=None, out=None):
                S.src, S.g, S.rs, S.gcol, S.hi, S.lo, S.n, S.tiles = src, g, rs, gcol, hi, lo, n, groups * g
                S.a0, S.rgrp, S.wait, S.out = tot["app"], tot["grp"], wait, out
                if out is None:
                    tot["app"] += S.tiles
                stages.append(S)

            def scale(S, e, t):
                G = t // S.g
                if S.out is not None:
                    dst = S.out[:, t, 0:S.n]
                else:
                    if S.a0 + t >= 3:
                        e.wait_ge(xn_ready, S.a0 + t - 2)
                    dst = xt[:, (S.a0 + t) % 3, 0:S.n]
                if S.gcol is None:
                    return e.tensor_tensor(dst, S.src[:, t, 0:S.n], S.rs[:, G, 0:S.n], ALU.mult)
                return e.scalar_tensor_tensor(out=dst, in0=S.src[:, t, 0:S.n], scalar=g1[:, S.gcol + t:S.gcol + t + 1],
                                              in1=S.rs[:, G, 0:S.n], op0=ALU.mult, op1=ALU.mult)

            def sub(S, e, t):
                a = S.a0 + t
                e.wait_ge(xh_done, a + 1)
                e.tensor_tensor(S.lo[:, t, 0:S.n], xt[:, a % 3, 0:S.n], S.hi[:, t, 0:S.n].bitcast(F32),
                                ALU.subtract).then_inc(xn_ready, 1)

            def dve(S, e):
                if S.wait:
                    S.wait(e)
                e.wait_ge(rstd_done, S.rgrp)
                for t in range(S.tiles):
                    ins = S.scale(e, t)
                    if S.out is not None:
                        link(e, "dve", ins)
                        continue
                    ins.then_inc(xt_done, 1)
                    if t >= 1:
                        S.sub(e, t - 1)
                if S.out is None:
                    S.sub(e, S.tiles - 1)

            def act(S, e):
                if S.out is not None:
                    return
                for t in range(S.tiles):
                    a = S.a0 + t
                    e.wait_ge(xt_done, a + 1)
                    nc.scalar.activation(S.hi[:, t, 0:S.n], xt[:, a % 3, 0:S.n], ACT.Copy).then_inc(xh_done, 1)

        def xn_wait():
            target = tot["app"]
            return lambda e: e.wait_ge(xn_ready, target)

        def x_tile(u):
            return lambda e, t: e.wait_ge(bank_free, u)

        def norm_x(gcol, first=False):
            u = tot["use"] + 2
            Stat(x, 1, KD, rstd1, (lambda e, t: e.wait_ge(tpa, 1)) if first else x_tile(u))
            Apply(x, 1, KD, rstd1, gcol, xnh, xnl)

        class Turn(Stage):

            def __init__(S, items, ready=None, act_ready=None, dve_ready=None):
                S.items, S.ready, S.ar, S.dr = items, ready, act_ready, dve_ready
                S.n0 = tot["tp"]
                tot["tp"] += len(items)
                stages.append(S)

            def pe(S, e):
                e.wait_ge(consts, CONSTS)
                if S.ready:
                    S.ready(e)
                for j, (pieces, _) in enumerate(S.items):
                    n = S.n0 + j
                    if n >= 2:
                        e.wait_ge(tpd if n % 2 else tpa, n // 2)
                    for src, rows, cs, col in pieces:
                        m = e.transpose(psum[0:cs, 6 + n % 2, col:col + rows], src, ident[0:rows, 0:rows])
                    m.then_inc(tp_done, 1)

            def run(S, e, par):
                if (S.ar, S.dr)[par]:
                    (S.ar, S.dr)[par](e)
                for j, (_, evict) in enumerate(S.items):
                    n = S.n0 + j
                    if n % 2 == par:
                        e.wait_ge(tp_done, n + 1)
                        evict(e, psum[:, 6 + par, :], par).then_inc(tpd if par else tpa, 1)

            def act(S, e): S.run(e, 0)
            def dve(S, e): S.run(e, 1)

        def mv(e, par, out, src, scale=None):
            if par == 0:
                return nc.scalar.activation(out, src, ACT.Copy, **({} if scale is None else dict(scale=scale)))
            if scale is None:
                return e.tensor_copy(out, src)
            return e.tensor_scalar(out, src, scale, None, ALU.mult)

        def turned():
            n = tot["tp"]
            def w(e):
                e.wait_ge(tpa, (n + 1) // 2)
                if n // 2:
                    e.wait_ge(tpd, n // 2)
            return w

        CONSTS = 16 * 5
        xtok = place("xtok", [P, 2, D], at=REG)
        xstok = place("xstok", [NS, D], at=REG + 8192)
        p1 = place("p1", [112, P], at=REG + 12288)
        p2 = place("p2", [120, P], at=REG + 12800)
        x_in = sem_of("x_in")
        p_in = sem_of("p_in")

        class Init(Stage):
            def act(S, e):
                e.dma_start(xtok[:, :, :], A["x_prompt"].rearrange("o (b p) d -> p (o b) d", p=P)).then_inc(x_in, 16)
                e.dma_start(xstok[:, :], A["x_sample"].rearrange("b o d -> (b o) d")).then_inc(x_in, 16)

            def pool(S, e):
                e.memset(cols[:, 61:62], 1.0).then_inc(lo_done, SLOTS)
                e.memset(cols[:, 62:63], 1.0).then_inc(chunk_done, 1)
                e.memset(cols[:, 63:64], 1.0).then_inc(bank_free, 2)
                e.memset(cols[:, 60:61], 1.0).then_inc(h_ready, 2)
                e.memset(ones[:, :], 1.0).then_inc(ones_set, 1)
                e.dma_start(ident[:, :], A["c_ident"]).then_inc(consts, 16)
                row = 0
                for name in ("norm_ffn1", "norm_mix", "norm_xattn", "norm_mem", "norm_ffn2"):
                    e.dma_start(p1[row:row + 16, :], A[name].rearrange("l (t p) -> (l t) p", p=P)).then_inc(p_in, 16)
                    row += 16
                e.dma_start(p1[80:88, :], A["norm_final"].rearrange("(t p) -> t p", p=P)).then_inc(p_in, 16)
                e.dma_start(p1[88:104, :], A["ssd_norm"].rearrange("l (t p) -> (l t) p", p=P)).then_inc(p_in, 16)
                e.dma_start(p1[104:112, :], A["mlstm_norm"].rearrange("l (t p) -> (l t) p", p=P)).then_inc(p_in, 16)
                e.dma_start(p2[0:96, :], A["ssd_conv_w"].rearrange("l j (t p) -> (l j t) p", p=P)).then_inc(p_in, 16)
                e.dma_start(p2[96:120, :], A["ssd_conv_b"].rearrange("l (t p) -> (l t) p", p=P)).then_inc(p_in, 16)
                e.dma_start(mask[:, :], A["c_mask"]).then_inc(consts, 16)
                e.dma_start(rot[:, :, :], A["c_rot"]).then_inc(consts, 16)
                e.dma_start(dtab[:, :, :], A["c_dtab"]).then_inc(consts, 16)
                e.dma_start(tail[:, :], A["c_tail"]).then_inc(consts, 16)
        stages.append(Init())

        def x_item(k0):
            pieces = []
            for q in range(4):
                k = k0 + q // 2
                pieces.append((xtok[:, q % 2, k * P:(k + 1) * P], P, P, q * P))
            return pieces, lambda e, bank, par: mv(e, par, x[:, k0:k0 + 2, 0:NP], bank.rearrange("p (k n) -> p k n", k=2))
        items = [x_item(k) for k in range(0, KD, 2)]
        items.append(([(xstok[:, k * P:(k + 1) * P], NS, P, k * NS) for k in range(KD)],
                      lambda e, bank, par: mv(e, par, x[:, :, NP:T], bank[:, 0:KD * NS].rearrange("p (k n) -> p k n", k=KD))))
        items.append(([(p1[:, :], 112, P, 0), (p2[:, :], 120, P, 128)],
                      lambda e, bank, par: (link(e, "dve", e.tensor_copy(g1[:, :], bank[:, 0:112])),
                                            e.tensor_copy(g2[:, :], bank[:, 128:248]))[1]))
        Turn(items, ready=lambda e: (e.wait_ge(x_in, 32), e.wait_ge(p_in, 160)))
        x_ready = turned()

        H_at = REG
        Hh = place("Hh", [P, KF, T], F32R, at=H_at)
        Hl = place("Hl", [P, KF, T], F32R, at=H_at + KF * T * 4)

        def ffn(layer, w_in, w_out):
            f0, q0 = tot["ffn"], tot["gate"]
            tot["ffn"] += KF
            tot["gate"] += KF

            def act(e, l, par, use):
                e.wait_ge(bank_free, use + 1)
                nc.scalar.activation(sg[:, par, :], psum[:, 2 * par, 0:T], ACT.Silu).then_inc(gate_ready, 1)

            def dve(e, l, par, use):
                e.wait_ge(gate_ready, l + (q0 + 1))
                e.wait_ge(h_ready, l + (f0 + 1))
                e.tensor_tensor(ht[:, par, :], sg[:, par, :], psum[:, 2 * par + 1, 0:T], ALU.mult).then_inc(bank_free, 1)
                e.wait_ge(bank_free, use + 3)
                hh, hl = Hh[:, bass.ds(l, 1), :], Hl[:, bass.ds(l, 1), :]
                e.tensor_copy(hh, ht[:, par:par + 1, :]).then_inc(h_hi, 1)
                e.wait_ge(h_hi, l + (f0 + 1))
                e.tensor_tensor(hl, ht[:, par:par + 1, :], hh.bitcast(F32), ALU.subtract).then_inc(h_ready, 1)
            kept = pending[:]
            pending.clear()

            class Wait(Stage):
                def dve(S, e):
                    for q, n in kept:
                        e.wait_ge(q, n)
            stages.append(Wait())
            Linear(w_in, KF, KD, 2, two_cols(w_in, 0, FF), (xnh, xnl), ready=xn_wait(), act=act, dve=dve)
            Linear(w_out, 2 * KD, KF // 2, 1, by_rows(w_out, KF // 2), (Hh, Hl),
                   ready=lambda e: e.wait_ge(h_ready, f0 + KF + 2), dve=add_to_x(0.5, 1), cpu=2)

        G_FFN1, G_MIX, G_X, G_MEM, G_FFN2, G_FIN, G_SSD, G_M = 0, 16, 32, 48, 64, 80, 88, 104


        def gated(dst, func):
            q0 = tot["gate"]

            def start(n):
                tot["gate"] += n

            def act(e, l, par, use):
                e.wait_ge(bank_free, use + 1)
                nc.scalar.activation((sg, ht)[par][:, :, :], psum[:, 2 * par:2 * par + 2, 0:T], func).then_inc(gate_ready, 1)

            def dve(e, l, par, use):
                e.wait_ge(gate_ready, l + (q0 + 1))
                d = dst[:, bass.ds(l * 2, 2), :]
                e.tensor_tensor(d, d, (sg, ht)[par][:, :, :], ALU.mult).then_inc(bank_free, 1)
            start(dst.shape[1] // 2)
            return act, dve

        def evicted():
            n = tot["use"] + 2
            return lambda e: e.wait_ge(bank_free, n)

        def all_of(*ws):
            return lambda e: [w(e) for w in ws] and None

        def at_least(s, n):
            return lambda e: e.wait_ge(s, n)

        def mixer_ab():
            W = A["w_in_ab"][0]
            R0, R1 = REG, REG + CT * T * 4
            R2 = R1 + 32 * T * 4
            xbc = place("xbc", [P, CT, T], at=R0)
            qf = place("qf", [P, 8, T], at=R1)
            kf = place("kf", [P, 8, T], at=R1 + 8 * T * 4)
            vf = place("vf", [P, 16, T], at=R1 + 16 * T * 4)
            hist = place("hist", [P, CT, 24], at=R2)
            crow = place("crow", [24, CONV_CH], at=R2 + 4096)
            ctok = place("ctok", [11, CONV_CH], at=R2 + 20480)
            utail = place("utail", [P, CT, 11], at=R2 + 32768)
            x_tm = place("x_tm", [P, 2, SSD_IN], at=R2)
            B_tm = place("B_tm", [P, 2, 512], at=R2 + 16384)
            CBm = place("CBm", [P, 4, 384], at=R2 + 20480)
            eb = place("eb", [P, 2, 384], at=R2 + 26624)
            at_ = place("at", [P, 2, 384], at=R2 + 29696)
            xw = place("xw", [P, 2, 2, P], at=R2 + 32768)
            hst = place("hst", [P, 4, P], at=R2 + 34816)
            scT = place("scT", [P, 7, 32], at=R2 + 36864)
            dtE = place("dtE", [P, 16, 16], at=R2 + 36864 + 896)
            rw = place("rw", [32, 7, T], at=norm_at)
            region_free = evicted()
            conv_in = sem_of("conv_in")
            conv_done = sem_of("conv_done")
            small_in = sem_of("small_in")
            d_in = sem_of("d_in")

            class Load(Stage):
                def pool(S, e):
                    region_free(e)
                    e.dma_start(crow[:, :], A["state_conv"].rearrange("l b j c -> (l b j) c")).then_inc(conv_in, 16)
                    with nc.allow_non_contiguous_dma(reason="32 numbers, one on each partition"):
                        e.dma_start(cols[0:32, 40:41], A["ssd_dt_bias"].rearrange("l h -> h l")).then_inc(small_in, 16)
                        e.dma_start(cols[0:32, 42:43], A["ssd_a_log"].rearrange("l h -> h l")).then_inc(small_in, 16)
                        for q in range(2):
                            src = A["ssd_d"].rearrange("l (j two) -> (l two) j", two=2)[q:q + 1, :].to_broadcast([64, 16])
                            e.dma_start(cols[64 * q:64 * q + 64, 0:16], src).then_inc(d_in, 16)
                    store(e, "pool", O[5][0, :, 0:2, :], A["state_conv"][0, :, 1:3, :])
            stages.append(Load())
            Turn([([(crow[:, t * P:(t + 1) * P], 24, P, (t - t0) * 24) for t in range(t0, t0 + 12)],
                   lambda e, bank, par, t0=t0: mv(e, par, hist[:, t0:t0 + 12, :], bank[:, 0:288].rearrange("p (t q) -> p t q", t=12)))
                  for t0 in (0, 12)], ready=at_least(conv_in, 16))
            hist_ready = turned()

            def conv_dve(e, l, par, use):
                go = L_xbc.chain(e, l)
                ps = psum[:, 2 * par:2 * par + 2, :]
                go(e.tensor_copy(utail[:, bass.ds(l * 2, 2), :], ps[:, :, T - 11:T]))
                for q in range(2):
                    w = lambda j: g2[:, bass.ds(l * 2 + (j * CT + q), 1)]
                    acc = xbc[:, bass.ds(l * 2 + q, 1), :]
                    u = ps[:, q:q + 1, :]
                    go(e.tensor_scalar(acc, u[:, :, 0:T], w(3), w(4), ALU.mult, ALU.add))
                    for j in (2, 1, 0):
                        d = 3 - j
                        a = acc[:, :, d:NP]
                        ins = e.scalar_tensor_tensor(out=a, in0=u[:, :, 0:NP - d], scalar=w(j), in1=a, op0=ALU.mult, op1=ALU.add)
                        if q == 1 and j == 0:
                            ins.then_inc(bank_free, 1)
                        else:
                            go(ins)
                    for j in (2, 1, 0):
                        a = acc[:, :, NP:T]
                        h = hist[:, bass.ds(l * 2 + q, 1), j:24:3]
                        ins = e.scalar_tensor_tensor(out=a, in0=h, scalar=w(j), in1=a, op0=ALU.mult, op1=ALU.add)
                        if q == 1 and j == 0:
                            ins.then_inc(conv_done, 1)
                        else:
                            go(ins)

            def conv_act(e, l, par, use):
                e.wait_ge(conv_done, l + 1)
                v = xbc[:, bass.ds(l * 2, 2), :]
                nc.scalar.activation(v, v, ACT.Silu).then_inc(xbc_ready, 1)
            xbc_ready = sem_of("xbc_ready")
            L_xbc = Linear(W, 12, KD, 2, by_cols(W, 2048), (xnh, xnl), ready=all_of(xn_wait(), hist_ready),
                           act=conv_act, dve=lambda e, l, par, use: conv_dve(e, l, par, use), per=15 - 2 + 0)
            dt_raw = sem_of("dt_raw")

            def dt_dve(e, l, par, use):
                e.wait_ge(small_in, 32)
                e.tensor_scalar(rw[:, 0, :], psum[0:32, 2 * par, 0:T], cols[0:32, 40:41], None, ALU.add).then_inc(bank_free, 1)

            def one_tile(W, c0):
                def parts(dst, i, r):
                    v = dst[:, 0:KD * P].rearrange("p (k n) -> p k n", k=KD)
                    src = W.rearrange("(k p) n -> p k n", p=P)
                    for a, b in ((0, 4), (4, 8)):
                        yield v[:, a:b, :], src[:, a:b, c0:c0 + P]
                return parts
            Linear(W, 1, KD, 1, one_tile(W, 5120), (xnh, xnl), dve=dt_dve)
            dt_out = evicted()
            ch_out = evicted()
            Turn([([(utail[:, t, :], P, 11, (t - t0) * P) for t in range(t0, t0 + 4)],
                   lambda e, bank, par, t0=t0: mv(e, par, ctok[:, t0 * P:(t0 + 4) * P], bank[0:11, :])) for t0 in range(0, CT, 4)],
                 ready=ch_out)
            ct_ready = turned()
            rows_done = sem_of("rows_done")
            abs_done = sem_of("abs_done")
            ln_done = sem_of("ln_done")
            exp_a = sem_of("exp_a")
            w_done = sem_of("w_done")
            ncs_done = sem_of("ncs_done")

            class Rows(Stage):
                def pool(S, e):
                    ct_ready(e)
                    store(e, "pool", O[4].rearrange("l o j c -> (l o j) c"), ctok[0:3, :])
                    store(e, "pool", O[5][0, :, 2, :], ctok[3:11, :])

                def dve(S, e):
                    dt_out(e)
                    e.scalar_tensor_tensor(out=rw[:, 1, :], in0=rw[:, 0, :], scalar=-1.0, in1=rw[:, 0, :], op0=ALU.mult,
                                           op1=ALU.max).then_inc(abs_done, 1)
                    e.wait_ge(ln_done, 1)
                    link(e, "dve", e.scalar_tensor_tensor(out=rw[:, 2, :], in0=rw[:, 0, :], scalar=0.0, in1=rw[:, 1, :],
                                                          op0=ALU.max, op1=ALU.add))
                    e.wait_ge(exp_a, 1)
                    link(e, "dve", e.tensor_scalar(rw[:, 3, :], rw[:, 2, :], cols[0:32, 41:42], None, ALU.mult))
                    e.wait_ge(ones_set, 1)
                    for b in range(2):
                        s = slice(b * P, (b + 1) * P)
                        link(e, "dve", e.tensor_tensor_scan(rw[:, 4, s], ones[0:32, :], rw[:, 3, s], 0.0, ALU.mult, ALU.add))
                    c = lambda j: cols[0:32, j:j + 1]
                    link(e, "dve", e.tensor_scalar(rw[:, 5, 0:P], rw[:, 4, 0:P], rw[:, 4, P - 1:P], None, ALU.subtract))
                    link(e, "dve", e.tensor_tensor(c(43), rw[:, 4, P - 1:P], rw[:, 4, NP - 1:NP], ALU.add))
                    link(e, "dve", e.tensor_scalar(rw[:, 6, 0:P], rw[:, 4, 0:P], c(43), None, ALU.subtract))
                    e.tensor_scalar(rw[:, 6, P:NP], rw[:, 4, P:NP], rw[:, 4, NP - 1:NP], None, ALU.subtract).then_inc(ncs_done, 1)
                    e.wait_ge(w_done, 2)
                    link(e, "dve", e.tensor_tensor(rw[:, 6, 0:NP], rw[:, 6, 0:NP], rw[:, 2, 0:NP], ALU.mult))
                    e.tensor_copy(rw[:, 5, P:P + NS], rw[:, 2, NP:T]).then_inc(rows_done, 1)

                def act(S, e):
                    e.wait_ge(small_in, 32)
                    nc.scalar.activation(cols[0:32, 41:42], cols[0:32, 42:43], ACT.Exp).then_inc(exp_a, 1)
                    e.wait_ge(abs_done, 1)
                    link(e, "act", nc.scalar.activation(rw[:, 1, :], rw[:, 1, :], ACT.Exp, scale=-1.0))
                    nc.scalar.activation(rw[:, 1, :], rw[:, 1, :], ACT.Ln, bias=1.0).then_inc(ln_done, 1)
                    e.wait_ge(ncs_done, 1)
                    nc.scalar.activation(rw[:, 6, 0:NP], rw[:, 6, 0:NP], ACT.Exp).then_inc(w_done, 1)
                    nc.scalar.activation(rw[:, 5, P + NS:P + 2 * NS], rw[:, 3, NP:T], ACT.Exp, scale=-1.0).then_inc(w_done, 1)
            stages.append(Rows())

            def rotary(dst, c, get):
                def dve(e, l, par, use):
                    go = get().chain(e, l)
                    p0, p1_ = psum[:, 2 * par, 0:T], psum[:, 2 * par + 1, 0:T]
                    go(e.tensor_tensor(sg[:, 0, :], p0, rot[:, c, :], ALU.mult))
                    go(e.tensor_tensor(ht[:, 0, :], p1_, rot[:, c + 1, :], ALU.mult))
                    go(e.tensor_tensor(dst[:, bass.ds(l * 2, 1), :], sg[:, 0:1, :], ht[:, 0:1, :], ALU.subtract))
                    go(e.tensor_tensor(sg[:, 1, :], p0, rot[:, c + 1, :], ALU.mult))
                    e.tensor_tensor(ht[:, 1, :], p1_, rot[:, c, :], ALU.mult).then_inc(bank_free, 1)
                    e.wait_ge(bank_free, use + 3)
                    go(e.tensor_tensor(dst[:, bass.ds(l * 2 + 1, 1), :], sg[:, 1:2, :], ht[:, 1:2, :], ALU.add))
                return dve
            LQ = Linear(W, 4, KD, 2, by_cols(W, 5152), (xnh, xnl), dve=rotary(qf, 0, lambda: LQ), per=5)
            LK = Linear(W, 4, KD, 2, by_cols(W, 6176), (xnh, xnl), dve=rotary(kf, 2, lambda: LK), per=5)
            Linear(W, 8, KD, 2, by_cols(W, 7200), (xnh, xnl), dve=copy_out(vf))
            qkv_out = evicted()

            items = []
            for t in range(16):
                if t % 2 == 0:
                    items.append(([(xbc[:, t + q // 2, (q % 2) * P:(q % 2 + 1) * P], P, P, (q % 2) * 256 + (q // 2) * P) for q in range(4)],
                                  lambda e, bank, par, t=t: mv(e, par, x_tm[:, :, t * P:(t + 2) * P], bank.rearrange("p (b n) -> p b n", b=2))))
            for t in (16, 18):
                items.append(([(xbc[:, t + q // 2, (q % 2) * P:(q % 2 + 1) * P], P, P, (q % 2) * 256 + (q // 2) * P) for q in range(4)],
                              lambda e, bank, par, t=t: mv(e, par, B_tm[:, :, (t - 16) * P:(t - 14) * P], bank.rearrange("p (b n) -> p b n", b=2))))
            srcs = [rw[:, 4, 0:P], rw[:, 4, P:NP], rw[:, 5, 0:P], rw[:, 2, 0:P], rw[:, 2, P:NP], rw[:, 6, 0:P], rw[:, 6, P:NP]]
            items.append(([(v, 32, P, j * 32) for j, v in enumerate(srcs)],
                          lambda e, bank, par: mv(e, par, scT[:, :, :], bank[:, 0:224].rearrange("p (j h) -> p j h", j=7))))
            Turn(items, ready=all_of(qkv_out, at_least(rows_done, 1)))
            tm_ready = turned()
            BCs = place("BCs", [NS, 2, 512], at=norm_at + 7 * T * 4)
            bcs_items = [([(xbc[:, 16 + 4 * q + g, NP:T], P, NS, g * P) for g in range(4)],
                          lambda e, bank, par, q=q: mv(e, par, BCs[:, q, :], bank[0:NS, :])) for q in range(2)]
            Turn(bcs_items)
            bcs_ready = turned()

            cb_done = sem_of("cb_done")
            cb_ready = sem_of("cb_ready")
            bc_done = sem_of("bc_done")
            bc_free = sem_of("bc_free")
            e_diag = sem_of("e_diag")
            e_done = sem_of("e_done")
            att_ready = sem_of("att_ready")
            y_done = sem_of("y_done")
            y_out_ = sem_of("y_out")
            dte_done = sem_of("dte_done")
            dte_ready = sem_of("dte_ready")
            xw_ready = sem_of("xw_ready")
            st_done = sem_of("st_done")
            st_out = sem_of("st_out")

            class SSDPrompt(Stage):

                def pe(S, e):
                    tm_ready(e)
                    for g in range(4):
                        if g >= 1:
                            e.wait_ge(cb_ready, g)
                        B, C = xbc[:, 16 + g, :], xbc[:, 20 + g, :]
                        e.matmul(psum[:, 4, 0:NP], B[:, 0:P], C[:, 0:NP], start=True, stop=True)
                        e.matmul(psum[:, 4, NP:NP + P], B[:, P:NP], C[:, P:NP], start=True, stop=True).then_inc(cb_done, 1)
                    for h in range(32):
                        q, j = h % 2, h // 2
                        m = e.matmul(psum[64 * q:64 * q + 64, 5, j * 16:(j + 1) * 16], ident[0:32, h:h + 1].to_broadcast([32, 64]),
                                     rw[:, 5, P:P + 2 * NS], start=True, stop=True)
                    m.then_inc(dte_done, 1)

                    def sums(h):
                        if h >= 2:
                            e.wait_ge(bc_free, h - 1)
                        e.matmul(psum[:, h % 2, 0:NP], ident[0:32, h:h + 1].to_broadcast([32, P]), rw[:, 4, 0:NP], start=True,
                                 stop=True).then_inc(bc_done, 1)
                    sums(0)
                    sums(1)
                    for h in range(32):
                        e.wait_ge(att_ready, h + 1)
                        if h % 2 == 0 and h >= 4:
                            e.wait_ge(y_out_, h // 2 - 1)
                        o = psum[64 * (h % 2):64 * (h % 2) + 64, 2 + (h // 2) % 2, 0:NP]
                        e.matmul(o, x_tm[:, 0, h * 64:(h + 1) * 64], at_[:, h % 2, 0:NP], start=True, stop=False)
                        e.matmul(o[:, P:NP], x_tm[:, 1, h * 64:(h + 1) * 64], at_[:, h % 2, NP:NP + P], start=False,
                                 stop=True).then_inc(y_done, 1)
                        if h + 2 < 32:
                            sums(h + 2)
                    for j in range(16):
                        e.wait_ge(xw_ready, j + 1)
                        if j == 0:
                            e.wait_ge(bc_free, 32)
                        if j % 4 == 0 and j >= 8:
                            e.wait_ge(st_out, j // 4 - 1)
                        o = psum[:, (j // 4) % 2, (j % 4) * P:(j % 4 + 1) * P]
                        for b in range(2):
                            m = e.matmul(o, xw[:, j % 2, b, :], B_tm[:, b, (j // 4) * P:(j // 4 + 1) * P], start=b == 0, stop=b == 1)
                        m.then_inc(st_done, 1)

                def dve(S, e):
                    ct_stored(e)
                    for g in range(4):
                        e.wait_ge(cb_done, g + 1)
                        e.tensor_tensor(CBm[:, g, :], psum[:, 4, 0:384], mask[:, :], ALU.mult).then_inc(cb_ready, 1)
                    tm_ready(e)
                    e.wait_ge(cb_ready, 4)

                    def gaps(h):
                        e.wait_ge(bc_done, h + 1)
                        if h >= 2:
                            e.wait_ge(att_ready, h - 1)
                        ps = psum[:, h % 2, :]
                        for b in range(2):
                            ins = e.tensor_scalar(eb[:, h % 2, 2 * b * P:(2 * b + 1) * P], ps[:, b * P:(b + 1) * P],
                                                  scT[:, b, h:h + 1], 0.0, ALU.subtract, ALU.max)
                        ins.then_inc(e_diag, 1)
                    gaps(0)
                    for h in range(32):
                        if h + 1 < 32:
                            gaps(h + 1)
                        e.wait_ge(e_done, h + 1)
                        if h >= 2:
                            e.wait_ge(y_done, h - 1)
                        g = h // 8
                        e.scalar_tensor_tensor(out=at_[:, h % 2, 0:NP], in0=eb[:, h % 2, 0:NP], scalar=scT[:, 3, h:h + 1],
                                               in1=CBm[:, g, 0:NP], op0=ALU.mult, op1=ALU.mult)
                        e.scalar_tensor_tensor(out=at_[:, h % 2, NP:384], in0=eb[:, h % 2, NP:384], scalar=scT[:, 4, h:h + 1],
                                               in1=CBm[:, g, NP:384], op0=ALU.mult, op1=ALU.mult).then_inc(att_ready, 1)
                        if h % 2 == 1 and h >= 3:
                            S.out(e, h // 2 - 1)
                    S.out(e, 15)

                def out(S, e, j):
                    e.wait_ge(y_done, 2 * j + 2)
                    if j == 0:
                        e.wait_ge(d_in, 32)
                    v = xbc[:, j, 0:NP]
                    e.scalar_tensor_tensor(out=v, in0=v, scalar=dcol[:, j:j + 1], in1=psum[:, 2 + j % 2, 0:NP], op0=ALU.mult,
                                           op1=ALU.add).then_inc(y_out_, 1)

                def act(S, e):
                    e.wait_ge(dte_done, 1)
                    nc.scalar.activation(dtE[:, :, :], psum[:, 5, 0:256].rearrange("p (j q) -> p j q", j=16), ACT.Copy).then_inc(dte_ready, 1)
                    tm_ready(e)
                    for h in range(32):
                        e.wait_ge(e_diag, h + 1)
                        ps = psum[:, h % 2, :]
                        nc.scalar.activation(eb[:, h % 2, P:2 * P], ps[:, P:2 * P], ACT.Exp, scale=-1.0,
                                             bias=scT[:, 2, h:h + 1]).then_inc(bc_free, 1)
                        v = eb[:, h % 2, :].rearrange("p (q n) -> p q n", q=3)[:, 0:3:2, :]
                        nc.scalar.activation(v, v, ACT.Exp, scale=-1.0).then_inc(e_done, 1)
                    for j4 in range(4):
                        e.wait_ge(st_done, 4 * j4 + 4)
                        if j4 >= 1:
                            e.wait_ge(hst_stored, 16 * j4)
                        nc.scalar.activation(hst[:, :, :], psum[:, j4 % 2, :].rearrange("p (j n) -> p j n", j=4), ACT.Copy).then_inc(st_out, 1)
                        e.wait_ge(st_out, j4 + 1)
                        dst = O[6].rearrange("l o (j two) d n -> (two d) (l o j) n", two=2)
                        e.dma_start(dst[:, 4 * j4:4 * j4 + 4, :], hst[:, :, :]).then_inc(hst_stored, 16)

                def pool(S, e):
                    tm_ready(e)
                    for j in range(16):
                        if j >= 2:
                            e.wait_ge(st_done, j - 1)
                        w = scT[:, 5:7, 2 * j:2 * j + 2].unsqueeze(3).to_broadcast([P, 2, 2, 64])
                        e.tensor_tensor(xw[:, j % 2, :, :].rearrange("p b (h n) -> p b h n", h=2),
                                        x_tm[:, :, j * P:(j + 1) * P].rearrange("p b (h n) -> p b h n", h=2), w, ALU.mult).then_inc(xw_ready, 1)

            hst_stored = sem_of("hst_stored")
            tot["stores"] += 48

            def ct_stored(e):
                e.wait_ge(stored["pool"], 48)
            stages.append(SSDPrompt())

            hb = place("hb", [P, 2, 16, P], at=R2)
            jk = place("jk", [P, 16, P], at=R2 + 16384)
            xdt = place("xdt", [P, 16, NS], at=R2 + 16384 + 8192)
            ysm = place("ysm", [P, 16, NS], at=R2 + 16384 + 8192 + 512)
            hb_in = [sem_of("hb_in0"), sem_of("hb_in1")]
            hb_out = [sem_of("hb_out0"), sem_of("hb_out1")]
            dec_done = sem_of("dec_done")
            bcb_done = sem_of("bcb_done")
            h_new = sem_of("h_new")
            hy_done = sem_of("hy_done")
            ssd_out = sem_of("ssd_out")
            st_view = lambda t, b: t[0, b].rearrange("(j two) d n -> (two d) j n", two=2)

            class SSDSample(Stage):

                def pool(S, e):
                    e.wait_ge(st_done, 16)
                    for b in range(NS):
                        if b >= 2:
                            e.wait_ge(hb_out[b % 2], 16 * (b // 2))
                            e.wait_ge(hy_done, b - 1)
                        e.dma_start(hb[:, b % 2, :, :], st_view(A["state_ssm"], b)).then_inc(hb_in[b % 2], 16)

                def act(S, e):
                    e.wait_ge(dte_ready, 1)
                    for b in range(NS):
                        e.wait_ge(hb_in[b % 2], 16 * (b // 2 + 1))
                        for j in range(16):
                            v = hb[:, b % 2, j, :]
                            ins = nc.scalar.activation(v, v, ACT.Copy, scale=dtE[:, j, NS + b:NS + b + 1])
                        ins.then_inc(dec_done, 1)
                        if b >= 1:
                            S.keep(e, b - 1)
                    S.keep(e, NS - 1)

                def keep(S, e, b):
                    e.wait_ge(h_new, b + 1)
                    e.dma_start(st_view(O[7], b), hb[:, b % 2, :, :]).then_inc(hb_out[b % 2], 16)

                def pe(S, e):
                    bcs_ready(e)
                    for b in range(NS):
                        if b == 0:
                            e.wait_ge(y_out_, 16)
                            e.wait_ge(st_out, 4)
                        if b >= 2:
                            e.wait_ge(hy_done, b - 1)
                        for q in range(2):
                            m = e.matmul(psum[:, 2 * (b % 2) + q, :], ident[0:NS, b:b + 1].to_broadcast([NS, P]), BCs[:, q, :], start=True, stop=True)
                        m.then_inc(bcb_done, 1)

                def dve(S, e):
                    e.wait_ge(dte_ready, 1)
                    e.wait_ge(hst_stored, 64)
                    link(e, "dve", e.tensor_tensor(xdt[:, :, :], xbc[:, 0:16, NP:T], dtE[:, :, 0:NS], ALU.mult))
                    for b in range(NS):
                        e.wait_ge(dec_done, b + 1)
                        e.wait_ge(bcb_done, b + 1)
                        for j in range(16):
                            g = j // 4
                            v = hb[:, b % 2, j, :]
                            ins = e.scalar_tensor_tensor(out=v, in0=psum[:, 2 * (b % 2), g * P:(g + 1) * P], scalar=xdt[:, j, b:b + 1],
                                                         in1=v, op0=ALU.mult, op1=ALU.add)
                        ins.then_inc(h_new, 1)
                        e.wait_ge(h_new, b + 1)
                        if b >= 1:
                            e.wait_ge(hy_done, b)
                        for j in range(16):
                            g = j // 4
                            ins = e.tensor_tensor_reduce(jk[:, j, :], hb[:, b % 2, j, :], psum[:, 2 * (b % 2) + 1, g * P:(g + 1) * P],
                                                         1.0, 0.0, ALU.mult, ALU.add, ysm[:, j, b:b + 1])
                        ins.then_inc(hy_done, 1)
                    e.wait_ge(hy_done, NS)
                    v = xbc[:, 0:16, NP:T]
                    link(e, "dve", e.tensor_tensor(v, v, dcol[:, :].unsqueeze(2).to_broadcast([P, 16, NS]), ALU.mult))
                    e.tensor_tensor(v, v, ysm[:, :, :], ALU.add).then_inc(ssd_out, 1)
            stages.append(SSDSample())

            yh = place("yh", [P, 16, T], F32R, at=R2)
            yl = place("yl", [P, 16, T], F32R, at=R2 + 16 * T * 4)
            y = xbc[:, 0:16, :]
            az, dz = gated(y, ACT.Silu)
            Linear(W, 8, KD, 2, by_cols(W, 0), (xnh, xnl), ready=at_least(ssd_out, 1), act=az, dve=dz)
            z_out = evicted()
            Stat(xbc, 4, 4, rstd4, lambda e, t: z_out(e) if t == 0 else None)
            hb_stored = lambda e: [e.wait_ge(q, 64) for q in hb_out] and None
            Apply(xbc, 4, 4, rstd4, G_SSD, yh, yl, wait=hb_stored)
            y_split = xn_wait()

            v_tm = place("v_tm", [P, 2, 2048], at=R0)
            k_tm = place("k_tm", [P, 2, 1024], at=R0 + 16384)
            ra = place("ra", [P, 2, 384], at=R2 + 32 * T * 4)
            vs = place("vs", [NS, 2048], at=norm_at)
            rst2 = place("rst2", [P, 512], at=R2 + 32 * T * 4)
            rst = place("rst", [P, 512], at=norm_at + 8192)
            items = []
            for t in range(0, 16, 2):
                items.append(([(vf[:, t + q // 2, (q % 2) * P:(q % 2 + 1) * P], P, P, (q % 2) * 256 + (q // 2) * P) for q in range(4)],
                              lambda e, bank, par, t=t: mv(e, par, v_tm[:, :, t * P:(t + 2) * P], bank.rearrange("p (b n) -> p b n", b=2))))
            for h in range(4):
                def ev(e, bank, par, h=h):
                    for b in range(2):
                        ins = mv(e, par, k_tm[:, b, h * 256:(h + 1) * 256], bank[:, b * 256:(b + 1) * 256], scale=tail[:, 2 * h + b:2 * h + b + 1])
                    return ins
                items.append(([(kf[:, 2 * h + q // 2, (q % 2) * P:(q % 2 + 1) * P], P, P, (q % 2) * 256 + (q // 2) * P) for q in range(4)], ev))
            for t0 in range(0, 16, 4):
                items.append(([(vf[:, t, NP:T], P, NS, (t - t0) * P) for t in range(t0, t0 + 4)],
                              lambda e, bank, par, t0=t0: mv(e, par, vs[:, t0 * P:(t0 + 4) * P], bank[0:NS, :])))
            Turn(items, ready=y_split)
            vt_ready = turned()
            rs_done = sem_of("ret_scores")
            ra_ready = sem_of("ret_att")
            ro_done = sem_of("ret_out_done")
            ro_out = sem_of("ret_out_copied")
            rS_done = sem_of("ret_state_done")
            rS_out = sem_of("ret_state_copied")
            rS_stored = [sem_of("ret_state_stored0"), sem_of("ret_state_stored1")]

            class RetPrompt(Stage):

                def pe(S, e):
                    vt_ready(e)
                    for h in range(RH):
                        if h >= 2:
                            e.wait_ge(ra_ready, h - 1)
                        for b in range(2):
                            o = psum[:, 4 + h % 2, b * NP:b * NP + NP - b * P]
                            for d in range(2):
                                m = e.matmul(o, kf[:, 2 * h + d, b * P:(b + 1) * P], qf[:, 2 * h + d, b * P:NP], start=d == 0, stop=d == 1)
                        m.then_inc(rs_done, 1)
                        if h > 0:
                            S.values(e, h - 1)
                    S.values(e, RH - 1)
                    for i in range(2 * RH):
                        h, d = i // 2, i % 2
                        if i >= 2:
                            e.wait_ge(rS_out, i - 1)
                        for b in range(2):
                            m = e.matmul(psum[:, 2 + i % 2, :], k_tm[:, b, h * 256 + d * P:h * 256 + (d + 1) * P],
                                         v_tm[:, b, h * 512:(h + 1) * 512], start=b == 0, stop=b == 1)
                        m.then_inc(rS_done, 1)

                def values(S, e, h):
                    e.wait_ge(ra_ready, h + 1)
                    for q in range(4):
                        n = 2 * h + q // 2
                        if q % 2 == 0 and n >= 2:
                            e.wait_ge(ro_out, n - 1)
                        c = h * 512 + q * P
                        o = psum[:, n % 2, (q % 2) * NP:(q % 2 + 1) * NP]
                        e.matmul(o, v_tm[:, 0, c:c + P], ra[:, h % 2, 0:NP], start=True, stop=False)
                        m = e.matmul(o[:, P:NP], v_tm[:, 1, c:c + P], ra[:, h % 2, NP:384], start=False, stop=True)
                        if q % 2 == 1:
                            m.then_inc(ro_done, 1)

                def dve(S, e):
                    for h in range(RH):
                        e.wait_ge(rs_done, h + 1)
                        if h >= 2:
                            e.wait_ge(ro_done, 2 * h - 2)
                        e.tensor_tensor(ra[:, h % 2, 0:NP], psum[:, 4 + h % 2, 0:NP], dtab[:, h, :], ALU.mult)
                        e.tensor_tensor(ra[:, h % 2, NP:384], psum[:, 4 + h % 2, NP:384], dtab[:, h, 0:P], ALU.mult).then_inc(ra_ready, 1)

                def act(S, e):
                    vt_ready(e)
                    for n in range(2 * RH):
                        e.wait_ge(ro_done, n + 1)
                        nc.scalar.activation(vf[:, 2 * n:2 * n + 2, 0:NP], psum[:, n % 2, :].rearrange("p (q n) -> p q n", q=2),
                                             ACT.Copy).then_inc(ro_out, 1)
                    for i in range(2 * RH):
                        e.wait_ge(rS_done, i + 1)
                        if i >= 2:
                            e.wait_ge(rS_stored[i % 2], 16 * (i // 2))
                        buf = (rst, rst2)[i % 2]
                        nc.scalar.activation(buf[:, :], psum[:, 2 + i % 2, :], ACT.Copy).then_inc(rS_out, 1)
                        e.wait_ge(rS_out, i + 1)
                        e.dma_start(O[8][0, 0, i // 2, (i % 2) * P:(i % 2 + 1) * P, :], buf[:, :]).then_inc(rS_stored[i % 2], 16)

            stages.append(RetPrompt())

            NB_ = 6
            sb = place("sb", [P, NB_, 2, 512], at=R0)
            sb_in = [sem_of(f"sb_in{i}") for i in range(NB_)]
            sb_out = [sem_of(f"sb_out{i}") for i in range(NB_)]
            sdec = sem_of("ret_decayed")
            vb_done = sem_of("ret_vb")
            s_new = sem_of("ret_s_new")
            s_used = sem_of("ret_s_used")
            rsm_out = sem_of("ret_sample_out")
            gam = [1.0 - 2.0 ** (-5 - h) for h in range(RH)]
            sv = lambda t, i: t[0, i // RH, i % RH].rearrange("(two p) n -> p two n", two=2)

            class RetSample(Stage):

                def pool(S, e):
                    e.wait_ge(rS_done, 2 * RH)
                    for i in range(NS * RH):
                        n = i // NB_
                        if n:
                            e.wait_ge(sb_out[i % NB_], 16 * n)
                            e.wait_ge(s_used, i - NB_ + 1)
                        e.dma_start(sb[:, i % NB_, :, :], sv(A["state_ret"], i)).then_inc(sb_in[i % NB_], 16)

                def keep(S, e, i):
                    e.wait_ge(s_new, i + 1)
                    e.dma_start(sv(O[9], i), sb[:, i % NB_, :, :]).then_inc(sb_out[i % NB_], 16)

                def act(S, e):
                    for i in range(NS * RH):
                        e.wait_ge(sb_in[i % NB_], 16 * (i // NB_ + 1))
                        v = sb[:, i % NB_, :, :]
                        nc.scalar.activation(v, v, ACT.Copy, scale=gam[i % RH]).then_inc(sdec, 1)
                        if i >= 2:
                            S.keep(e, i - 2)
                    for i in (NS * RH - 2, NS * RH - 1):
                        S.keep(e, i)

                def dve(S, e):
                    for i in range(NS * RH):
                        b, h = i // RH, i % RH
                        e.wait_ge(sdec, i + 1)
                        e.wait_ge(vb_done, i + 1)
                        for d in range(2):
                            v = sb[:, i % NB_, d, :]
                            ins = e.scalar_tensor_tensor(out=v, in0=psum[:, i % 4, :], scalar=kf[:, 2 * h + d, NP + b:NP + b + 1], in1=v,
                                                         op0=ALU.mult, op1=ALU.add)
                        ins.then_inc(s_new, 1)
                    e.wait_ge(s_used, NS * RH)
                    e.tensor_copy(vf[:, :, NP:T], psum[:, 4, 0:128].rearrange("p (t b) -> p t b", t=16)).then_inc(rsm_out, 1)

                def pe(S, e):
                    e.wait_ge(rS_out, 2 * RH)
                    e.wait_ge(ra_ready, RH)
                    e.wait_ge(ro_out, 2 * RH)

                    def bc(i):
                        if i >= 4:
                            e.wait_ge(s_new, i - 3)
                        e.matmul(psum[:, i % 4, :], ident[0:NS, i // RH:i // RH + 1].to_broadcast([NS, P]),
                                 vs[:, (i % RH) * 512:(i % RH + 1) * 512], start=True, stop=True).then_inc(vb_done, 1)
                    for i in range(3):
                        bc(i)
                    for i in range(NS * RH):
                        if i + 3 < NS * RH:
                            bc(i + 3)
                        b, h = i // RH, i % RH
                        e.wait_ge(s_new, i + 1)
                        for q in range(4):
                            o = psum[:, 4, (4 * h + q) * NS + b:(4 * h + q) * NS + b + 1]
                            for d in range(2):
                                m = e.matmul(o, sb[:, i % NB_, d, q * P:(q + 1) * P], qf[:, 2 * h + d, NP + b:NP + b + 1], start=d == 0, stop=d == 1)
                        m.then_inc(s_used, 1)
            stages.append(RetSample())
            rh_ = place("rh", [P, 16, T], F32R, at=R1)
            rl_ = place("rl", [P, 16, T], F32R, at=R0)
            Stat(vf, 4, 4, rstd4, lambda e, t: e.wait_ge(rsm_out, 1) if t == 0 else None)
            ag, dg = gated(vf, ACT.Silu)
            Linear(W, 8, KD, 2, by_cols(W, 9248), (xnh, xnl), act=ag, dve=dg)
            g_out = evicted()
            Apply(vf, 4, 4, rstd4, None, rh_, rl_, wait=all_of(g_out, lambda e: [e.wait_ge(sb_out[i], 16 * ((NS * RH - i + NB_ - 1) // NB_)) for i in range(NB_)] and None))
            Linear(A["w_out_ab"][0], 16, 16, 1, by_rows(A["w_out_ab"][0], 16), [(yh, yl), (rh_, rl_)], ready=xn_wait(),
                   dve=add_to_x(1.0, 1), cpu=2)

        X = {n: sem_of("x_" + n) for n in ("mem_in", "score", "nmax", "exp", "prob", "pv", "oh", "ol", "qb", "kused", "smax", "sexp", "sprob",
                                           "spv", "soh", "sol")}
        kc_in = [sem_of("kc_in0"), sem_of("kc_in1")]
        vc_in = [sem_of("vc_in0"), sem_of("vc_in1")]
        xbuf = None

        def cross_buffers():
            R = REG
            return dict(
                mtok=place("mtok", [P, 2, D], at=R), mT=place("mT", [P, KD, MEM], at=R + 8192),
                mh=place("mh", [P, KD, MEM], F32R, at=R + 16384), ml=place("ml", [P, KD, MEM], F32R, at=R + 24576),
                Kf=place("Kf", [P, KD, MEM], at=R + 32768), Vt=place("Vt", [P, 2, D], at=R + 40960),
                Kt=place("Kt", [P, 2, D], at=R + 49152), xq=place("xq", [P, KD, T], at=R + 57344),
                pp=place("pp", [P, 8, MEM], at=R + 65792), pT=place("pT", [P, XH, 512], at=R + 73984),
                qtm=place("qtm", [NS, 2, 512], at=R + 82176), sc=place("sc", [P, 2, 32], at=R + 86272),
                ps_=place("ps_", [32, MEM], at=R + 86528), pTs=place("pTs", [P, 64], at=R + 87552),
                st=place("st", [P, 4, 8], at=R + 87808), sst=place("sst", [32, 4], at=R + 87936),
                kc=place("kc", [P, 2, 2, D], at=R), vc=place("vc", [P, 2, 2, D], at=R + 16384))

        def cross(layer):
            nonlocal xbuf
            if xbuf is None:
                xbuf = cross_buffers()
            B = type("B", (), xbuf)
            lc = layer
            gcol = G_X + 8 * layer
            region_free = evicted()
            W = A["w_xkv"][layer]

            kept = pending[:]
            pending.clear()

            class Load(Stage):
                def pool(S, e):
                    region_free(e)
                    for q, n in kept:
                        e.wait_ge(q, n)
                    e.dma_start(B.mtok[:, :, :], A["mem_prompt"].rearrange("o (b p) d -> p (o b) d", p=P)).then_inc(X["mem_in"], 16)
            stages.append(Load())
            norm_x(gcol)
            xn_ok = xn_wait()
            Turn([([(B.mtok[:, q % 2, (k + q // 2) * P:(k + q // 2 + 1) * P], P, P, q * P) for q in range(4)],
                   lambda e, bank, par, k=k: mv(e, par, B.mT[:, k:k + 2, :], bank.rearrange("p (k n) -> p k n", k=2))) for k in range(0, KD, 2)],
                 ready=at_least(X["mem_in"], 16 * (layer + 1)))
            mt = turned()
            Stat(B.mT, 1, KD, rstd1, lambda e, t: mt(e) if t == 0 else None, n=MEM)
            Apply(B.mT, 1, KD, rstd1, G_MEM + 8 * layer, B.mh, B.ml, n=MEM)
            Linear(W, 4, KD, 2, by_cols(W, 0), (B.mh, B.ml), ready=xn_wait(), dve=copy_out(B.Kf, n=MEM), cols=MEM)

            def v_out(e, l, par, use):
                e.tensor_copy(B.Vt[:, :, bass.ds(l * 256, 256)], psum[:, 2 * par:2 * par + 2, 0:256]).then_inc(bank_free, 1)
            Linear(W, 4, KD, 2, by_cols(W, D), (B.mh, B.ml), dve=v_out, cols=256, turned=True)
            kv_out = evicted()
            Turn([([(B.Kf[:, k0 + q, b * P:(b + 1) * P], P, P, q * P) for q in range(4)],
                   lambda e, bank, par, b=b, k0=k0: mv(e, par, B.Kt[:, b, k0 * P:(k0 + 4) * P], bank)) for b in range(2) for k0 in (0, 4)],
                 ready=kv_out)
            kt_ready = turned()

            class Keep(Stage):
                def pool(S, e):
                    kt_ready(e)
                    kv_out(e)
                    v = lambda o: o[layer, 0].rearrange("(b p) h d -> p b (h d)", p=P)
                    store(e, "pool", v(O[2]), B.Kt[:, :, :])
                    store(e, "pool", v(O[3]), B.Vt[:, :, :])
                    for b in range(2):
                        load_cache(e, "cache_mem_k", B.kc, kc_in, b)
                        load_cache(e, "cache_mem_v", B.vc, vc_in, b)

            def load_cache(e, name, buf, sems, b):
                e.dma_start(buf[:, b % 2, :, :], A[name][layer, b].rearrange("(m p) h d -> p m (h d)", p=P)).then_inc(sems[b % 2], 16)
            stages.append(Keep())
            tot["stores"] += 32
            pending.append((stored["pool"], tot["stores"]))
            Wq = A["w_xq"][layer]
            Linear(Wq, 4, KD, 2, by_cols(Wq, 0), (xnh, xnl), ready=xn_ok, dve=copy_out(B.xq))
            q_out = evicted()

            class Scores(Stage):
                def pe(S, e):
                    q_out(e)
                    for u in range(8):
                        h, lb = u // 2, u % 2
                        if u >= 2:
                            e.wait_ge(X["exp"], 8 * lc + u - 1)
                        for d in range(2):
                            m = e.matmul(psum[:, u % 2, 0:MEM], B.xq[:, 2 * h + d, lb * P:(lb + 1) * P], B.Kf[:, 2 * h + d, :], start=d == 0, stop=d == 1)
                        m.then_inc(X["score"], 1)

                def dve(S, e):
                    for u in range(8):
                        e.wait_ge(X["score"], 8 * lc + u + 1)
                        link(e, "dve", e.tensor_reduce(B.st[:, 0, u:u + 1], psum[:, u % 2, 0:MEM], AX, ALU.max))
                        e.tensor_scalar(B.st[:, 1, u:u + 1], B.st[:, 0, u:u + 1], -XD ** -0.5, None, ALU.mult).then_inc(X["nmax"], 1)
                        if u >= 1:
                            S.divide(e, u - 1)
                    S.divide(e, 7)

                def divide(S, e, u):
                    e.wait_ge(X["exp"], 8 * lc + u + 1)
                    link(e, "dve", e.reciprocal(B.st[:, 3, u:u + 1], B.st[:, 2, u:u + 1]))
                    e.tensor_scalar(B.pp[:, u, :], B.pp[:, u, :], B.st[:, 3, u:u + 1], None, ALU.mult).then_inc(X["prob"], 1)

                def act(S, e):
                    for u in range(8):
                        e.wait_ge(X["nmax"], 8 * lc + u + 1)
                        nc.scalar.activation(B.pp[:, u, :], psum[:, u % 2, 0:MEM], ACT.Exp, scale=XD ** -0.5, bias=B.st[:, 1, u:u + 1],
                                             accum_out=B.st[:, 2, u:u + 1]).then_inc(X["exp"], 1)
            stages.append(Scores())
            Turn([([(B.pp[:, 2 * h + lb, m * P:(m + 1) * P], P, P, m * 256 + lb * P) for m in range(2) for lb in range(2)],
                   lambda e, bank, par, h=h: mv(e, par, B.pT[:, h, :], bank)) for h in range(XH)], ready=at_least(X["prob"], 8 * lc + 8))
            pt_ready = turned()
            Turn([([(B.xq[:, k, NP:T], P, NS, (k - k0) * P) for k in range(k0, k0 + 4)],
                   lambda e, bank, par, k0=k0: mv(e, par, B.qtm[:, k0 // 4, :], bank[0:NS, :])) for k0 in (0, 4)])
            qt_ready = turned()

            class Values(Stage):
                def pe(S, e):
                    pt_ready(e)
                    for i in range(8):
                        if i >= 2:
                            e.wait_ge(X["ol"], 8 * lc + i - 1)
                        h, d = i // 2, i % 2
                        for m_ in range(2):
                            m = e.matmul(psum[:, 2 + i % 2, 0:NP], B.Vt[:, m_, h * XD + d * P:h * XD + (d + 1) * P], B.pT[:, h, m_ * 256:(m_ + 1) * 256],
                                         start=m_ == 0, stop=m_ == 1)
                        m.then_inc(X["pv"], 1)

                def act(S, e):
                    for i in range(8):
                        e.wait_ge(X["pv"], 8 * lc + i + 1)
                        nc.scalar.activation(xnh[:, i, 0:NP], psum[:, 2 + i % 2, 0:NP], ACT.Copy).then_inc(X["oh"], 1)

                def dve(S, e):
                    for i in range(8):
                        e.wait_ge(X["oh"], 8 * lc + i + 1)
                        e.tensor_tensor(xnl[:, i, 0:NP], psum[:, 2 + i % 2, 0:NP], xnh[:, i, 0:NP].bitcast(F32), ALU.subtract).then_inc(X["ol"], 1)
            stages.append(Values())

            class SampleScores(Stage):
                def pool(S, e):
                    for b in range(2, NS):
                        e.wait_ge(X["kused"], NS * lc + b - 1)
                        load_cache(e, "cache_mem_k", B.kc, kc_in, b)

                def pe(S, e):
                    qt_ready(e)
                    e.wait_ge(X["exp"], 8 * lc + 8)
                    for b in range(NS):
                        if b >= 2:
                            e.wait_ge(X["kused"], NS * lc + b - 1)
                        elif b == 1:
                            e.wait_ge(X["ol"], 8 * lc + 8)
                        for q in range(2):
                            m = e.matmul(psum[:, 2 * (b % 2) + q, :], ident[0:NS, b:b + 1].to_broadcast([NS, P]), B.qtm[:, q, :], start=True, stop=True)
                        m.then_inc(X["qb"], 1)

                def dve(S, e):
                    for b in range(NS):
                        e.wait_ge(kc_in[b % 2], 16 * (4 * lc + b // 2 + 1))
                        e.wait_ge(X["qb"], NS * lc + b + 1)
                        for m_ in range(2):
                            for h in range(XH):
                                k = B.kc[:, b % 2, m_, h * XD:(h + 1) * XD]
                                ins = e.tensor_tensor_reduce(k, k, psum[:, 2 * (b % 2) + h // 2, (h % 2) * XD:(h % 2 + 1) * XD], XD ** -0.5, 0.0,
                                                             ALU.mult, ALU.add, B.sc[:, m_, b * XH + h:b * XH + h + 1])
                        ins.then_inc(X["kused"], 1)
            stages.append(SampleScores())
            Turn([([(B.sc[:, m_, :], P, 32, m_ * P) for m_ in range(2)],
                   lambda e, bank, par: mv(e, par, B.ps_[:, :], bank[0:32, 0:MEM]))], ready=at_least(X["kused"], NS * lc + NS))
            s_ready = turned()

            class SampleSoftmax(Stage):
                def dve(S, e):
                    s_ready(e)
                    link(e, "dve", e.tensor_reduce(B.sst[:, 0:1], B.ps_[:, :], AX, ALU.max))
                    e.tensor_scalar(B.sst[:, 1:2], B.sst[:, 0:1], -1.0, None, ALU.mult).then_inc(X["smax"], 1)
                    e.wait_ge(X["sexp"], lc + 1)
                    link(e, "dve", e.reciprocal(B.sst[:, 3:4], B.sst[:, 2:3]))
                    e.tensor_scalar(B.ps_[:, :], B.ps_[:, :], B.sst[:, 3:4], None, ALU.mult).then_inc(X["sprob"], 1)

                def act(S, e):
                    s_ready(e)
                    e.wait_ge(X["smax"], lc + 1)
                    nc.scalar.activation(B.ps_[:, :], B.ps_[:, :], ACT.Exp, bias=B.sst[:, 1:2], accum_out=B.sst[:, 2:3]).then_inc(X["sexp"], 1)
            stages.append(SampleSoftmax())
            Turn([([(B.ps_[:, m_ * P:(m_ + 1) * P], 32, P, m_ * 32) for m_ in range(2)],
                   lambda e, bank, par: mv(e, par, B.pTs[:, :], bank[:, 0:64]))], ready=at_least(X["sprob"], lc + 1))
            ps_ready = turned()

            class SampleValues(Stage):
                def pool(S, e):
                    for b in range(2, NS):
                        e.wait_ge(X["spv"], NS * lc + b - 1)
                        load_cache(e, "cache_mem_v", B.vc, vc_in, b)

                def pe(S, e):
                    ps_ready(e)
                    for b in range(NS):
                        e.wait_ge(vc_in[b % 2], 16 * (4 * lc + b // 2 + 1))
                        for t in range(KD):
                            for m_ in range(2):
                                m = e.matmul(psum[:, 5, t * NS + b:t * NS + b + 1], B.vc[:, b % 2, m_, t * P:(t + 1) * P],
                                             B.pTs[:, m_ * 32 + b * XH + t // 2:m_ * 32 + b * XH + t // 2 + 1], start=m_ == 0, stop=m_ == 1)
                        m.then_inc(X["spv"], 1)

                def act(S, e):
                    e.wait_ge(X["spv"], NS * lc + NS)
                    nc.scalar.activation(xnh[:, :, NP:T], psum[:, 5, 0:64].rearrange("p (t b) -> p t b", t=KD), ACT.Copy).then_inc(X["soh"], 1)

                def dve(S, e):
                    e.wait_ge(X["soh"], lc + 1)
                    e.tensor_tensor(xnl[:, :, NP:T], psum[:, 5, 0:64].rearrange("p (t b) -> p t b", t=KD), xnh[:, :, NP:T].bitcast(F32),
                                    ALU.subtract).then_inc(X["sol"], 1)
            stages.append(SampleValues())
            Wo = A["w_xo"][layer]
            Linear(Wo, 4, KD, 2, by_cols(Wo, 0), (xnh, xnl), ready=at_least(X["sol"], lc + 1), dve=add_to_x(1.0, 2))

        def mixer_c():
            W = A["w_in_c"][0]
            R = REG
            q = place("cq", [P, 4, T], at=R)
            k = place("ck", [P, 4, T], at=R + 4 * T * 4)
            v = place("cv", [P, 8, T], at=R + 8 * T * 4)
            R2 = R + 16 * T * 4
            ktm = place("cktm", [P, 2, 512], at=R2)
            vtm = place("cvtm", [P, 2, 1024], at=R2 + 4096)
            qk = place("cqk", [P, 4, 384], at=R2 + 12288)
            ee = place("cee", [P, 4, 384], at=R2 + 18432)
            gcs = place("cgcs", [P, 4, 4], at=R2 + 24576)
            den = place("cden", [P, 4, NP], at=R2 + 24640)
            cst = place("ccst", [P, 4, 256], at=R2 + 28736)
            nst = place("cnst", [P, 4], at=R2 + 32832)
            vsr = place("cvs", [NS, 1024], at=R2 + 32864)
            cb = place("ccb", [P, 4, 4, 256], at=R2 + 36960)
            fib = place("cfib", [P, 4, 24], at=R2 + 53344)
            ki = place("cki", [P, 4, NS], at=R2 + 53728)
            nT = place("cnT", [P, NS, 4], at=R2 + 53856)
            qn = place("cqn", [P, NS, 4], at=R2 + 53984)
            dn = place("cdn", [P, NS, 4], at=R2 + 54112)
            nrow = place("cnrow", [32, P], at=R2 + 54240)
            gr = place("cgr", [4, 8, T], at=R2 + 54752)
            sm = place("csm", [4, 6, NS], at=R2 + 54752 + 8448)
            mtok2 = sem_of("c_in")
            n_in = sem_of("c_n_in")
            S_ = {n: sem_of("c_" + n) for n in ("gates", "abs", "ln", "rows", "wl", "srow", "sexp", "fi", "qk", "qkm", "bc", "ebc", "gap", "exp", "att",
                                                 "den", "guard", "rden", "num", "hh", "st", "stc", "sts", "n_new", "qn", "dns", "vb", "dec", "cnew",
                                                 "cused", "hs", "bgd", "kib")}
            region_free = evicted()

            class Load(Stage):
                def pool(S, e):
                    region_free(e)
                    with nc.allow_non_contiguous_dma(reason="a few numbers, one on each partition"):
                        e.dma_start(cols[0:4, 44:45], A["mlstm_i_bias"].rearrange("l h -> h l")).then_inc(mtok2, 16)
                        e.dma_start(cols[0:4, 45:46], A["mlstm_f_bias"].rearrange("l h -> h l")).then_inc(mtok2, 16)
                        e.dma_start(sm[:, 0, :], A["state_mlstm_m"][0].rearrange("b h -> h b")).then_inc(mtok2, 16)
                    e.dma_start(nrow[:, :], A["state_mlstm_n"].rearrange("l b h d -> (l b h) d")).then_inc(n_in, 16)
            stages.append(Load())
            Linear(W, 2, KD, 2, by_cols(W, 0), (xnh, xnl), ready=xn_wait(), dve=copy_out(q))
            Linear(W, 2, KD, 2, by_cols(W, 512), (xnh, xnl), dve=copy_out(k, MDK ** -0.5))
            Linear(W, 4, KD, 2, by_cols(W, 1024), (xnh, xnl), dve=copy_out(v))

            def gates(e, l, par, use):
                e.wait_ge(mtok2, 48)
                e.tensor_scalar(gr[:, 0, :], psum[0:4, 2 * par, 0:T], cols[0:4, 44:45], None, ALU.add)
                e.tensor_scalar(gr[:, 1, :], psum[0:4, 2 * par + 1, 0:T], cols[0:4, 45:46], None, ALU.add).then_inc(bank_free, 1)
            Linear(W, 1, KD, 2, two_cols(W, 2048, 2052), (xnh, xnl), dve=gates)
            in_out = evicted()

            class Rows(Stage):
                def dve(S, e):
                    go = lambda ins: link(e, "dve", ins)
                    in_out(e)
                    e.scalar_tensor_tensor(out=gr[:, 2, :], in0=gr[:, 1, :], scalar=-1.0, in1=gr[:, 1, :], op0=ALU.mult, op1=ALU.max).then_inc(S_["abs"], 1)
                    e.wait_ge(S_["ln"], 1)
                    go(e.scalar_tensor_tensor(out=gr[:, 3, :], in0=gr[:, 1, :], scalar=0.0, in1=gr[:, 2, :], op0=ALU.min, op1=ALU.subtract))
                    c = slice(0, NP)
                    go(e.tensor_tensor_scan(gr[:, 4, 0:P], ones[0:4, :], gr[:, 3, 0:P], 0.0, ALU.mult, ALU.add))
                    go(e.tensor_tensor_scan(gr[:, 4, P:NP], ones[0:4, :], gr[:, 3, P:NP], gr[:, 4, P - 1:P], ALU.mult, ALU.add))
                    go(e.tensor_tensor(gr[:, 5, c], gr[:, 0, c], gr[:, 4, c], ALU.subtract))
                    go(e.tensor_tensor_scan(gr[:, 2, c], gr[:, 5, c], gr[:, 5, c], 0.0, ALU.max, ALU.max))
                    go(e.tensor_scalar(gr[:, 6, c], gr[:, 2, c], -1.0, None, ALU.mult))
                    go(e.tensor_tensor(gr[:, 7, c], gr[:, 6, c], gr[:, 4, c], ALU.subtract))
                    e.tensor_scalar(cols[0:4, 46:47], gr[:, 7, NP - 1:NP], -1.0, None, ALU.mult).then_inc(S_["rows"], 1)
                    go(e.tensor_tensor(sm[:, 1, :], gr[:, 3, NP:T], sm[:, 0, :], ALU.add))
                    go(e.tensor_tensor(sm[:, 2, :], sm[:, 1, :], gr[:, 0, NP:T], ALU.max))
                    go(e.tensor_tensor(sm[:, 3, :], sm[:, 1, :], sm[:, 2, :], ALU.subtract))
                    go(e.tensor_tensor(sm[:, 4, :], gr[:, 0, NP:T], sm[:, 2, :], ALU.subtract))
                    e.tensor_scalar(sm[:, 5, :], sm[:, 2, :], -1.0, None, ALU.mult).then_inc(S_["srow"], 1)

                def act(S, e):
                    e.wait_ge(S_["abs"], 1)
                    link(e, "act", nc.scalar.activation(gr[:, 2, :], gr[:, 2, :], ACT.Exp, scale=-1.0))
                    nc.scalar.activation(gr[:, 2, :], gr[:, 2, :], ACT.Ln, bias=1.0).then_inc(S_["ln"], 1)
                    e.wait_ge(S_["rows"], 1)
                    nc.scalar.activation(gr[:, 1, 0:NP], gr[:, 5, 0:NP], ACT.Exp, bias=gr[:, 6, NP - 1:NP]).then_inc(S_["wl"], 1)
                    e.wait_ge(S_["srow"], 1)
                    nc.scalar.activation(sm[:, 3:6, :], sm[:, 3:6, :], ACT.Exp).then_inc(S_["sexp"], 1)

                def pool(S, e):
                    e.wait_ge(S_["srow"], 1)
                    with nc.allow_non_contiguous_dma(reason="the stabilisers: 36 numbers"):
                        store(e, "pool", O[14].rearrange("l o h -> (l h) o"), cols[0:4, 46:47])
                        store(e, "pool", O[15][0].rearrange("b h -> h b"), sm[:, 2, :])
            stages.append(Rows())
            gitem = [([(src, 4, P, j * 4) for j, src in enumerate((gr[:, 5, 0:P], gr[:, 5, P:NP], gr[:, 1, 0:P], gr[:, 1, P:NP]))],
                      lambda e, bank, par: mv(e, par, gcs[:, :, :], bank[:, 0:16].rearrange("p (j h) -> p j h", j=4)))]
            Turn(gitem, ready=at_least(S_["wl"], 1))
            g_ready = turned()
            four = lambda t, j: [(t[:, j + i // 2, (i % 2) * P:(i % 2 + 1) * P], P, P, (i % 2) * 256 + (i // 2) * P) for i in range(4)]
            items = []
            for h in (0, 2):
                def ev(e, bank, par, h=h):
                    for b in range(2):
                        for i in range(2):
                            c = (h + i) * P
                            ins = mv(e, par, ktm[:, b, c:c + P], bank[:, b * 256 + i * P:b * 256 + (i + 1) * P], scale=gcs[:, 2 + b, h + i:h + i + 1])
                    return ins
                items.append((four(k, h), ev))
            for t in range(0, 8, 2):
                items.append((four(v, t), lambda e, bank, par, t=t: mv(e, par, vtm[:, :, t * P:(t + 2) * P], bank.rearrange("p (b n) -> p b n", b=2))))
            for t0 in (0, 4):
                items.append(([(v[:, t, NP:T], P, NS, (t - t0) * P) for t in range(t0, t0 + 4)],
                              lambda e, bank, par, t0=t0: mv(e, par, vsr[:, t0 * P:(t0 + 4) * P], bank[0:NS, :])))
            items.append(([(nrow[:, :], 32, P, 0)], lambda e, bank, par: mv(e, par, nT[:, :, :], bank[:, 0:32].rearrange("p (b h) -> p b h", b=NS))))
            Turn(items, ready=at_least(n_in, 16), act_ready=g_ready, dve_ready=g_ready)
            t_ready = turned()

            class Prompt(Stage):
                def pe(S, e):
                    t_ready(e)
                    e.wait_ge(S_["sexp"], 1)
                    for h in range(MH):
                        if h >= 2:
                            e.wait_ge(S_["qkm"], h - 1)
                            e.wait_ge(S_["ebc"], h - 1)
                        e.matmul(psum[:, h % 2, 0:NP], k[:, h, 0:P], q[:, h, 0:NP], start=True, stop=True)
                        e.matmul(psum[:, h % 2, NP:384], k[:, h, P:NP], q[:, h, P:NP], start=True, stop=True).then_inc(S_["qk"], 1)
                        for j in range(2):
                            m = e.matmul(psum[:, 2 + h % 2, j * NP:(j + 1) * NP], ident[0:4, h:h + 1].to_broadcast([4, P]), gr[:, 6 + j, 0:NP], start=True, stop=True)
                        m.then_inc(S_["bc"], 1)
                    e.wait_ge(S_["qkm"], 4)
                    for h in range(MH):
                        e.wait_ge(S_["att"], h + 1)
                        if h >= 1:
                            e.wait_ge(S_["rden"], h)
                            e.wait_ge(S_["hh"], h)
                        e.matmul(psum[:, 4, 0:NP], ones[:, :], ee[:, h, 0:NP], start=True, stop=False)
                        e.matmul(psum[:, 4, P:NP], ones[:, :], ee[:, h, NP:384], start=False, stop=True).then_inc(S_["den"], 1)
                        for i in range(2):
                            c = h * MDV + i * P
                            o = psum[:, 5, i * NP:(i + 1) * NP]
                            e.matmul(o, vtm[:, 0, c:c + P], ee[:, h, 0:NP], start=True, stop=False)
                            m = e.matmul(o[:, P:NP], vtm[:, 1, c:c + P], ee[:, h, NP:384], start=False, stop=True)
                        m.then_inc(S_["num"], 1)
                    for h in range(MH):
                        if h >= 2:
                            e.wait_ge(S_["stc"], h - 1)
                        for b in range(2):
                            e.matmul(psum[:, h % 2, 0:256], ktm[:, b, h * P:(h + 1) * P], vtm[:, b, h * MDV:(h + 1) * MDV], start=b == 0, stop=b == 1)
                        for b in range(2):
                            m = e.matmul(psum[:, h % 2, 256:257], ktm[:, b, h * P:(h + 1) * P], ones[:, 0:1], start=b == 0, stop=b == 1)
                        m.then_inc(S_["st"], 1)
                    for h in range(MH):
                        m = e.matmul(psum[:, 2, h * 24:(h + 1) * 24], ident[0:4, h:h + 1].to_broadcast([4, P]), sm[:, 3:6, :].rearrange("h q b -> h (q b)"), start=True, stop=True)
                    m.then_inc(S_["fi"], 1)

                def dve(S, e):
                    t_ready(e)
                    for h in range(MH):
                        e.wait_ge(S_["qk"], h + 1)
                        e.tensor_tensor(qk[:, h, :], psum[:, h % 2, 0:384], mask[:, :], ALU.mult).then_inc(S_["qkm"], 1)
                        e.wait_ge(S_["bc"], h + 1)
                        e.tensor_scalar(ee[:, h, 0:NP], psum[:, 2 + h % 2, 0:NP], gcs[:, 0, h:h + 1], 0.0, ALU.add, ALU.min)
                        e.tensor_scalar(ee[:, h, NP:384], psum[:, 2 + h % 2, P:NP], gcs[:, 1, h:h + 1], 0.0, ALU.add, ALU.min).then_inc(S_["gap"], 1)
                    for h in range(MH):
                        e.wait_ge(S_["exp"], h + 1)
                        if h == 0:
                            e.wait_ge(S_["qkm"], 4)
                        e.tensor_tensor(ee[:, h, :], ee[:, h, :], qk[:, h, :], ALU.mult).then_inc(S_["att"], 1)
                    for h in range(MH):
                        e.wait_ge(S_["guard"], h + 1)
                        go = lambda ins: link(e, "dve", ins)
                        d = psum[:, 4, 0:NP]
                        go(e.tensor_tensor(ms[:, 0:NP], d, den[:, h, :], ALU.max))
                        e.scalar_tensor_tensor(out=den[:, h, :], in0=d, scalar=-1.0, in1=ms[:, 0:NP], op0=ALU.mult, op1=ALU.max).then_inc(S_["rden"], 1)
                        e.wait_ge(S_["rden"], h + 1)
                        go(e.reciprocal(den[:, h, :], den[:, h, :]))
                        e.wait_ge(S_["num"], h + 1)
                        e.tensor_tensor(v[:, 2 * h:2 * h + 2, 0:NP], psum[:, 5, :].rearrange("p (i n) -> p i n", i=2),
                                        den[:, h, :].unsqueeze(1).to_broadcast([P, 2, NP]), ALU.mult).then_inc(S_["hh"], 1)

                def act(S, e):
                    for h in range(MH):
                        e.wait_ge(S_["gap"], h + 1)
                        nc.scalar.activation(ee[:, h, :], ee[:, h, :], ACT.Exp).then_inc(S_["exp"], 1)
                        nc.scalar.activation(den[:, h, :], psum[:, 2 + h % 2, NP:512], ACT.Exp).then_inc(S_["ebc"], 1)
                    e.wait_ge(S_["ebc"], 4)
                    for h in range(MH):
                        e.wait_ge(S_["den"], h + 1)
                        nc.scalar.activation(nst[:, h:h + 1], ones[:, 0:1], ACT.Copy).then_inc(S_["guard"], 1)
                    for h in range(MH):
                        e.wait_ge(S_["st"], h + 1)
                        if h == 0:
                            e.wait_ge(S_["guard"], 4)
                        nc.scalar.activation(cst[:, h, :], psum[:, h % 2, 0:256], ACT.Copy)
                        nc.scalar.activation(nst[:, h:h + 1], psum[:, h % 2, 256:257], ACT.Copy).then_inc(S_["stc"], 1)
                    e.wait_ge(S_["fi"], 1)
                    nc.scalar.activation(fib[:, :, :], psum[:, 2, 0:96].rearrange("p (h q) -> p h q", h=4), ACT.Copy).then_inc(S_["bgd"], 1)

                def pool(S, e):
                    e.wait_ge(S_["stc"], 4)
                    store(e, "pool", O[10][0, 0].rearrange("h d e -> d h e"), cst[:, :, :])
                    with nc.allow_non_contiguous_dma(reason="the prompt's n: 512 numbers"):
                        store(e, "pool", O[12][0, 0].rearrange("h d -> d h"), nst[:, :])
            stages.append(Prompt())
            cin = [sem_of(f"cin{i}") for i in range(4)]
            cout = [sem_of(f"cout{i}") for i in range(4)]
            cview = lambda t, b: t[0, b].rearrange("h d e -> d h e")
            tot["stores"] += 80
            pending.extend([(stored["pool"], tot["stores"])] + [(c, 32) for c in cout])

            class SampleN(Stage):
                def dve(S, e):
                    go = lambda ins: link(e, "dve", ins)
                    e.wait_ge(S_["bgd"], 1)
                    hb_ = lambda j: fib[:, :, j * NS:(j + 1) * NS]
                    go(e.tensor_tensor(ki[:, :, :], k[:, :, NP:T], hb_(1), ALU.mult))
                    go(e.tensor_tensor(nT[:, :, :], nT[:, :, :], hb_(0).rearrange("p h b -> p b h"), ALU.mult))
                    e.tensor_tensor(nT[:, :, :], nT[:, :, :], ki[:, :, :].rearrange("p h b -> p b h"), ALU.add).then_inc(S_["n_new"], 1)
                    e.wait_ge(S_["n_new"], 1)
                    e.tensor_tensor(qn[:, :, :], nT[:, :, :], q[:, :, NP:T].rearrange("p h b -> p b h"), ALU.mult).then_inc(S_["qn"], 1)
                    e.wait_ge(S_["dns"], 1)
                    d = psum[:, 2, 128:160].rearrange("p (b h) -> p b h", b=NS)
                    go(e.tensor_tensor(dn[:, :, :], d, hb_(2).rearrange("p h b -> p b h"), ALU.max))
                    go(e.scalar_tensor_tensor(out=dn[:, :, :], in0=d, scalar=-1.0, in1=dn[:, :, :], op0=ALU.mult, op1=ALU.max))
                    go(e.reciprocal(dn[:, :, :], dn[:, :, :]))

                def pe(S, e):
                    e.wait_ge(S_["qn"], 1)
                    e.wait_ge(S_["bgd"], 1)
                    e.matmul(psum[:, 2, 128:160], ones[:, :], qn[:, :, :].rearrange("p b h -> p (b h)"), start=True, stop=True).then_inc(S_["dns"], 1)

                def pool(S, e):
                    for b in range(4):
                        e.dma_start(cb[:, b, :, :], cview(A["state_mlstm_c"], b)).then_inc(cin[b], 16)
            stages.append(SampleN())
            Turn([([(nT[:, :, :].rearrange("p b h -> p (b h)"), P, 32, 0)], lambda e, bank, par: mv(e, par, nrow[:, :], bank[0:32, 0:P]))],
                 ready=at_least(S_["n_new"], 1))
            nr_ready = turned()

            class SampleC(Stage):
                def pool(S, e):
                    nr_ready(e)
                    store(e, "pool", O[13].rearrange("l b h d -> (l b h) d"), nrow[:, :])
                    for b in range(4, NS):
                        e.wait_ge(cout[b % 4], 16)
                        e.wait_ge(S_["cused"], b - 3)
                        e.dma_start(cb[:, b % 4, :, :], cview(A["state_mlstm_c"], b)).then_inc(cin[b % 4], 16)

                def act(S, e):
                    e.wait_ge(S_["bgd"], 1)
                    for b in range(NS):
                        e.wait_ge(cin[b % 4], 16 * (b // 4 + 1))
                        for h in range(MH):
                            c = cb[:, b % 4, h, :]
                            ins = nc.scalar.activation(c, c, ACT.Copy, scale=fib[:, h, b:b + 1])
                        ins.then_inc(S_["dec"], 1)
                        if b >= 1:
                            S.keep(e, b - 1)
                    S.keep(e, NS - 1)

                def keep(S, e, b):
                    e.wait_ge(S_["cnew"], b + 1)
                    e.dma_start(cview(O[11], b), cb[:, b % 4, :, :]).then_inc(cout[b % 4], 16)

                def bank(S, b):
                    return 4 * (b % 2)

                def pe(S, e):
                    e.wait_ge(S_["stc"], 4)
                    e.wait_ge(S_["hh"], 4)

                    def bc(b):
                        if b >= 2:
                            e.wait_ge(S_["cnew"], b - 1)
                        for j in range(2):
                            m = e.matmul(psum[:, S.bank(b) + j, :], ident[0:NS, b:b + 1].to_broadcast([NS, P]), vsr[:, j * 512:(j + 1) * 512], start=True, stop=True)
                        m.then_inc(S_["vb"], 1)
                    bc(0)
                    bc(1)
                    for b in range(NS):
                        e.wait_ge(S_["cnew"], b + 1)
                        for h in range(MH):
                            for i in range(2):
                                t = (2 * h + i) * NS + b
                                m = e.matmul(psum[:, 3, t:t + 1], cb[:, b % 4, h, i * P:(i + 1) * P], q[:, h, NP + b:NP + b + 1], start=True, stop=True)
                        m.then_inc(S_["cused"], 1)
                        if b + 2 < NS:
                            bc(b + 2)

                def dve(S, e):
                    for b in range(NS):
                        e.wait_ge(S_["dec"], b + 1)
                        e.wait_ge(S_["vb"], b + 1)
                        for h in range(MH):
                            c = cb[:, b % 4, h, :]
                            ins = e.scalar_tensor_tensor(out=c, in0=psum[:, S.bank(b) + h // 2, (h % 2) * 256:(h % 2 + 1) * 256],
                                                         scalar=ki[:, h, b:b + 1], in1=c, op0=ALU.mult, op1=ALU.add)
                        ins.then_inc(S_["cnew"], 1)
                    e.wait_ge(S_["cused"], NS)
                    for i in range(2):
                        ins = e.tensor_tensor(v[:, i:8:2, NP:T], psum[:, 3, 0:64].rearrange("p (h i b) -> p h i b", h=4, i=2)[:, :, i, :],
                                              dn[:, :, :].rearrange("p b h -> p h b"), ALU.mult)
                    ins.then_inc(S_["hs"], 1)
            stages.append(SampleC())
            Stat(v, 4, 2, rstd4, lambda e, t: e.wait_ge(S_["hs"], 1) if t == 0 else None)
            ao, do = gated(v, ACT.Sigmoid)
            Linear(W, 4, KD, 2, by_cols(W, 2056), (xnh, xnl), act=ao, dve=do)
            o_out = evicted()
            Apply(v, 4, 2, rstd4, G_M, xnh, xnl, wait=o_out)
            Wo = A["w_out_c"][0]
            Linear(Wo, 4, KD, 2, by_cols(Wo, 0), (xnh, xnl), ready=xn_wait(), dve=add_to_x(1.0, 2))

        for layer in range(2):
            if layer == 0:
                u = None
                Stat(x, 1, KD, rstd1, lambda e, t: x_ready(e) if t == 0 else None)
                Apply(x, 1, KD, rstd1, G_FFN1, xnh, xnl)
            else:
                norm_x(G_FFN1 + 8 * layer)
            ffn(layer, A["w_ffn1_in"][layer], A["w_ffn1_out"][layer])
            if stop == f"f1_{layer}": break
            norm_x(G_MIX + 8 * layer)
            (mixer_ab if layer == 0 else mixer_c)()
            if stop == f"mix_{layer}": break
            cross(layer)
            if stop == f"x_{layer}": break
            norm_x(G_FFN2 + 8 * layer)
            ffn(layer, A["w_ffn2_in"][layer], A["w_ffn2_out"][layer])
            if stop == f"f2_{layer}": break

        yT = place("yT", [P, KD, T], at=REG)
        ytok = place("ytok", [P, 2, D], at=REG + 8448)
        ystok = place("ystok", [NS, D], at=REG + 8448 + 8192)
        Stat(x, 1, KD, rstd1, x_tile(tot["use"] + 2))
        Apply(x, 1, KD, rstd1, G_FIN, None, None, out=yT)
        y_scaled = sem_of("y_scaled")

        class Mark(Stage):
            def dve(S, e):
                nc.vector.memset(ms[:, 0:1], 0.0).then_inc(y_scaled, 1)
        stages.append(Mark())
        src = x if stop else yT
        items = []
        for b in range(2):
            for k0 in (0, 4):
                items.append(([(src[:, k, b * P:(b + 1) * P], P, P, (k - k0) * P) for k in range(k0, k0 + 4)],
                              lambda e, bank, par, b=b, k0=k0: mv(e, par, ytok[:, b, k0 * P:(k0 + 4) * P], bank)))
        for k0 in (0, 4):
            items.append(([(src[:, k, NP:T], P, NS, (k - k0) * P) for k in range(k0, k0 + 4)],
                          lambda e, bank, par, k0=k0: mv(e, par, ystok[:, k0 * P:(k0 + 4) * P], bank[0:NS, :])))
        Turn(items, ready=lambda e: e.wait_ge(y_scaled, 1))
        y_out = turned()

        class Final(Stage):
            def sp(S, e):
                y_out(e)
                store(e, "sp", O[0].rearrange("o (b p) d -> p (o b) d", p=P), ytok[:, :, :])
                store(e, "sp", O[1].rearrange("b o d -> (b o) d"), ystok[:, :])
        stages.append(Final())

        block = ctx.enter_context(nc.Block())

        @block.tensor
        def _(pe):
            for s in stages:
                s.pe(pe)

        @block.scalar
        def _(act):
            for s in stages:
                s.act(act)

        @block.vector
        def _(dve):
            for s in stages:
                s.dve(dve)

        @block.gpsimd
        def _(pool):
            for s in stages:
                s.pool(pool)

        @block.sync
        def _(sp):
            for s in stages:
                s.sp(sp)
            for q in stored:
                if stores[q]:
                    assert q == "sp" or stop or stores[q] == tot["stores"]
                    sp.wait_ge(stored[q], stores[q])


OUTS = [(1, NP, D), (NS, 1, D), (2, 1, MEM, XH, XD), (2, 1, MEM, XH, XD), (1, 1, 3, CONV_CH), (1, NS, 3, CONV_CH),
        (1, 1, SSD_HEADS, SSD_P, SSD_N), (1, NS, SSD_HEADS, SSD_P, SSD_N), (1, 1, RH, RDK, RDV), (1, NS, RH, RDK, RDV),
        (1, 1, MH, MDK, MDV), (1, NS, MH, MDK, MDV), (1, 1, MH, MDK), (1, NS, MH, MDK), (1, 1, MH), (1, NS, MH)]
PAST_LEN = 2048


def constants():
    s, t = np.arange(P)[:, None], np.arange(P)[None, :]
    upper = (s <= t).astype(np.float32)
    mask = np.concatenate([upper, np.ones((P, P), np.float32), upper], 1)
    half = RDK // 2
    inv = np.exp(np.float32(-np.log(10000.0)) * np.arange(half, dtype=np.float32) / np.float32(half)).astype(np.float32)
    pos = np.concatenate([np.arange(NP), np.full(NS, PAST_LEN)]).astype(np.float32)
    ang = (inv[:, None] * pos[None, :]).astype(np.float64)
    c, sn = np.cos(ang), np.sin(ang)
    rot = np.stack([c, sn, c * RDK ** -0.5, sn * RDK ** -0.5], 1).astype(np.float32)
    lg = np.log1p(-np.exp2(-5.0 - np.arange(RH)))
    diff = np.arange(NP)[None, :] - np.arange(P)[:, None]
    dtab = np.stack([np.where(diff >= 0, np.exp(np.maximum(diff, 0) * g), 0.0) for g in lg], 1).astype(np.float32)
    end = np.stack([np.exp((NP - 1 - b * P - np.arange(P)) * g) for g in lg for b in range(2)], 1).astype(np.float32)
    return {"c_ident": np.eye(P, dtype=np.float32), "c_mask": mask, "c_rot": rot, "c_dtab": dtab, "c_tail": end}


def kernel(**inputs):
    import concourse.bacc as bacc
    from concourse.bass_utils import run_bass_kernel_spmd

    nc = bacc.Bacc("TRN2", target_bir_lowering=False, num_devices=1)
    arrays, A = {}, {}
    for name, a in {**inputs, **constants()}.items():
        a = np.ascontiguousarray(a)
        arrays[f"in_{name}"] = a
        A[name] = nc.dram_tensor(f"in_{name}", a.shape, mybir.dt.from_np(a.dtype), kind="ExternalInput").ap()
    O = [nc.dram_tensor(f"out_{i}", shape, F32, kind="ExternalOutput").ap() for i, shape in enumerate(OUTS)]
    build(nc, A, O)
    r = run_bass_kernel_spmd(nc, [arrays], core_ids=[0])
    return tuple(r.results[0][f"out_{i}"] for i in range(len(OUTS)))
```

```python
from contextlib import ExitStack

import numpy as np
import concourse.bass as bass
from concourse import mybir

F32 = mybir.dt.float32
F32R = mybir.dt.float32r
ALU = mybir.AluOpType
ACT = mybir.ActivationFunctionType
AX = mybir.AxisListType.X

P = 128
D = 1024
KD = D // P
NP = 256
NS = 8
T = NP + NS
FF = 2816
KF = FF // P
EPS = 1e-6
SSD_HEADS, SSD_P, SSD_G, SSD_N = 32, 64, 4, 128
SSD_IN = SSD_HEADS * SSD_P
CONV_CH = SSD_IN + 2 * SSD_G * SSD_N
CT = CONV_CH // P
RH, RDK, RDV = 4, 256, 512
MH, MDK, MDV = 4, 128, 256
XH, XD, MEM = 4, 256, 256
SLOTS = 4
CHUNK = 2048


def build(nc, A, O):
    with ExitStack() as ctx:
        sem_of = lambda name: ctx.enter_context(nc.semaphore(name))
        base = (nc.sbuf_base + 63) // 64 * 64
        top = [base]

        def place(name, shape, dt=F32, at=None):
            n = int(np.prod(shape[1:])) * 4
            if at is None:
                at = top[0]
                top[0] += (n + 31) // 32 * 32
            return nc.alloc_sbuf_tensor_at(name, shape, dt, offset=at)

        raw = place("raw", [P, SLOTS, CHUNK])
        whi = place("whi", [P, 2, CHUNK], F32R)
        wlo = place("wlo", [P, 2, CHUNK], F32R)
        x = place("x", [P, KD, T])
        xnh = place("xnh", [P, KD, T], F32R)
        xnl = place("xnl", [P, KD, T], F32R)
        ident = place("ident", [P, P])
        ones = place("ones", [P, P])
        mask = place("mask", [P, 3 * P])
        g1 = place("g1", [P, 112])
        g2 = place("g2", [P, 120])
        tab_at = top[0]
        rot = place("rot", [P, 4, T])
        rstd4 = place("rstd4", [P, 4, T], at=tab_at)
        dtab = place("dtab", [P, RH, NP])
        tail = place("tail", [P, 2 * RH])
        cols = place("cols", [P, 64])
        dcol = cols[:, 0:16]
        norm_at = top[0]
        sq = place("sq", [P, 2, T])
        ms = place("ms", [P, T])
        rstd1 = place("rstd1", [P, 1, T])
        xt = place("xt", [P, 3, T])
        gate_at = top[0]
        sg = place("sg", [P, 2, T])
        ht = place("ht", [P, 2, T])
        acc = place("acc", [P, 2, T], at=gate_at)
        REG = top[0]

        psum = ctx.enter_context(nc.psum_tensor("psum", [P, 8, 512], F32))
        SSB = 4

        landed = [sem_of(f"landed{i}") for i in range(SLOTS)]
        hi_done = sem_of("hi_done")
        lo_done = sem_of("lo_done")
        chunk_done = sem_of("chunk_done")
        bank_free = sem_of("bank_free")
        seeded = sem_of("seeded")
        h_hi = sem_of("h_hi")
        gate_ready = sem_of("gate_ready")
        h_ready = sem_of("h_ready")
        sq_ready = sem_of("sq_ready")
        ss_done = sem_of("ss_done")
        ms_done = sem_of("ms_done")
        sd_done = sem_of("sd_done")
        rstd_done = sem_of("rstd_done")
        xt_done = sem_of("xt_done")
        xh_done = sem_of("xh_done")
        xn_ready = sem_of("xn_ready")
        xs_ready = sem_of("xs_ready")
        acc_done = sem_of("acc_done")
        xss_done = sem_of("xss_done")
        xms_done = sem_of("xms_done")
        xsd_done = sem_of("xsd_done")
        xrs_done = sem_of("xrs_done")
        tp_done = sem_of("tp_done")
        tpa = sem_of("tpa")
        tpd = sem_of("tpd")
        consts = sem_of("consts")
        ones_set = sem_of("ones_set")
        stored = {"sp": sem_of("stored_sp"), "pool": sem_of("stored_pool")}
        order = {"act": sem_of("act_order"), "dve": sem_of("dve_order"), "pool": sem_of("pool_order"),
                 "lin": sem_of("linear_order")}
        count = {"act": 0, "dve": 0, "pool": 0, "lin": 0}
        stores = {"sp": 0, "pool": 0}
        tot = dict(nx=0, xq=0, xacc=0, chunk=0, use=0, ffn=0, gate=0, stores=0, sq=0, grp=0, app=0, tp=0)

        def link(eng, which, ins):
            count[which] += 1
            ins.then_inc(order[which], 1)
            eng.wait_ge(order[which], count[which])

        def store(eng, which, out, src):
            stores[which] += 16
            eng.dma_start(out, src).then_inc(stored[which], 16)

        stages = []

        class Stage:
            def sp(S, e): pass
            def pe(S, e): pass
            def act(S, e): pass
            def dve(S, e): pass
            def pool(S, e): pass

        def walk(eng, n, fn, last=0, first=0):
            g = (n - last - first) // 4
            for l in range(first):
                fn(0, l)
            if g >= 2:
                with eng.Fori(0, g) as i:
                    for r in range(4):
                        fn(i, first + r)
            else:
                g = 0
            for l in range(first + 4 * g, n - last):
                fn(0, l)

        def behind(make):
            n = len(stages)
            make()
            sub = stages[n:]
            del stages[n:]
            return sub

        linears = []
        pending = []

        class Linear(Stage):

            def __init__(S, W, n, kt, tiles, parts, rhs, ready=None, act=None, dve=None, cpu=1, cols=T, turned=False, per=0, kwise=None, pool=None, hooks=None, early=False):
                S.W, S.n, S.kt, S.tiles, S.parts, S.rhs = W, n, kt, tiles, parts, rhs
                S.ready, S.eact, S.edve, S.cpu, S.cols, S.turned, S.per = ready, act, dve, cpu, cols, turned, per
                S.c0, S.use0 = tot["chunk"], tot["use"]
                tot["chunk"] += n
                tot["use"] += n // cpu
                S.early = early
                S.kwise, S.epool, S.hooks = kwise, pool, hooks or {}
                S.next = None
                if linears:
                    linears[-1].next = S
                linears.append(S)
                stages.append(S)

            def uses_end(S):
                return S.use0 + S.n // S.cpu

            def sp(S, e):
                def load(i, r):
                    slot = (S.c0 + r) % SLOTS
                    e.wait_ge(lo_done, i * 4 + (S.c0 + r + 1))
                    for dst, src in S.parts(raw[:, slot, :], i, r):
                        e.dma_start(dst, src).then_inc(landed[slot], 16)
                walk(e, S.n, load)

            def split_hi(S, e, i, r):
                c = S.c0 + r
                e.wait_ge(landed[c % SLOTS], i * 32 + 32 * (c // SLOTS + 1))
                if r > 0 or S.c0 > 0:
                    e.wait_ge(chunk_done, i * 4 + c)
                m = S.kt * S.tiles * P
                nc.scalar.activation(whi[:, c % 2, 0:m], raw[:, c % SLOTS, 0:m], ACT.Copy).then_inc(hi_done, 1)

            def split_lo(S, e, i, r):
                c = S.c0 + r
                m = S.kt * S.tiles * P
                e.wait_ge(hi_done, i * 4 + (c + 1))
                nc.vector.tensor_tensor(wlo[:, c % 2, 0:m], raw[:, c % SLOTS, 0:m], whi[:, c % 2, 0:m].bitcast(F32),
                                        ALU.subtract).then_inc(lo_done, 1)

            def pe(S, e):
                if S.ready:
                    S.ready(e)
                def mul(i, r):
                    c, half, par = S.c0 + r, r % S.cpu, (S.use0 + r // S.cpu) % 2
                    e.wait_ge(lo_done, i * 4 + (c + 1 + SLOTS))
                    if half == 0:
                        e.wait_ge(bank_free, i * (4 // S.cpu) + (S.use0 + r // S.cpu + 1))
                    wh = whi[:, c % 2, 0:S.kt * S.tiles * P].rearrange("p (k n) -> p k n", k=S.kt)
                    wl = wlo[:, c % 2, 0:S.kt * S.tiles * P].rearrange("p (k n) -> p k n", k=S.kt)
                    hi, lo = S.rhs[half] if isinstance(S.rhs, list) else S.rhs
                    if S.kwise is not None and r == 0 and isinstance(i, int):
                        for k in range(S.kt):
                            e.wait_ge(xn_ready, S.kwise + k + 1)
                            for t in range(S.tiles):
                                out = psum[:, 2 * par + t, 0:S.cols]
                                a, b = wh[:, k, t * P:(t + 1) * P], wl[:, k, t * P:(t + 1) * P]
                                e.matmul(out, a, hi[:, k, 0:S.cols], start=k == 0, stop=False)
                                e.matmul(out, a, lo[:, k, 0:S.cols], start=False, stop=False)
                                m = e.matmul(out, b, hi[:, k, 0:S.cols], start=False, stop=k == S.kt - 1)
                        m.then_inc(chunk_done, 1)
                        S.hook("pe", e, i, r)
                        return
                    for t in range(S.tiles):
                        out = psum[:, 2 * par + t, 0:S.cols]
                        for k in range(S.kt):
                            kk = k if isinstance(S.rhs, list) else half * S.kt + k
                            first, final = half == 0 and k == 0, half == S.cpu - 1 and k == S.kt - 1
                            if S.turned:
                                ah, al = hi[:, kk, t * P:(t + 1) * P], lo[:, kk, t * P:(t + 1) * P]
                                e.matmul(out, ah, wh[:, k, :], start=first, stop=False)
                                e.matmul(out, ah, wl[:, k, :], start=False, stop=False)
                                m = e.matmul(out, al, wh[:, k, :], start=False, stop=final)
                            else:
                                a, b = wh[:, k, t * P:(t + 1) * P], wl[:, k, t * P:(t + 1) * P]
                                e.matmul(out, a, hi[:, kk, 0:S.cols], start=first, stop=False)
                                e.matmul(out, a, lo[:, kk, 0:S.cols], start=False, stop=False)
                                m = e.matmul(out, b, hi[:, kk, 0:S.cols], start=False, stop=final)
                    m.then_inc(chunk_done, 1)
                    S.hook("pe", e, i, r)
                walk(e, S.n, mul, first=max([0 if S.kwise is None else 1] + [l + 1 for l in S.hooks]))

            def evict(S, e, fn, which, i, r):
                if fn is None or r % S.cpu != S.cpu - 1:
                    return
                e.wait_ge(chunk_done, i * 4 + (S.c0 + r + 2))
                u = r // S.cpu
                fn(e, i * (4 // S.cpu) + u, (S.use0 + u) % 2, i * (4 // S.cpu) + (S.use0 + u))

            def both(S, e, split, fn, which):
                if S is linears[0]:
                    split(S, e, 0, 0)

                def step(i, r):
                    split(S, e, i, r + 1)
                    if S.early:
                        S.hook(which, e, i, r)
                    S.evict(e, fn, which, i, r)
                    if not S.early:
                        S.hook(which, e, i, r)
                walk(e, S.n, step, last=1, first=min(S.n - 1, max([0] + [l + 1 for l in S.hooks])))
                if S.next:
                    split(S.next, e, 0, 0)
                if S.early:
                    S.hook(which, e, 0, S.n - 1)
                S.evict(e, fn, which, 0, S.n - 1)
                if not S.early:
                    S.hook(which, e, 0, S.n - 1)

            def hook(S, which, e, i, l):
                if isinstance(i, int):
                    for stage in S.hooks.get(l, ()):
                        dict(pe=stage.pe, act=stage.act, dve=stage.dve, pool=stage.pool)[which](e)

            def act(S, e):
                S.both(e, Linear.split_hi, S.eact, "act")

            def pool(S, e):
                if S.epool:
                    S.epool(S, e)
                for l in range(S.n):
                    S.hook("pool", e, 0, l)

            def dve(S, e):
                S.base = count["lin"]
                S.both(e, Linear.split_lo, S.edve, "dve")
                count["lin"] = S.base + S.per * (S.n // S.cpu)

            def chain(S, e, l):
                n = [0]

                def go(ins):
                    n[0] += 1
                    assert n[0] <= S.per
                    ins.then_inc(order["lin"], 1)
                    e.wait_ge(order["lin"], l * S.per + (S.base + n[0]))
                return go

        def by_cols(W, col0, w=256, kt=KD):
            def parts(dst, i, r):
                v = dst[:, 0:kt * w].rearrange("p (k n) -> p k n", k=kt)
                src = W.rearrange("(k p) n -> p k n", p=P)
                h = kt // 2
                at = i * (4 * w) + (r * w + col0)
                for a, b in ((0, h), (h, kt)):
                    yield v[:, a:b, :], src[:, a:b, bass.ds(at, w)]
            return parts

        def two_cols(W, col0, col1):
            def parts(dst, i, r):
                v = dst[:, 0:KD * 256].rearrange("p (k two n) -> p k two n", k=KD, two=2)
                src = W.rearrange("(k p) n -> p k n", p=P)
                for q, c in ((0, col0), (1, col1)):
                    yield v[:, :, q, :], src[:, :, bass.ds(i * 512 + (r * P + c), P)]
            return parts

        def by_rows(W, kt):
            def parts(dst, i, r):
                v = dst[:, 0:kt * P].rearrange("p (k n) -> p k n", k=kt)
                src = W[(r % 2) * kt * P:(r % 2 + 1) * kt * P, :].rearrange("(k p) n -> p k n", p=P)
                h = kt // 2
                for a, b in ((0, h), (h, kt)):
                    yield v[:, a:b, :], src[:, a:b, bass.ds(i * 256 + (r // 2) * P, P)]
            return parts

        def residual(W, n, kt, tiles, parts, rhs, scale, ready=None, cpu=1):
            q0, a0, u0 = tot["xq"], tot["xacc"], tot["use"]
            tot["xq"] += KD // tiles
            tot["xacc"] += KD // tiles + 1
            nx = tot["nx"]
            tot["nx"] += 1

            def dve(e, l, par, use):
                ps = psum[:, 2 * par:2 * par + tiles, 0:T]
                xs = x[:, bass.ds(l * tiles, tiles), :]
                e.scalar_tensor_tensor(out=xs, in0=ps, scalar=scale, in1=xs, op0=ALU.mult, op1=ALU.add).then_inc(bank_free, 1)

            def pool(S, e):
                e.wait_ge(bank_free, u0 + 2)
                e.memset(acc[:, :, :], 0.0).then_inc(acc_done, 1)

                def add(i, r):
                    if r % cpu != cpu - 1:
                        return
                    u = r // cpu
                    l = i * (4 // cpu) + u
                    par = (S.use0 + u) % 2
                    at = slice(0, 2) if tiles == 2 else slice(par, par + 1)
                    e.wait_ge(bank_free, i * (4 // cpu) + (S.use0 + u + 3))
                    e.wait_ge(acc_done, l + (a0 + 1))
                    xs = x[:, bass.ds(l * tiles, tiles), :]
                    e.tensor_tensor(sq[:, at, :], xs, xs, ALU.mult).then_inc(xs_ready, 1)
                    e.wait_ge(xs_ready, l + (q0 + 1))
                    e.tensor_tensor(acc[:, at, :], acc[:, at, :], sq[:, at, :], ALU.add).then_inc(acc_done, 1)
                walk(e, S.n, add)
            return Linear(W, n, kt, tiles, parts, rhs, ready=ready, dve=dve, cpu=cpu, pool=pool)

        def copy_out(dst, scale=1.0, n=T):
            def dve(e, l, par, use):
                e.tensor_scalar(dst[:, bass.ds(l * 2, 2), :], psum[:, 2 * par:2 * par + 2, 0:n], scale, None,
                                ALU.mult).then_inc(bank_free, 1)
            return dve

        class Stat(Stage):

            def __init__(S, src, groups, g, out, wait=None, n=T):
                S.src, S.groups, S.g, S.out, S.wait, S.n = src, groups, g, out, wait, n
                S.q0, S.g0 = tot["sq"], tot["grp"]
                tot["sq"] += groups * g
                tot["grp"] += groups
                stages.append(S)

            def act(S, e):
                for t in range(S.groups * S.g):
                    if S.wait:
                        S.wait(e, t)
                    if S.q0 + t >= 2:
                        e.wait_ge(ss_done, S.q0 + t - 1)
                    nc.scalar.activation(sq[:, t % 2, 0:S.n], S.src[:, t, 0:S.n], ACT.Square).then_inc(sq_ready, 1)
                    if t % S.g == S.g - 1:
                        G = t // S.g
                        e.wait_ge(ms_done, S.g0 + G + 1)
                        nc.scalar.activation(S.out[:, G, 0:S.n], ms[:, 0:S.n], ACT.Sqrt).then_inc(sd_done, 1)

            def pe(S, e):
                for t in range(S.groups * S.g):
                    G = S.g0 + t // S.g
                    if t % S.g == 0 and G > 0:
                        e.wait_ge(ms_done, G)
                    if t == 0:
                        e.wait_ge(ones_set, 1)
                    e.wait_ge(sq_ready, S.q0 + t + 1)
                    e.matmul(psum[:, SSB, 0:S.n], ones[:, :], sq[:, t % 2, 0:S.n], start=t % S.g == 0,
                             stop=t % S.g == S.g - 1).then_inc(ss_done, 1)

            def dve(S, e):
                for G in range(S.groups):
                    e.wait_ge(ss_done, S.q0 + (G + 1) * S.g)
                    if S.g0 + G > 0:
                        e.wait_ge(sd_done, S.g0 + G)
                    e.tensor_scalar(ms[:, 0:S.n], psum[:, SSB, 0:S.n], 1.0 / (S.g * P), EPS, ALU.mult, ALU.add).then_inc(ms_done, 1)
                    e.wait_ge(sd_done, S.g0 + G + 1)
                    e.reciprocal(S.out[:, G, 0:S.n], S.out[:, G, 0:S.n]).then_inc(rstd_done, 1)

        class Apply(Stage):

            def __init__(S, src, groups, g, rs, gcol, hi, lo, n=T, wait=None, out=None):
                S.src, S.g, S.rs, S.gcol, S.hi, S.lo, S.n, S.tiles = src, g, rs, gcol, hi, lo, n, groups * g
                S.a0, S.rgrp, S.wait, S.out = tot["app"], tot["grp"], wait, out
                if out is None:
                    tot["app"] += S.tiles
                stages.append(S)

            def scale(S, e, t):
                G = t // S.g
                if S.out is not None:
                    dst = S.out[:, t, 0:S.n]
                else:
                    if S.a0 + t >= 3:
                        e.wait_ge(xn_ready, S.a0 + t - 2)
                    dst = xt[:, (S.a0 + t) % 3, 0:S.n]
                if S.gcol is None:
                    return e.tensor_tensor(dst, S.src[:, t, 0:S.n], S.rs[:, G, 0:S.n], ALU.mult)
                return e.scalar_tensor_tensor(out=dst, in0=S.src[:, t, 0:S.n], scalar=g1[:, S.gcol + t:S.gcol + t + 1],
                                              in1=S.rs[:, G, 0:S.n], op0=ALU.mult, op1=ALU.mult)

            def sub(S, e, t):
                a = S.a0 + t
                e.wait_ge(xh_done, a + 1)
                e.tensor_tensor(S.lo[:, t, 0:S.n], xt[:, a % 3, 0:S.n], S.hi[:, t, 0:S.n].bitcast(F32),
                                ALU.subtract).then_inc(xn_ready, 1)

            def dve(S, e):
                if S.wait:
                    S.wait(e)
                e.wait_ge(rstd_done, S.rgrp)
                for t in range(S.tiles):
                    ins = S.scale(e, t)
                    if S.out is not None:
                        link(e, "dve", ins)
                        continue
                    ins.then_inc(xt_done, 1)
                    if t >= 1:
                        S.sub(e, t - 1)
                if S.out is None:
                    S.sub(e, S.tiles - 1)

            def act(S, e):
                if S.out is not None:
                    return
                for t in range(S.tiles):
                    a = S.a0 + t
                    e.wait_ge(xt_done, a + 1)
                    nc.scalar.activation(S.hi[:, t, 0:S.n], xt[:, a % 3, 0:S.n], ACT.Copy).then_inc(xh_done, 1)

        def xn_wait():
            target = tot["app"]
            return lambda e: e.wait_ge(xn_ready, target)

        class XStat(Stage):

            def __init__(S):
                S.n, S.acc = tot["nx"], tot["xacc"]
                stages.append(S)

            def pe(S, e):
                e.wait_ge(acc_done, S.acc)
                e.matmul(psum[:, 5, 0:T], ones[:, :], acc[:, 0, :], start=True, stop=False)
                e.matmul(psum[:, 5, 0:T], ones[:, :], acc[:, 1, :], start=False, stop=True).then_inc(xss_done, 1)

            def dve(S, e):
                e.wait_ge(xss_done, S.n)
                e.tensor_scalar(rstd1[:, 0, :], psum[:, 5, 0:T], 1.0 / D, EPS, ALU.mult, ALU.add).then_inc(xms_done, 1)
                e.wait_ge(xsd_done, S.n)
                e.reciprocal(rstd1[:, 0, :], rstd1[:, 0, :]).then_inc(xrs_done, 1)
                e.wait_ge(xrs_done, S.n)

            def act(S, e):
                e.wait_ge(xms_done, S.n)
                nc.scalar.activation(rstd1[:, 0, :], rstd1[:, 0, :], ACT.Sqrt).then_inc(xsd_done, 1)

        def norm_x(gcol, hi=xnh, lo=xnl, out=None):
            XStat()
            Apply(x, 1, KD, rstd1, gcol, hi, lo, out=out)

        def after_norm(W, n, parts, **kw):
            return Linear(W, n, KD, 2, parts, (xnh, xnl), kwise=tot["app"] - KD, **kw)

        class Turn(Stage):

            def __init__(S, items, ready=None, act_ready=None, dve_ready=None):
                S.items, S.ready, S.ar, S.dr = items, ready, act_ready, dve_ready
                S.n0 = tot["tp"]
                tot["tp"] += len(items)
                stages.append(S)

            def pe(S, e):
                e.wait_ge(consts, CONSTS)
                if S.ready:
                    S.ready(e)
                for j, (pieces, _) in enumerate(S.items):
                    n = S.n0 + j
                    if n >= 2:
                        e.wait_ge(tpd if n % 2 else tpa, n // 2)
                    for src, rows, cs, col in pieces:
                        m = e.transpose(psum[0:cs, 6 + n % 2, col:col + rows], src, ident[0:rows, 0:rows])
                    m.then_inc(tp_done, 1)

            def run(S, e, par):
                if (S.ar, S.dr)[par]:
                    (S.ar, S.dr)[par](e)
                for j, (_, evict) in enumerate(S.items):
                    n = S.n0 + j
                    if n % 2 == par:
                        e.wait_ge(tp_done, n + 1)
                        evict(e, psum[:, 6 + par, :], par).then_inc(tpd if par else tpa, 1)

            def act(S, e): S.run(e, 0)
            def dve(S, e): S.run(e, 1)

        def mv(e, par, out, src, scale=None):
            if par == 0:
                return nc.scalar.activation(out, src, ACT.Copy, **({} if scale is None else dict(scale=scale)))
            if scale is None:
                return e.tensor_copy(out, src)
            return e.tensor_scalar(out, src, scale, None, ALU.mult)

        def turned():
            n = tot["tp"]
            def w(e):
                e.wait_ge(tpa, (n + 1) // 2)
                if n // 2:
                    e.wait_ge(tpd, n // 2)
            return w

        CONSTS = 16 * 5
        xtok = place("xtok", [P, 2, D], at=REG)
        xstok = place("xstok", [NS, D], at=REG + 8192)
        p1 = place("p1", [112, P], at=REG + 12288)
        p2 = place("p2", [120, P], at=REG + 12800)
        x_in = sem_of("x_in")
        p_in = sem_of("p_in")

        class Init(Stage):
            def act(S, e):
                e.dma_start(xtok[:, :, :], A["x_prompt"].rearrange("o (b p) d -> p (o b) d", p=P)).then_inc(x_in, 16)
                e.dma_start(xstok[:, :], A["x_sample"].rearrange("b o d -> (b o) d")).then_inc(x_in, 16)

            def pool(S, e):
                e.memset(cols[:, 61:62], 1.0).then_inc(lo_done, SLOTS)
                e.memset(cols[:, 62:63], 1.0).then_inc(chunk_done, 1)
                e.memset(cols[:, 63:64], 1.0).then_inc(bank_free, 2)
                e.memset(cols[:, 60:61], 1.0).then_inc(h_ready, 2)
                e.memset(ones[:, :], 1.0).then_inc(ones_set, 1)
                e.dma_start(ident[:, :], A["c_ident"]).then_inc(consts, 16)
                row = 0
                for name in ("norm_ffn1", "norm_mix", "norm_xattn", "norm_mem", "norm_ffn2"):
                    e.dma_start(p1[row:row + 16, :], A[name].rearrange("l (t p) -> (l t) p", p=P)).then_inc(p_in, 16)
                    row += 16
                e.dma_start(p1[80:88, :], A["norm_final"].rearrange("(t p) -> t p", p=P)).then_inc(p_in, 16)
                e.dma_start(p1[88:104, :], A["ssd_norm"].rearrange("l (t p) -> (l t) p", p=P)).then_inc(p_in, 16)
                e.dma_start(p1[104:112, :], A["mlstm_norm"].rearrange("l (t p) -> (l t) p", p=P)).then_inc(p_in, 16)
                e.dma_start(p2[0:96, :], A["ssd_conv_w"].rearrange("l j (t p) -> (l j t) p", p=P)).then_inc(p_in, 16)
                e.dma_start(p2[96:120, :], A["ssd_conv_b"].rearrange("l (t p) -> (l t) p", p=P)).then_inc(p_in, 16)
                e.dma_start(mask[:, :], A["c_mask"]).then_inc(consts, 16)
                e.dma_start(rot[:, :, :], A["c_rot"]).then_inc(consts, 16)
                e.dma_start(dtab[:, :, :], A["c_dtab"]).then_inc(consts, 16)
                e.dma_start(tail[:, :], A["c_tail"]).then_inc(consts, 16)
        stages.append(Init())

        def x_item(k0):
            pieces = []
            for q in range(4):
                k = k0 + q // 2
                pieces.append((xtok[:, q % 2, k * P:(k + 1) * P], P, P, q * P))
            return pieces, lambda e, bank, par: mv(e, par, x[:, k0:k0 + 2, 0:NP], bank.rearrange("p (k n) -> p k n", k=2))
        items = [x_item(k) for k in range(0, KD, 2)]
        items.append(([(xstok[:, k * P:(k + 1) * P], NS, P, k * NS) for k in range(KD)],
                      lambda e, bank, par: mv(e, par, x[:, :, NP:T], bank[:, 0:KD * NS].rearrange("p (k n) -> p k n", k=KD))))
        items.append(([(p1[:, :], 112, P, 0), (p2[:, :], 120, P, 128)],
                      lambda e, bank, par: (link(e, "dve", e.tensor_copy(g1[:, :], bank[:, 0:112])),
                                            e.tensor_copy(g2[:, :], bank[:, 128:248]))[1]))
        Turn(items, ready=lambda e: (e.wait_ge(x_in, 32), e.wait_ge(p_in, 160)))
        x_ready = turned()

        H_at = REG
        Hh = place("Hh", [P, KF, T], F32R, at=H_at)
        Hl = place("Hl", [P, KF, T], F32R, at=H_at + KF * T * 4)

        def ffn(layer, w_in, w_out):
            f0, q0 = tot["ffn"], tot["gate"]
            tot["ffn"] += KF
            tot["gate"] += KF

            def act(e, l, par, use):
                e.wait_ge(bank_free, use + 1)
                nc.scalar.activation(sg[:, par, :], psum[:, 2 * par, 0:T], ACT.Silu).then_inc(gate_ready, 1)

            def dve(e, l, par, use):
                e.wait_ge(gate_ready, l + (q0 + 1))
                e.wait_ge(h_ready, l + (f0 + 1))
                e.tensor_tensor(ht[:, par, :], sg[:, par, :], psum[:, 2 * par + 1, 0:T], ALU.mult).then_inc(bank_free, 1)
                e.wait_ge(bank_free, use + 3)
                hh, hl = Hh[:, bass.ds(l, 1), :], Hl[:, bass.ds(l, 1), :]
                e.tensor_copy(hh, ht[:, par:par + 1, :]).then_inc(h_hi, 1)
                e.wait_ge(h_hi, l + (f0 + 1))
                e.tensor_tensor(hl, ht[:, par:par + 1, :], hh.bitcast(F32), ALU.subtract).then_inc(h_ready, 1)
            kept = pending[:]
            pending.clear()

            class Wait(Stage):
                def dve(S, e):
                    for q, n in kept:
                        e.wait_ge(q, n)
            stages.append(Wait())
            after_norm(w_in, KF, two_cols(w_in, 0, FF), act=act, dve=dve)
            residual(w_out, 2 * KD, KF // 2, 1, by_rows(w_out, KF // 2), (Hh, Hl), 0.5,
                     ready=lambda e: e.wait_ge(h_ready, f0 + KF + 2), cpu=2)

        G_FFN1, G_MIX, G_X, G_MEM, G_FFN2, G_FIN, G_SSD, G_M = 0, 16, 32, 48, 64, 80, 88, 104


        def gated(dst, func):
            q0 = tot["gate"]

            def start(n):
                tot["gate"] += n

            def act(e, l, par, use):
                e.wait_ge(bank_free, use + 1)
                nc.scalar.activation((sg, ht)[par][:, :, :], psum[:, 2 * par:2 * par + 2, 0:T], func).then_inc(gate_ready, 1)

            def dve(e, l, par, use):
                e.wait_ge(gate_ready, l + (q0 + 1))
                d = dst[:, bass.ds(l * 2, 2), :]
                e.tensor_tensor(d, d, (sg, ht)[par][:, :, :], ALU.mult).then_inc(bank_free, 1)
            start(dst.shape[1] // 2)
            return act, dve

        def evicted():
            n = tot["use"] + 2
            return lambda e: e.wait_ge(bank_free, n)

        def all_of(*ws):
            return lambda e: [w(e) for w in ws] and None

        def at_least(s, n):
            return lambda e: e.wait_ge(s, n)

        s_in = [sem_of(f"s_in{i}") for i in range(6)]
        s_out = [sem_of(f"s_out{i}") for i in range(6)]
        ret_moves = [16 * len(range(i, NS * RH, 6)) for i in range(6)]

        def mixer_ab():
            W = A["w_in_ab"][0]
            R0, R1 = REG, REG + CT * T * 4
            R2 = R1 + 32 * T * 4
            xbc = place("xbc", [P, CT, T], at=R0)
            qf = place("qf", [P, 8, T], at=R1)
            kf = place("kf", [P, 8, T], at=R1 + 8 * T * 4)
            vf = place("vf", [P, 16, T], at=R1 + 16 * T * 4)
            hist = place("hist", [P, CT, 24], at=R2)
            crow = place("crow", [24, CONV_CH], at=R2 + 4096)
            ctok = place("ctok", [11, CONV_CH], at=R2 + 20480)
            utail = place("utail", [P, CT, 11], at=R2 + 32768)
            x_tm = place("x_tm", [P, 2, SSD_IN], at=R2)
            B_tm = place("B_tm", [P, 2, 512], at=R2 + 16384)
            CBm = place("CBm", [P, 4, 384], at=R2 + 20480)
            eb = place("eb", [P, 2, 384], at=R2 + 26624)
            at_ = place("at", [P, 4, 384], at=R2 + 29696)
            XW = 8
            xw = place("xw", [P, XW, 2, P], at=R2 + 26624)
            hst = place("hst", [P, 4, P], at=R2 + 34816)
            scT = place("scT", [P, 7, 32], at=R2 + 36864)
            dtE = place("dtE", [P, 16, 16], at=R2 + 36864 + 896)
            rw = place("rw", [32, 7, T], at=norm_at)
            region_free = evicted()
            conv_in = sem_of("conv_in")
            small_in = sem_of("small_in")
            d_in = sem_of("d_in")

            class Load(Stage):
                def pool(S, e):
                    region_free(e)
                    e.dma_start(crow[:, :], A["state_conv"].rearrange("l b j c -> (l b j) c")).then_inc(conv_in, 16)
                    with nc.allow_non_contiguous_dma(reason="32 numbers, one on each partition"):
                        e.dma_start(cols[0:32, 40:41], A["ssd_dt_bias"].rearrange("l h -> h l")).then_inc(small_in, 16)
                        e.dma_start(cols[0:32, 42:43], A["ssd_a_log"].rearrange("l h -> h l")).then_inc(small_in, 16)
                        for q in range(2):
                            src = A["ssd_d"].rearrange("l (j two) -> (l two) j", two=2)[q:q + 1, :].to_broadcast([64, 16])
                            e.dma_start(cols[64 * q:64 * q + 64, 0:16], src).then_inc(d_in, 16)
                    store(e, "pool", O[5][0, :, 0:2, :], A["state_conv"][0, :, 1:3, :])
            stages.append(Load())
            hist_turn = behind(lambda: Turn([([(crow[:, t * P:(t + 1) * P], 24, P, (t - t0) * 24) for t in range(t0, t0 + 12)],
                   lambda e, bank, par, t0=t0: mv(e, par, hist[:, t0:t0 + 12, :], bank[:, 0:288].rearrange("p (t q) -> p t q", t=12)))
                  for t0 in (0, 12)], ready=at_least(conv_in, 16)))
            hist_ready = turned()

            w_conv = lambda j, l, q: g2[:, bass.ds(l * 2 + (j * CT + q), 1)]
            conv_own = sem_of("conv_own")
            conv_hist = sem_of("conv_hist")

            def conv_act(e, l, par, use):
                ps = psum[:, 2 * par:2 * par + 2, :]
                nc.scalar.activation(utail[:, bass.ds(l * 2, 2), :], ps[:, :, T - 11:T], ACT.Copy)
                for q in range(2):
                    ins = nc.scalar.activation(xbc[:, bass.ds(l * 2 + q, 1), :], ps[:, q:q + 1, 0:T], ACT.Identity,
                                               scale=w_conv(3, l, q), bias=w_conv(4, l, q))
                ins.then_inc(conv_own, 1)

            def conv_dve(e, l, par, use):
                e.wait_ge(conv_own, l + 1)
                n = 0
                for j in (2, 1, 0):
                    for q in range(2):
                        d = 3 - j
                        if n >= 2:
                            e.wait_ge(order["lin"], l * 5 + (L_xbc.base + n - 1))
                        a = xbc[:, bass.ds(l * 2 + q, 1), d:NP]
                        n += 1
                        e.scalar_tensor_tensor(out=a, in0=psum[:, 2 * par + q:2 * par + q + 1, 0:NP - d], scalar=w_conv(j, l, q),
                                               in1=a, op0=ALU.mult, op1=ALU.add).then_inc(order["lin"] if n < 6 else bank_free, 1)
            L_xbc = after_norm(W, 12, by_cols(W, 2048), hooks={0: hist_turn}, act=conv_act, dve=conv_dve, per=5)
            xbc_out = evicted()
            dt_raw = sem_of("dt_raw")

            def dt_dve(e, l, par, use):
                e.wait_ge(small_in, 32)
                e.tensor_scalar(rw[:, 0, :], psum[0:32, 2 * par, 0:T], cols[0:32, 40:41], None, ALU.add).then_inc(bank_free, 1)

            def one_tile(W, c0):
                def parts(dst, i, r):
                    v = dst[:, 0:KD * P].rearrange("p (k n) -> p k n", k=KD)
                    src = W.rearrange("(k p) n -> p k n", p=P)
                    for a, b in ((0, 4), (4, 8)):
                        yield v[:, a:b, :], src[:, a:b, c0:c0 + P]
                return parts
            Linear(W, 1, KD, 1, one_tile(W, 5120), (xnh, xnl), dve=dt_dve)
            dt_out = evicted()
            jh = place("jh", [P, CT, NS], at=norm_at + 7 * T * 4)

            class ConvEnd(Stage):
                def dve(S, e):
                    xbc_out(e)
                    hist_ready(e)
                    v = xbc[:, :, NP:T]
                    for j in range(3):
                        w = g2[:, j * CT:(j + 1) * CT].unsqueeze(2).to_broadcast([P, CT, NS])
                        link(e, "dve", e.tensor_tensor(jh[:, :, :], hist[:, :, j:24:3], w, ALU.mult))
                        e.tensor_tensor(v, v, jh[:, :, :], ALU.add).then_inc(conv_hist, 1)
                        e.wait_ge(conv_hist, j + 1)

                def act(S, e):
                    e.wait_ge(conv_hist, 3)
                    for t in range(0, CT, 4):
                        v = xbc[:, t:t + 4, :]
                        nc.scalar.activation(v, v, ACT.Silu).then_inc(xbc_ready, 1)
            xbc_ready = sem_of("xbc_ready")
            ch_out = evicted()
            ut_turn = behind(lambda: Turn([([(utail[:, t, :], P, 11, (t - t0) * P) for t in range(t0, t0 + 4)],
                   lambda e, bank, par, t0=t0: mv(e, par, ctok[:, t0 * P:(t0 + 4) * P], bank[0:11, :])) for t0 in range(0, CT, 4)],
                 ready=ch_out))
            ct_ready = turned()
            rows_done = sem_of("rows_done")
            abs_done = sem_of("abs_done")
            ln_done = sem_of("ln_done")
            exp_a = sem_of("exp_a")
            w_done = sem_of("w_done")
            ncs_done = sem_of("ncs_done")

            class Rows(Stage):
                def pool(S, e):
                    ct_ready(e)
                    store(e, "pool", O[4].rearrange("l o j c -> (l o j) c"), ctok[0:3, :])
                    store(e, "pool", O[5][0, :, 2, :], ctok[3:11, :])

                def dve(S, e):
                    dt_out(e)
                    e.scalar_tensor_tensor(out=rw[:, 1, :], in0=rw[:, 0, :], scalar=-1.0, in1=rw[:, 0, :], op0=ALU.mult,
                                           op1=ALU.max).then_inc(abs_done, 1)
                    e.wait_ge(ln_done, 1)
                    link(e, "dve", e.scalar_tensor_tensor(out=rw[:, 2, :], in0=rw[:, 0, :], scalar=0.0, in1=rw[:, 1, :],
                                                          op0=ALU.max, op1=ALU.add))
                    e.wait_ge(exp_a, 1)
                    link(e, "dve", e.tensor_scalar(rw[:, 3, :], rw[:, 2, :], cols[0:32, 41:42], None, ALU.mult))
                    e.wait_ge(ones_set, 1)
                    for b in range(2):
                        s = slice(b * P, (b + 1) * P)
                        link(e, "dve", e.tensor_tensor_scan(rw[:, 4, s], ones[0:32, :], rw[:, 3, s], 0.0, ALU.mult, ALU.add))
                    c = lambda j: cols[0:32, j:j + 1]
                    link(e, "dve", e.tensor_scalar(rw[:, 5, 0:P], rw[:, 4, 0:P], rw[:, 4, P - 1:P], None, ALU.subtract))
                    link(e, "dve", e.tensor_tensor(c(43), rw[:, 4, P - 1:P], rw[:, 4, NP - 1:NP], ALU.add))
                    link(e, "dve", e.tensor_scalar(rw[:, 6, 0:P], rw[:, 4, 0:P], c(43), None, ALU.subtract))
                    e.tensor_scalar(rw[:, 6, P:NP], rw[:, 4, P:NP], rw[:, 4, NP - 1:NP], None, ALU.subtract).then_inc(ncs_done, 1)
                    e.wait_ge(w_done, 2)
                    link(e, "dve", e.tensor_tensor(rw[:, 6, 0:NP], rw[:, 6, 0:NP], rw[:, 2, 0:NP], ALU.mult))
                    e.tensor_copy(rw[:, 5, P:P + NS], rw[:, 2, NP:T]).then_inc(rows_done, 1)

                def act(S, e):
                    e.wait_ge(small_in, 32)
                    nc.scalar.activation(cols[0:32, 41:42], cols[0:32, 42:43], ACT.Exp).then_inc(exp_a, 1)
                    e.wait_ge(abs_done, 1)
                    link(e, "act", nc.scalar.activation(rw[:, 1, :], rw[:, 1, :], ACT.Exp, scale=-1.0))
                    nc.scalar.activation(rw[:, 1, :], rw[:, 1, :], ACT.Ln, bias=1.0).then_inc(ln_done, 1)
                    e.wait_ge(ncs_done, 1)
                    nc.scalar.activation(rw[:, 6, 0:NP], rw[:, 6, 0:NP], ACT.Exp).then_inc(w_done, 1)
                    nc.scalar.activation(rw[:, 5, P + NS:P + 2 * NS], rw[:, 3, NP:T], ACT.Exp, scale=-1.0).then_inc(w_done, 1)

            def rotary(dst, c, get):
                def dve(e, l, par, use):
                    go = get().chain(e, l)
                    p0, p1_ = psum[:, 2 * par, 0:T], psum[:, 2 * par + 1, 0:T]
                    go(e.tensor_tensor(sg[:, 0, :], p0, rot[:, c, :], ALU.mult))
                    go(e.tensor_tensor(ht[:, 0, :], p1_, rot[:, c + 1, :], ALU.mult))
                    go(e.tensor_tensor(dst[:, bass.ds(l * 2, 1), :], sg[:, 0:1, :], ht[:, 0:1, :], ALU.subtract))
                    go(e.tensor_tensor(sg[:, 1, :], p0, rot[:, c + 1, :], ALU.mult))
                    e.tensor_tensor(ht[:, 1, :], p1_, rot[:, c, :], ALU.mult).then_inc(bank_free, 1)
                    e.wait_ge(bank_free, use + 3)
                    go(e.tensor_tensor(dst[:, bass.ds(l * 2 + 1, 1), :], sg[:, 1:2, :], ht[:, 1:2, :], ALU.add))
                return dve
            items = []
            for t in range(16):
                if t % 2 == 0:
                    items.append(([(xbc[:, t + q // 2, (q % 2) * P:(q % 2 + 1) * P], P, P, (q % 2) * 256 + (q // 2) * P) for q in range(4)],
                                  lambda e, bank, par, t=t: mv(e, par, x_tm[:, :, t * P:(t + 2) * P], bank.rearrange("p (b n) -> p b n", b=2))))
            for t in (16, 18):
                items.append(([(xbc[:, t + q // 2, (q % 2) * P:(q % 2 + 1) * P], P, P, (q % 2) * 256 + (q // 2) * P) for q in range(4)],
                              lambda e, bank, par, t=t: mv(e, par, B_tm[:, :, (t - 16) * P:(t - 14) * P], bank.rearrange("p (b n) -> p b n", b=2))))
            srcs = [rw[:, 4, 0:P], rw[:, 4, P:NP], rw[:, 5, 0:P], rw[:, 2, 0:P], rw[:, 2, P:NP], rw[:, 6, 0:P], rw[:, 6, P:NP]]
            items.append(([(v, 32, P, j * 32) for j, v in enumerate(srcs)],
                          lambda e, bank, par: mv(e, par, scT[:, :, :], bank[:, 0:224].rearrange("p (j h) -> p j h", j=7))))
            tm_turn = behind(lambda: Turn(items, ready=all_of(at_least(rows_done, 1), at_least(xbc_ready, 6))))
            tm_ready = turned()
            cb_done = sem_of("cb_done")
            cb_ready = sem_of("cb_ready")
            bc_done = sem_of("bc_done")
            bc_free = sem_of("bc_free")
            e_diag = sem_of("e_diag")
            e_done = sem_of("e_done")
            att_ready = sem_of("att_ready")
            y_done = sem_of("y_done")
            y_out_ = sem_of("y_out")
            dte_done = sem_of("dte_done")
            dte_ready = sem_of("dte_ready")
            xw_ready = sem_of("xw_ready")
            st_done = sem_of("st_done")
            st_out = sem_of("st_out")

            hst_stored = sem_of("hst_stored")
            tot["stores"] += 48

            class SSDStart(Stage):

                def pe(S, e):
                    tm_ready(e)
                    for g in range(4):
                        if g >= 2:
                            e.wait_ge(cb_ready, g - 1)
                        B, C = xbc[:, 16 + g, :], xbc[:, 20 + g, :]
                        e.matmul(psum[:, 4 + g % 2, 0:NP], B[:, 0:P], C[:, 0:NP], start=True, stop=True)
                        e.matmul(psum[:, 4 + g % 2, NP:NP + P], B[:, P:NP], C[:, P:NP], start=True, stop=True).then_inc(cb_done, 1)
                    for h in range(32):
                        q, j = h % 2, h // 2
                        m = e.matmul(psum[64 * q:64 * q + 64, 7, j * 16:(j + 1) * 16], ident[0:32, h:h + 1].to_broadcast([32, 64]),
                                     rw[:, 5, P:P + 2 * NS], start=True, stop=True)
                    m.then_inc(dte_done, 1)

                def dve(S, e):
                    e.wait_ge(stored["pool"], 48)
                    for g in range(4):
                        e.wait_ge(cb_done, g + 1)
                        e.tensor_tensor(CBm[:, g, :], psum[:, 4 + g % 2, 0:384], mask[:, :], ALU.mult).then_inc(cb_ready, 1)

                def act(S, e):
                    e.wait_ge(dte_done, 1)
                    nc.scalar.activation(dtE[:, :, :], psum[:, 7, 0:256].rearrange("p (j q) -> p j q", j=16), ACT.Copy).then_inc(dte_ready, 1)

            class SSDState(Stage):

                def __init__(S, j4):
                    S.j4 = j4

                def pe(S, e):
                    if S.j4 < 2:
                        e.wait_ge(cb_ready, 4)
                    else:
                        e.wait_ge(st_out, S.j4 - 1)
                    for j in range(4 * S.j4, 4 * S.j4 + 4):
                        e.wait_ge(xw_ready, j + 1)
                        o = psum[:, 4 + S.j4 % 2, (j % 4) * P:(j % 4 + 1) * P]
                        for b in range(2):
                            m = e.matmul(o, xw[:, j % XW, b, :], B_tm[:, b, S.j4 * P:(S.j4 + 1) * P], start=b == 0, stop=b == 1)
                        m.then_inc(st_done, 1)

                def act(S, e):
                    e.wait_ge(st_done, 4 * S.j4 + 4)
                    if S.j4 >= 1:
                        e.wait_ge(hst_stored, 16 * S.j4)
                    nc.scalar.activation(hst[:, :, :], psum[:, 4 + S.j4 % 2, :].rearrange("p (j n) -> p j n", j=4), ACT.Copy).then_inc(st_out, 1)
                    e.wait_ge(st_out, S.j4 + 1)
                    dst = O[6].rearrange("l o (j two) d n -> (two d) (l o j) n", two=2)
                    e.dma_start(dst[:, 4 * S.j4:4 * S.j4 + 4, :], hst[:, :, :]).then_inc(hst_stored, 16)

                def pool(S, e):
                    if S.j4 == 0:
                        tm_ready(e)
                        e.wait_ge(stored["pool"], 48)
                    for j in range(4 * S.j4, 4 * S.j4 + 4):
                        if j >= XW:
                            e.wait_ge(st_done, j - XW + 1)
                        w = scT[:, 5:7, 2 * j:2 * j + 2].unsqueeze(3).to_broadcast([P, 2, 2, 64])
                        e.tensor_tensor(xw[:, j % XW, :, :].rearrange("p b (h n) -> p b h n", h=2),
                                        x_tm[:, :, j * P:(j + 1) * P].rearrange("p b (h n) -> p b h n", h=2), w, ALU.mult).then_inc(xw_ready, 1)

            HG = 4

            def ssd_sums(e, s):
                if s == 0:
                    e.wait_ge(st_out, 4)
                else:
                    e.wait_ge(bc_free, HG * s)
                for q in range(HG):
                    h = HG * s + q
                    e.matmul(psum[:, 4 + q % 2, (q // 2) * NP:(q // 2 + 1) * NP], ident[0:32, h:h + 1].to_broadcast([32, P]),
                             rw[:, 4, 0:NP], start=True, stop=True).then_inc(bc_done, 1)

            class SSDSums(Stage):
                def pe(S, e):
                    ssd_sums(e, 0)

            class SSDHeads(Stage):

                def __init__(S, s):
                    S.s = s

                def pe(S, e):
                    if S.s + 1 < 32 // HG:
                        ssd_sums(e, S.s + 1)
                    if S.s == 0:
                        e.wait_ge(dte_ready, 1)
                    else:
                        e.wait_ge(y_out_, 2 * S.s)
                    for q in range(HG):
                        h = HG * S.s + q
                        e.wait_ge(att_ready, h + 1)
                        o = psum[64 * (q % 2):64 * (q % 2) + 64, 6 + q // 2, 0:NP]
                        e.matmul(o, x_tm[:, 0, h * 64:(h + 1) * 64], at_[:, q, 0:NP], start=True, stop=False)
                        e.matmul(o[:, P:NP], x_tm[:, 1, h * 64:(h + 1) * 64], at_[:, q, NP:NP + P], start=False,
                                 stop=True).then_inc(y_done, 1)

                def gaps(S, e, h):
                    q = h % HG
                    e.wait_ge(bc_done, HG * S.s + q % 2 + 3)
                    if h >= 2:
                        e.wait_ge(att_ready, h - 1)
                    ps = psum[:, 4 + q % 2, (q // 2) * NP:(q // 2 + 1) * NP]
                    for b in range(2):
                        ins = e.tensor_scalar(eb[:, h % 2, 2 * b * P:(2 * b + 1) * P], ps[:, b * P:(b + 1) * P],
                                              scT[:, b, h:h + 1], 0.0, ALU.subtract, ALU.max)
                    ins.then_inc(e_diag, 1)

                def dve(S, e):
                    if S.s == 0:
                        tm_ready(e)
                        e.wait_ge(cb_ready, 4)
                        e.wait_ge(hst_stored, 64)
                        e.wait_ge(st_done, 16)
                    else:
                        for j in (2 * S.s - 2, 2 * S.s - 1):
                            ssd_out_pair(e, j)
                    h0 = HG * S.s
                    S.gaps(e, h0)
                    for h in range(h0, h0 + HG):
                        if h + 1 < h0 + HG:
                            S.gaps(e, h + 1)
                        e.wait_ge(e_done, h + 1)
                        g, q = h // 8, h % HG
                        e.scalar_tensor_tensor(out=at_[:, q, 0:NP], in0=eb[:, h % 2, 0:NP], scalar=scT[:, 3, h:h + 1],
                                               in1=CBm[:, g, 0:NP], op0=ALU.mult, op1=ALU.mult)
                        e.scalar_tensor_tensor(out=at_[:, q, NP:384], in0=eb[:, h % 2, NP:384], scalar=scT[:, 4, h:h + 1],
                                               in1=CBm[:, g, NP:384], op0=ALU.mult, op1=ALU.mult).then_inc(att_ready, 1)

                def act(S, e):
                    if S.s == 0:
                        tm_ready(e)
                    for h in range(HG * S.s, HG * S.s + HG):
                        q = h % HG
                        e.wait_ge(e_diag, h + 1)
                        ps = psum[:, 4 + q % 2, (q // 2) * NP:(q // 2 + 1) * NP]
                        nc.scalar.activation(eb[:, h % 2, P:2 * P], ps[:, P:2 * P], ACT.Exp, scale=-1.0,
                                             bias=scT[:, 2, h:h + 1]).then_inc(bc_free, 1)
                        v = eb[:, h % 2, :].rearrange("p (q n) -> p q n", q=3)[:, 0:3:2, :]
                        nc.scalar.activation(v, v, ACT.Exp, scale=-1.0).then_inc(e_done, 1)

            def ssd_out_pair(e, j):
                e.wait_ge(y_done, 2 * j + 2)
                if j == 0:
                    e.wait_ge(d_in, 32)
                v = xbc[:, j, 0:NP]
                e.scalar_tensor_tensor(out=v, in0=v, scalar=dcol[:, j:j + 1], in1=psum[:, 6 + j % 2, 0:NP], op0=ALU.mult,
                                       op1=ALU.add).then_inc(y_out_, 1)

            LQ = Linear(W, 4, KD, 2, by_cols(W, 5152), (xnh, xnl), dve=rotary(qf, 0, lambda: LQ), per=5,
                        hooks={0: [ConvEnd()] + ut_turn, 1: [Rows()], 3: tm_turn})
            LK = Linear(W, 4, KD, 2, by_cols(W, 6176), (xnh, xnl), dve=rotary(kf, 2, lambda: LK), per=5,
                        hooks={0: [SSDStart()], 1: [SSDState(0)], 2: [SSDState(1), SSDState(2)], 3: [SSDState(3), SSDSums()]})
            Linear(W, 8, KD, 2, by_cols(W, 7200), (xnh, xnl), dve=copy_out(vf), early=True,
                   hooks={s: [SSDHeads(s)] for s in range(8)})
            qkv_out = evicted()

            class SSDLast(Stage):
                def dve(S, e):
                    for j in (14, 15):
                        ssd_out_pair(e, j)
            stages.append(SSDLast())
            BCs = place("BCs", [NS, 2, 512], at=norm_at + 7 * T * 4)
            bcs_items = [([(xbc[:, 16 + 4 * q + g, NP:T], P, NS, g * P) for g in range(4)],
                          lambda e, bank, par, q=q: mv(e, par, BCs[:, q, :], bank[0:NS, :])) for q in range(2)]
            Turn(bcs_items, ready=all_of(qkv_out, at_least(y_out_, 16)))
            bcs_ready = turned()

            hb = place("hb", [P, 2, 16, P], at=R2)
            jk = place("jk", [P, 16, P], at=R2 + 16384)
            xdt = place("xdt", [P, 16, NS], at=R2 + 16384 + 8192)
            ysm = place("ysm", [P, 16, NS], at=R2 + 16384 + 8192 + 512)
            hb_in = [sem_of("hb_in0"), sem_of("hb_in1")]
            hb_out = [sem_of("hb_out0"), sem_of("hb_out1")]
            dec_done = sem_of("dec_done")
            bcb_done = sem_of("bcb_done")
            h_new = sem_of("h_new")
            hy_done = sem_of("hy_done")
            ssd_out = sem_of("ssd_out")
            st_view = lambda t, b: t[0, b].rearrange("(j two) d n -> (two d) j n", two=2)

            class SSDSample(Stage):

                def pool(S, e):
                    e.wait_ge(y_done, 32)
                    for b in range(NS):
                        if b >= 2:
                            e.wait_ge(hb_out[b % 2], 16 * (b // 2))
                            e.wait_ge(hy_done, b - 1)
                        e.dma_start(hb[:, b % 2, :, :], st_view(A["state_ssm"], b)).then_inc(hb_in[b % 2], 16)

                def act(S, e):
                    e.wait_ge(dte_ready, 1)
                    for b in range(NS):
                        e.wait_ge(hb_in[b % 2], 16 * (b // 2 + 1))
                        for j in range(16):
                            v = hb[:, b % 2, j, :]
                            ins = nc.scalar.activation(v, v, ACT.Copy, scale=dtE[:, j, NS + b:NS + b + 1])
                        ins.then_inc(dec_done, 1)
                        if b >= 1:
                            S.keep(e, b - 1)
                    S.keep(e, NS - 1)

                def keep(S, e, b):
                    e.wait_ge(h_new, b + 1)
                    e.dma_start(st_view(O[7], b), hb[:, b % 2, :, :]).then_inc(hb_out[b % 2], 16)

                def pe(S, e):
                    bcs_ready(e)
                    for b in range(NS):
                        if b == 0:
                            e.wait_ge(y_out_, 16)
                            e.wait_ge(st_out, 4)
                        if b >= 2:
                            e.wait_ge(hy_done, b - 1)
                        for q in range(2):
                            m = e.matmul(psum[:, 2 * (b % 2) + q, :], ident[0:NS, b:b + 1].to_broadcast([NS, P]), BCs[:, q, :], start=True, stop=True)
                        m.then_inc(bcb_done, 1)

                def dve(S, e):
                    e.wait_ge(dte_ready, 1)
                    link(e, "dve", e.tensor_tensor(xdt[:, :, :], xbc[:, 0:16, NP:T], dtE[:, :, 0:NS], ALU.mult))
                    for b in range(NS):
                        e.wait_ge(dec_done, b + 1)
                        e.wait_ge(bcb_done, b + 1)
                        for j in range(16):
                            g = j // 4
                            v = hb[:, b % 2, j, :]
                            ins = e.scalar_tensor_tensor(out=v, in0=psum[:, 2 * (b % 2), g * P:(g + 1) * P], scalar=xdt[:, j, b:b + 1],
                                                         in1=v, op0=ALU.mult, op1=ALU.add)
                        ins.then_inc(h_new, 1)
                        e.wait_ge(h_new, b + 1)
                        if b >= 1:
                            e.wait_ge(hy_done, b)
                        for j in range(16):
                            g = j // 4
                            ins = e.tensor_tensor_reduce(jk[:, j, :], hb[:, b % 2, j, :], psum[:, 2 * (b % 2) + 1, g * P:(g + 1) * P],
                                                         1.0, 0.0, ALU.mult, ALU.add, ysm[:, j, b:b + 1])
                        ins.then_inc(hy_done, 1)
                    e.wait_ge(hy_done, NS)
                    v = xbc[:, 0:16, NP:T]
                    link(e, "dve", e.tensor_tensor(v, v, dcol[:, :].unsqueeze(2).to_broadcast([P, 16, NS]), ALU.mult))
                    e.tensor_tensor(v, v, ysm[:, :, :], ALU.add).then_inc(ssd_out, 1)
            stages.append(SSDSample())

            yh = place("yh", [P, 16, T], F32R, at=R2)
            yl = place("yl", [P, 16, T], F32R, at=R2 + 16 * T * 4)
            y = xbc[:, 0:16, :]
            az, dz = gated(y, ACT.Silu)
            Linear(W, 8, KD, 2, by_cols(W, 0), (xnh, xnl), ready=at_least(ssd_out, 1), act=az, dve=dz)
            z_out = evicted()
            Stat(xbc, 4, 4, rstd4, lambda e, t: z_out(e) if t == 0 else None)
            hb_stored = lambda e: [e.wait_ge(q, 64) for q in hb_out] and None
            Apply(xbc, 4, 4, rstd4, G_SSD, yh, yl, wait=hb_stored)
            y_split = xn_wait()

            v_tm = place("v_tm", [P, 2, 2048], at=R0)
            k_tm = place("k_tm", [P, 2, 1024], at=R0 + 16384)
            ra = place("ra", [P, 2, 384], at=R2 + 32 * T * 4)
            vs = place("vs", [NS, 2048], at=norm_at)
            rst2 = place("rst2", [P, 512], at=R2 + 32 * T * 4)
            rst = place("rst", [P, 512], at=norm_at + 8192)
            items = []
            for t in range(0, 16, 2):
                items.append(([(vf[:, t + q // 2, (q % 2) * P:(q % 2 + 1) * P], P, P, (q % 2) * 256 + (q // 2) * P) for q in range(4)],
                              lambda e, bank, par, t=t: mv(e, par, v_tm[:, :, t * P:(t + 2) * P], bank.rearrange("p (b n) -> p b n", b=2))))
            for h in range(4):
                def ev(e, bank, par, h=h):
                    for b in range(2):
                        ins = mv(e, par, k_tm[:, b, h * 256:(h + 1) * 256], bank[:, b * 256:(b + 1) * 256], scale=tail[:, 2 * h + b:2 * h + b + 1])
                    return ins
                items.append(([(kf[:, 2 * h + q // 2, (q % 2) * P:(q % 2 + 1) * P], P, P, (q % 2) * 256 + (q // 2) * P) for q in range(4)], ev))
            for t0 in range(0, 16, 4):
                items.append(([(vf[:, t, NP:T], P, NS, (t - t0) * P) for t in range(t0, t0 + 4)],
                              lambda e, bank, par, t0=t0: mv(e, par, vs[:, t0 * P:(t0 + 4) * P], bank[0:NS, :])))
            Turn(items, ready=y_split)
            vt_ready = turned()
            rs_done = sem_of("ret_scores")
            ra_ready = sem_of("ret_att")
            ro_done = sem_of("ret_out_done")
            ro_out = sem_of("ret_out_copied")
            rS_done = sem_of("ret_state_done")
            rS_out = sem_of("ret_state_copied")
            rS_stored = [sem_of("ret_state_stored0"), sem_of("ret_state_stored1")]

            class RetPrompt(Stage):

                def pe(S, e):
                    vt_ready(e)
                    for h in range(RH):
                        if h >= 2:
                            e.wait_ge(ra_ready, h - 1)
                        for b in range(2):
                            o = psum[:, 4 + h % 2, b * NP:b * NP + NP - b * P]
                            for d in range(2):
                                m = e.matmul(o, kf[:, 2 * h + d, b * P:(b + 1) * P], qf[:, 2 * h + d, b * P:NP], start=d == 0, stop=d == 1)
                        m.then_inc(rs_done, 1)
                        if h > 0:
                            S.values(e, h - 1)
                    S.values(e, RH - 1)
                    for i in range(2 * RH):
                        h, d = i // 2, i % 2
                        if i >= 2:
                            e.wait_ge(rS_out, i - 1)
                        for b in range(2):
                            m = e.matmul(psum[:, 2 + i % 2, :], k_tm[:, b, h * 256 + d * P:h * 256 + (d + 1) * P],
                                         v_tm[:, b, h * 512:(h + 1) * 512], start=b == 0, stop=b == 1)
                        m.then_inc(rS_done, 1)

                def values(S, e, h):
                    e.wait_ge(ra_ready, h + 1)
                    for q in range(4):
                        n = 2 * h + q // 2
                        if q % 2 == 0 and n >= 2:
                            e.wait_ge(ro_out, n - 1)
                        c = h * 512 + q * P
                        o = psum[:, n % 2, (q % 2) * NP:(q % 2 + 1) * NP]
                        e.matmul(o, v_tm[:, 0, c:c + P], ra[:, h % 2, 0:NP], start=True, stop=False)
                        m = e.matmul(o[:, P:NP], v_tm[:, 1, c:c + P], ra[:, h % 2, NP:384], start=False, stop=True)
                        if q % 2 == 1:
                            m.then_inc(ro_done, 1)

                def dve(S, e):
                    for h in range(RH):
                        e.wait_ge(rs_done, h + 1)
                        if h >= 2:
                            e.wait_ge(ro_done, 2 * h - 2)
                        e.tensor_tensor(ra[:, h % 2, 0:NP], psum[:, 4 + h % 2, 0:NP], dtab[:, h, :], ALU.mult)
                        e.tensor_tensor(ra[:, h % 2, NP:384], psum[:, 4 + h % 2, NP:384], dtab[:, h, 0:P], ALU.mult).then_inc(ra_ready, 1)

                def act(S, e):
                    vt_ready(e)
                    for n in range(2 * RH):
                        e.wait_ge(ro_done, n + 1)
                        nc.scalar.activation(vf[:, 2 * n:2 * n + 2, 0:NP], psum[:, n % 2, :].rearrange("p (q n) -> p q n", q=2),
                                             ACT.Copy).then_inc(ro_out, 1)
                    for i in range(2 * RH):
                        e.wait_ge(rS_done, i + 1)
                        if i >= 2:
                            e.wait_ge(rS_stored[i % 2], 16 * (i // 2))
                        buf = (rst, rst2)[i % 2]
                        nc.scalar.activation(buf[:, :], psum[:, 2 + i % 2, :], ACT.Copy).then_inc(rS_out, 1)
                        e.wait_ge(rS_out, i + 1)
                        e.dma_start(O[8][0, 0, i // 2, (i % 2) * P:(i % 2 + 1) * P, :], buf[:, :]).then_inc(rS_stored[i % 2], 16)

            stages.append(RetPrompt())

            NB_ = len(s_in)
            sb = place("sb", [P, NB_, 2, 512], at=R0)
            sb_in, sb_out = s_in, s_out
            sdec = sem_of("ret_decayed")
            vb_done = sem_of("ret_vb")
            s_new = sem_of("ret_s_new")
            s_used = sem_of("ret_s_used")
            rsm_out = sem_of("ret_sample_out")
            gam = [1.0 - 2.0 ** (-5 - h) for h in range(RH)]
            sv = lambda t, i: t[0, i // RH, i % RH].rearrange("(two p) n -> p two n", two=2)

            class RetSample(Stage):

                def pool(S, e):
                    e.wait_ge(rS_done, 2 * RH)
                    for i in range(NS * RH):
                        n = i // NB_
                        if n:
                            e.wait_ge(sb_out[i % NB_], 16 * n)
                            e.wait_ge(s_used, i - NB_ + 1)
                        e.dma_start(sb[:, i % NB_, :, :], sv(A["state_ret"], i)).then_inc(sb_in[i % NB_], 16)

                def keep(S, e, i):
                    e.wait_ge(s_new, i + 1)
                    e.dma_start(sv(O[9], i), sb[:, i % NB_, :, :]).then_inc(sb_out[i % NB_], 16)

                def act(S, e):
                    for i in range(NS * RH):
                        e.wait_ge(sb_in[i % NB_], 16 * (i // NB_ + 1))
                        v = sb[:, i % NB_, :, :]
                        nc.scalar.activation(v, v, ACT.Copy, scale=gam[i % RH]).then_inc(sdec, 1)
                        if i >= 2:
                            S.keep(e, i - 2)
                    for i in (NS * RH - 2, NS * RH - 1):
                        S.keep(e, i)

                def dve(S, e):
                    for i in range(NS * RH):
                        b, h = i // RH, i % RH
                        e.wait_ge(sdec, i + 1)
                        e.wait_ge(vb_done, i + 1)
                        for d in range(2):
                            v = sb[:, i % NB_, d, :]
                            ins = e.scalar_tensor_tensor(out=v, in0=psum[:, i % 4, :], scalar=kf[:, 2 * h + d, NP + b:NP + b + 1], in1=v,
                                                         op0=ALU.mult, op1=ALU.add)
                        ins.then_inc(s_new, 1)
                    e.wait_ge(s_used, NS * RH)
                    e.tensor_copy(vf[:, :, NP:T], psum[:, 4, 0:128].rearrange("p (t b) -> p t b", t=16)).then_inc(rsm_out, 1)

                def pe(S, e):
                    e.wait_ge(rS_out, 2 * RH)
                    e.wait_ge(ra_ready, RH)
                    e.wait_ge(ro_out, 2 * RH)

                    def bc(i):
                        if i >= 4:
                            e.wait_ge(s_new, i - 3)
                        e.matmul(psum[:, i % 4, :], ident[0:NS, i // RH:i // RH + 1].to_broadcast([NS, P]),
                                 vs[:, (i % RH) * 512:(i % RH + 1) * 512], start=True, stop=True).then_inc(vb_done, 1)
                    for i in range(3):
                        bc(i)
                    for i in range(NS * RH):
                        if i + 3 < NS * RH:
                            bc(i + 3)
                        b, h = i // RH, i % RH
                        e.wait_ge(s_new, i + 1)
                        for q in range(4):
                            o = psum[:, 4, (4 * h + q) * NS + b:(4 * h + q) * NS + b + 1]
                            for d in range(2):
                                m = e.matmul(o, sb[:, i % NB_, d, q * P:(q + 1) * P], qf[:, 2 * h + d, NP + b:NP + b + 1], start=d == 0, stop=d == 1)
                        m.then_inc(s_used, 1)
            stages.append(RetSample())
            rh_ = place("rh", [P, 16, T], F32R, at=R1)
            rl_ = place("rl", [P, 16, T], F32R, at=R0)
            Stat(vf, 4, 4, rstd4, lambda e, t: e.wait_ge(rsm_out, 1) if t == 0 else None)
            ag, dg = gated(vf, ACT.Silu)
            Linear(W, 8, KD, 2, by_cols(W, 9248), (xnh, xnl), act=ag, dve=dg)
            g_out = evicted()
            Apply(vf, 4, 4, rstd4, None, rh_, rl_, wait=all_of(g_out, lambda e: [e.wait_ge(sb_out[i], 16 * ((NS * RH - i + NB_ - 1) // NB_)) for i in range(NB_)] and None))
            residual(A["w_out_ab"][0], 16, 16, 1, by_rows(A["w_out_ab"][0], 16), [(yh, yl), (rh_, rl_)], 1.0, ready=xn_wait(), cpu=2)

        X = {n: sem_of("x_" + n) for n in ("mem_in", "score", "nmax", "exp", "prob", "pv", "oh", "ol", "qb", "kused", "smax", "sexp", "sprob",
                                           "spv", "soh", "sol")}
        kc_in = [sem_of("kc_in0"), sem_of("kc_in1")]
        vc_in = [sem_of(f"vc_in{i}") for i in range(2)]
        xbuf = None

        def cross_buffers():
            R = REG
            return dict(
                mtok=place("mtok", [P, 2, D], at=R), mT=place("mT", [P, KD, MEM], at=R + 8192),
                mh=place("mh", [P, KD, MEM], F32R, at=R + 16384), ml=place("ml", [P, KD, MEM], F32R, at=R + 24576),
                Kf=place("Kf", [P, KD, MEM], at=R + 32768), Vt=place("Vt", [P, 2, D], at=R + 40960),
                Kt=place("Kt", [P, 2, D], at=R + 49152), xq=place("xq", [P, KD, T], at=R + 57344),
                pp=place("pp", [P, 8, MEM], at=R + 65792), pT=place("pT", [P, XH, 512], at=R + 73984),
                qtm=place("qtm", [NS, 2, 512], at=R + 82176), sc=place("sc", [P, 2, 32], at=R + 86272),
                ps_=place("ps_", [32, MEM], at=R + 86528), pTs=place("pTs", [P, 64], at=R + 87552),
                st=place("st", [P, 4, 8], at=R + 87808), sst=place("sst", [32, 4], at=R + 87936),
                kc=place("kc", [P, 2, 2, D], at=R + 65792), vc=place("vc", [P, 2, 2, D], at=R))

        def cross(layer):
            nonlocal xbuf
            if xbuf is None:
                xbuf = cross_buffers()
            B = type("B", (), xbuf)
            lc = layer
            gcol = G_X + 8 * layer
            region_free = evicted()
            W = A["w_xkv"][layer]

            kept = pending[:]
            pending.clear()

            class Load(Stage):
                def pool(S, e):
                    region_free(e)
                    for q, n in kept:
                        e.wait_ge(q, n)
                    e.dma_start(B.mtok[:, :, :], A["mem_prompt"].rearrange("o (b p) d -> p (o b) d", p=P)).then_inc(X["mem_in"], 16)
                    for b in range(2):
                        load_k(e, b)

                def dve(S, e):
                    for q, n in kept:
                        e.wait_ge(q, n)
            stages.append(Load())

            def load_k(e, b):
                e.dma_start(B.kc[:, b % 2, :, :], A["cache_mem_k"][layer, b].rearrange("(m p) h d -> p m (h d)", p=P)).then_inc(kc_in[b % 2], 16)

            def load_v(e, b):
                e.dma_start(B.vc[:, b % 2, :, :], A["cache_mem_v"][layer, b].rearrange("(m p) h d -> p m (h d)", p=P)).then_inc(vc_in[b % 2], 16)

            norm_x(gcol)
            split_x = tot["app"] - KD
            mem_turn = behind(lambda: Turn([([(B.mtok[:, q % 2, (k + q // 2) * P:(k + q // 2 + 1) * P], P, P, q * P) for q in range(4)],
                lambda e, bank, par, k=k: mv(e, par, B.mT[:, k:k + 2, :], bank.rearrange("p (k n) -> p k n", k=2))) for k in range(0, KD, 2)],
                ready=at_least(X["mem_in"], 16 * (layer + 1))))
            mt = turned()
            mem_stat = behind(lambda: Stat(B.mT, 1, KD, rstd1, lambda e, t: mt(e) if t == 0 else None, n=MEM))
            mem_apply = behind(lambda: Apply(B.mT, 1, KD, rstd1, G_MEM + 8 * layer, B.mh, B.ml, n=MEM))
            mem_split = xn_wait()
            Wq = A["w_xq"][layer]
            Linear(Wq, 4, KD, 2, by_cols(Wq, 0), (xnh, xnl), kwise=split_x, dve=copy_out(B.xq), hooks={0: mem_turn, 1: mem_stat, 2: mem_apply})
            q_out = evicted()

            class FirstV(Stage):
                def pool(S, e):
                    mem_split(e)
                    for b in range(2):
                        load_v(e, b)
            stages.append(FirstV())
            q_turn = behind(lambda: Turn([([(B.xq[:, k, NP:T], P, NS, (k - k0) * P) for k in range(k0, k0 + 4)],
                lambda e, bank, par, k0=k0: mv(e, par, B.qtm[:, k0 // 4, :], bank[0:NS, :])) for k0 in (0, 4)], ready=q_out))
            qt_ready = turned()

            class SampleScores(Stage):
                def __init__(S, b):
                    S.b = b
                    S.bank = 4 + 2 * (b % 2)

                def pool(S, e):
                    b = S.b
                    if b + 2 < NS:
                        e.wait_ge(X["kused"], NS * lc + b + 1)
                        load_k(e, b + 2)

                def pe(S, e):
                    b = S.b
                    if b == 0:
                        qt_ready(e)
                    elif b >= 2:
                        e.wait_ge(X["kused"], NS * lc + b - 1)
                    for q in range(2):
                        m = e.matmul(psum[:, S.bank + q, :], ident[0:NS, b:b + 1].to_broadcast([NS, P]), B.qtm[:, q, :], start=True, stop=True)
                    m.then_inc(X["qb"], 1)

                def dve(S, e):
                    b = S.b
                    e.wait_ge(kc_in[b % 2], 16 * (4 * lc + b // 2 + 1))
                    e.wait_ge(X["qb"], NS * lc + b + 1)
                    for m_ in range(2):
                        for h in range(XH):
                            k = B.kc[:, b % 2, m_, h * XD:(h + 1) * XD]
                            ins = e.tensor_tensor_reduce(k, k, psum[:, S.bank + h // 2, (h % 2) * XD:(h % 2 + 1) * XD], XD ** -0.5, 0.0,
                                                         ALU.mult, ALU.add, B.sc[:, m_, b * XH + h:b * XH + h + 1])
                    ins.then_inc(X["kused"], 1)
            units = [SampleScores(b) for b in range(NS)]
            score_turn = behind(lambda: Turn([([(B.sc[:, m_, :], P, 32, m_ * P) for m_ in range(2)],
                lambda e, bank, par: mv(e, par, B.ps_[:, :], bank[0:32, 0:MEM]))], ready=at_least(X["kused"], NS * lc + NS)))
            s_ready = turned()
            Linear(W, 4, KD, 2, by_cols(W, 0), (B.mh, B.ml), kwise=tot["app"] - KD, dve=copy_out(B.Kf, n=MEM), cols=MEM,
                   hooks={0: q_turn + units[0:2], 1: units[2:4], 2: units[4:6], 3: units[6:8] + score_turn})
            k_out = evicted()

            def v_out(e, l, par, use):
                e.tensor_copy(B.Vt[:, :, bass.ds(l * 256, 256)], psum[:, 2 * par:2 * par + 2, 0:256]).then_inc(bank_free, 1)
            k_turn = behind(lambda: Turn([([(B.Kf[:, k0 + q, b * P:(b + 1) * P], P, P, q * P) for q in range(4)],
                lambda e, bank, par, b=b, k0=k0: mv(e, par, B.Kt[:, b, k0 * P:(k0 + 4) * P], bank)) for b in range(2) for k0 in (0, 4)], ready=k_out))
            kt_ready = turned()
            class SampleSoftmax(Stage):
                def dve(S, e):
                    s_ready(e)
                    link(e, "dve", e.tensor_reduce(B.sst[:, 0:1], B.ps_[:, :], AX, ALU.max))
                    e.tensor_scalar(B.sst[:, 1:2], B.sst[:, 0:1], -1.0, None, ALU.mult).then_inc(X["smax"], 1)
                    e.wait_ge(X["sexp"], lc + 1)
                    link(e, "dve", e.reciprocal(B.sst[:, 3:4], B.sst[:, 2:3]))
                    e.tensor_scalar(B.ps_[:, :], B.ps_[:, :], B.sst[:, 3:4], None, ALU.mult).then_inc(X["sprob"], 1)

                def act(S, e):
                    s_ready(e)
                    e.wait_ge(X["smax"], lc + 1)
                    nc.scalar.activation(B.ps_[:, :], B.ps_[:, :], ACT.Exp, bias=B.sst[:, 1:2], accum_out=B.sst[:, 2:3]).then_inc(X["sexp"], 1)
            prob_turn = behind(lambda: Turn([([(B.ps_[:, m_ * P:(m_ + 1) * P], 32, P, m_ * 32) for m_ in range(2)],
                lambda e, bank, par: mv(e, par, B.pTs[:, :], bank[:, 0:64]))], ready=at_least(X["sprob"], lc + 1)))
            ps_ready = turned()
            class SampleValues(Stage):
                def __init__(S, b0, b1):
                    S.b0, S.b1 = b0, b1

                def pool(S, e):
                    for b in range(S.b0, S.b1):
                        if b + 2 < NS:
                            e.wait_ge(X["spv"], NS * lc + b + 1)
                            load_v(e, b + 2)

                def pe(S, e):
                    ps_ready(e)
                    for b in range(S.b0, S.b1):
                        e.wait_ge(vc_in[b % 2], 16 * (4 * lc + b // 2 + 1))
                        for t in range(KD):
                            for m_ in range(2):
                                m = e.matmul(psum[:, 5, t * NS + b:t * NS + b + 1], B.vc[:, b % 2, m_, t * P:(t + 1) * P],
                                             B.pTs[:, m_ * 32 + b * XH + t // 2:m_ * 32 + b * XH + t // 2 + 1], start=m_ == 0, stop=m_ == 1)
                        m.then_inc(X["spv"], 1)

                def act(S, e):
                    if S.b1 < NS:
                        return
                    e.wait_ge(X["spv"], NS * lc + NS)
                    nc.scalar.activation(xnh[:, :, NP:T], psum[:, 5, 0:64].rearrange("p (t b) -> p t b", t=KD), ACT.Copy).then_inc(X["soh"], 1)

                def dve(S, e):
                    if S.b1 < NS:
                        return
                    e.wait_ge(X["soh"], lc + 1)
                    e.tensor_tensor(xnl[:, :, NP:T], psum[:, 5, 0:64].rearrange("p (t b) -> p t b", t=KD), xnh[:, :, NP:T].bitcast(F32),
                                    ALU.subtract).then_inc(X["sol"], 1)
            Linear(W, 4, KD, 2, by_cols(W, D), (B.mh, B.ml), dve=v_out, cols=256, turned=True,
                   hooks={0: k_turn + [SampleSoftmax()], 1: prob_turn + [SampleValues(0, 1)], 2: [SampleValues(1, 3)], 3: [SampleValues(3, 5)]})
            kv_out = evicted()

            class Keep(Stage):
                def pool(S, e):
                    kt_ready(e)
                    kv_out(e)
                    v = lambda o: o[layer, 0].rearrange("(b p) h d -> p b (h d)", p=P)
                    store(e, "pool", v(O[2]), B.Kt[:, :, :])
                    store(e, "pool", v(O[3]), B.Vt[:, :, :])
            stages.append(Keep())
            tot["stores"] += 32
            pending.append((stored["pool"], tot["stores"]))

            class Scores(Stage):
                def pe(S, e):
                    kv_out(e)
                    for u in range(8):
                        h, lb = u // 2, u % 2
                        if u >= 2:
                            e.wait_ge(X["exp"], 8 * lc + u - 1)
                        for d in range(2):
                            m = e.matmul(psum[:, u % 2, 0:MEM], B.xq[:, 2 * h + d, lb * P:(lb + 1) * P], B.Kf[:, 2 * h + d, :], start=d == 0, stop=d == 1)
                        m.then_inc(X["score"], 1)

                def dve(S, e):
                    for u in range(8):
                        e.wait_ge(X["score"], 8 * lc + u + 1)
                        link(e, "dve", e.tensor_reduce(B.st[:, 0, u:u + 1], psum[:, u % 2, 0:MEM], AX, ALU.max))
                        e.tensor_scalar(B.st[:, 1, u:u + 1], B.st[:, 0, u:u + 1], -XD ** -0.5, None, ALU.mult).then_inc(X["nmax"], 1)
                        if u >= 1:
                            S.divide(e, u - 1)
                    S.divide(e, 7)

                def divide(S, e, u):
                    e.wait_ge(X["exp"], 8 * lc + u + 1)
                    link(e, "dve", e.reciprocal(B.st[:, 3, u:u + 1], B.st[:, 2, u:u + 1]))
                    e.tensor_scalar(B.pp[:, u, :], B.pp[:, u, :], B.st[:, 3, u:u + 1], None, ALU.mult).then_inc(X["prob"], 1)

                def act(S, e):
                    for u in range(8):
                        e.wait_ge(X["nmax"], 8 * lc + u + 1)
                        nc.scalar.activation(B.pp[:, u, :], psum[:, u % 2, 0:MEM], ACT.Exp, scale=XD ** -0.5, bias=B.st[:, 1, u:u + 1],
                                             accum_out=B.st[:, 2, u:u + 1]).then_inc(X["exp"], 1)
            stages.append(Scores())
            stages.append(SampleValues(5, NS))
            Turn([([(B.pp[:, 2 * h + lb, m * P:(m + 1) * P], P, P, m * 256 + lb * P) for m in range(2) for lb in range(2)],
                   lambda e, bank, par, h=h: mv(e, par, B.pT[:, h, :], bank)) for h in range(XH)], ready=at_least(X["prob"], 8 * lc + 8))
            pt_ready = turned()
            class Values(Stage):
                def pe(S, e):
                    pt_ready(e)
                    for i in range(8):
                        if i >= 2:
                            e.wait_ge(X["ol"], 8 * lc + i - 1)
                        h, d = i // 2, i % 2
                        for m_ in range(2):
                            m = e.matmul(psum[:, 2 + i % 2, 0:NP], B.Vt[:, m_, h * XD + d * P:h * XD + (d + 1) * P], B.pT[:, h, m_ * 256:(m_ + 1) * 256],
                                         start=m_ == 0, stop=m_ == 1)
                        m.then_inc(X["pv"], 1)

                def act(S, e):
                    for i in range(8):
                        e.wait_ge(X["pv"], 8 * lc + i + 1)
                        nc.scalar.activation(xnh[:, i, 0:NP], psum[:, 2 + i % 2, 0:NP], ACT.Copy).then_inc(X["oh"], 1)

                def dve(S, e):
                    for i in range(8):
                        e.wait_ge(X["oh"], 8 * lc + i + 1)
                        e.tensor_tensor(xnl[:, i, 0:NP], psum[:, 2 + i % 2, 0:NP], xnh[:, i, 0:NP].bitcast(F32), ALU.subtract).then_inc(X["ol"], 1)
            stages.append(Values())

            Wo = A["w_xo"][layer]
            residual(Wo, 4, KD, 2, by_cols(Wo, 0), (xnh, xnl), 1.0, ready=all_of(at_least(X["sol"], lc + 1), at_least(X["ol"], 8 * lc + 8)))

        def mixer_c():
            W = A["w_in_c"][0]
            R = REG
            q = place("cq", [P, 4, T], at=R)
            k = place("ck", [P, 4, T], at=R + 4 * T * 4)
            v = place("cv", [P, 8, T], at=R + 8 * T * 4)
            R2 = R + 16 * T * 4
            ktm = place("cktm", [P, 2, 512], at=R2)
            vtm = place("cvtm", [P, 2, 1024], at=R2 + 4096)
            qk = place("cqk", [P, 4, 384], at=R2 + 12288)
            ee = place("cee", [P, 4, 384], at=R2 + 18432)
            gcs = place("cgcs", [P, 4, 4], at=R2 + 24576)
            den = place("cden", [P, 4, NP], at=R2 + 24640)
            cst = place("ccst", [P, 4, 256], at=R2 + 28736)
            nst = place("cnst", [P, 4], at=R2 + 32832)
            vsr = place("cvs", [NS, 1024], at=R2 + 32864)
            cb = place("ccb", [P, 4, 4, 256], at=R2 + 36960)
            fib = place("cfib", [P, 4, 24], at=R2 + 53344)
            ki = place("cki", [P, 4, NS], at=R2 + 53728)
            nT = place("cnT", [P, NS, 4], at=R2 + 53856)
            qn = place("cqn", [P, NS, 4], at=R2 + 53984)
            dn = place("cdn", [P, NS, 4], at=R2 + 54112)
            nrow = place("cnrow", [32, P], at=R2 + 54240)
            gr = place("cgr", [4, 8, T], at=R2 + 54752)
            sm = place("csm", [4, 6, NS], at=R2 + 54752 + 8448)
            mtok2 = sem_of("c_in")
            n_in = sem_of("c_n_in")
            S_ = {n: sem_of("c_" + n) for n in ("gates", "abs", "ln", "rows", "wl", "srow", "sexp", "fi", "qk", "qkm", "bc", "ebc", "gap", "exp", "att",
                                                 "den", "guard", "rden", "num", "hh", "st", "stc", "sts", "n_new", "qn", "dns", "vb", "dec", "cnew",
                                                 "cused", "hs", "bgd", "kib")}
            region_free = evicted()

            class Load(Stage):
                def pool(S, e):
                    region_free(e)
                    with nc.allow_non_contiguous_dma(reason="a few numbers, one on each partition"):
                        e.dma_start(cols[0:4, 44:45], A["mlstm_i_bias"].rearrange("l h -> h l")).then_inc(mtok2, 16)
                        e.dma_start(cols[0:4, 45:46], A["mlstm_f_bias"].rearrange("l h -> h l")).then_inc(mtok2, 16)
                        e.dma_start(sm[:, 0, :], A["state_mlstm_m"][0].rearrange("b h -> h b")).then_inc(mtok2, 16)
                    e.dma_start(nrow[:, :], A["state_mlstm_n"].rearrange("l b h d -> (l b h) d")).then_inc(n_in, 16)
            stages.append(Load())
            after_norm(W, 2, by_cols(W, 0), dve=copy_out(q))
            Linear(W, 2, KD, 2, by_cols(W, 512), (xnh, xnl), dve=copy_out(k, MDK ** -0.5))
            Linear(W, 4, KD, 2, by_cols(W, 1024), (xnh, xnl), dve=copy_out(v))

            def gates(e, l, par, use):
                e.wait_ge(mtok2, 48)
                e.tensor_scalar(gr[:, 0, :], psum[0:4, 2 * par, 0:T], cols[0:4, 44:45], None, ALU.add)
                e.tensor_scalar(gr[:, 1, :], psum[0:4, 2 * par + 1, 0:T], cols[0:4, 45:46], None, ALU.add).then_inc(bank_free, 1)
            Linear(W, 1, KD, 2, two_cols(W, 2048, 2052), (xnh, xnl), dve=gates)
            in_out = evicted()

            class Rows(Stage):
                def dve(S, e):
                    go = lambda ins: link(e, "dve", ins)
                    in_out(e)
                    e.scalar_tensor_tensor(out=gr[:, 2, :], in0=gr[:, 1, :], scalar=-1.0, in1=gr[:, 1, :], op0=ALU.mult, op1=ALU.max).then_inc(S_["abs"], 1)
                    e.wait_ge(S_["ln"], 1)
                    go(e.scalar_tensor_tensor(out=gr[:, 3, :], in0=gr[:, 1, :], scalar=0.0, in1=gr[:, 2, :], op0=ALU.min, op1=ALU.subtract))
                    c = slice(0, NP)
                    go(e.tensor_tensor_scan(gr[:, 4, 0:P], ones[0:4, :], gr[:, 3, 0:P], 0.0, ALU.mult, ALU.add))
                    go(e.tensor_tensor_scan(gr[:, 4, P:NP], ones[0:4, :], gr[:, 3, P:NP], gr[:, 4, P - 1:P], ALU.mult, ALU.add))
                    go(e.tensor_tensor(gr[:, 5, c], gr[:, 0, c], gr[:, 4, c], ALU.subtract))
                    go(e.tensor_tensor_scan(gr[:, 2, c], gr[:, 5, c], gr[:, 5, c], 0.0, ALU.max, ALU.max))
                    go(e.tensor_scalar(gr[:, 6, c], gr[:, 2, c], -1.0, None, ALU.mult))
                    go(e.tensor_tensor(gr[:, 7, c], gr[:, 6, c], gr[:, 4, c], ALU.subtract))
                    e.tensor_scalar(cols[0:4, 46:47], gr[:, 7, NP - 1:NP], -1.0, None, ALU.mult).then_inc(S_["rows"], 1)
                    go(e.tensor_tensor(sm[:, 1, :], gr[:, 3, NP:T], sm[:, 0, :], ALU.add))
                    go(e.tensor_tensor(sm[:, 2, :], sm[:, 1, :], gr[:, 0, NP:T], ALU.max))
                    go(e.tensor_tensor(sm[:, 3, :], sm[:, 1, :], sm[:, 2, :], ALU.subtract))
                    go(e.tensor_tensor(sm[:, 4, :], gr[:, 0, NP:T], sm[:, 2, :], ALU.subtract))
                    e.tensor_scalar(sm[:, 5, :], sm[:, 2, :], -1.0, None, ALU.mult).then_inc(S_["srow"], 1)

                def act(S, e):
                    e.wait_ge(S_["abs"], 1)
                    link(e, "act", nc.scalar.activation(gr[:, 2, :], gr[:, 2, :], ACT.Exp, scale=-1.0))
                    nc.scalar.activation(gr[:, 2, :], gr[:, 2, :], ACT.Ln, bias=1.0).then_inc(S_["ln"], 1)
                    e.wait_ge(S_["rows"], 1)
                    nc.scalar.activation(gr[:, 1, 0:NP], gr[:, 5, 0:NP], ACT.Exp, bias=gr[:, 6, NP - 1:NP]).then_inc(S_["wl"], 1)
                    e.wait_ge(S_["srow"], 1)
                    nc.scalar.activation(sm[:, 3:6, :], sm[:, 3:6, :], ACT.Exp).then_inc(S_["sexp"], 1)

                def pool(S, e):
                    e.wait_ge(S_["srow"], 1)
                    with nc.allow_non_contiguous_dma(reason="the stabilisers: 36 numbers"):
                        store(e, "pool", O[14].rearrange("l o h -> (l h) o"), cols[0:4, 46:47])
                        store(e, "pool", O[15][0].rearrange("b h -> h b"), sm[:, 2, :])
            stages.append(Rows())
            gitem = [([(src, 4, P, j * 4) for j, src in enumerate((gr[:, 5, 0:P], gr[:, 5, P:NP], gr[:, 1, 0:P], gr[:, 1, P:NP]))],
                      lambda e, bank, par: mv(e, par, gcs[:, :, :], bank[:, 0:16].rearrange("p (j h) -> p j h", j=4)))]
            Turn(gitem, ready=at_least(S_["wl"], 1))
            g_ready = turned()
            four = lambda t, j: [(t[:, j + i // 2, (i % 2) * P:(i % 2 + 1) * P], P, P, (i % 2) * 256 + (i // 2) * P) for i in range(4)]
            items = []
            for h in (0, 2):
                def ev(e, bank, par, h=h):
                    for b in range(2):
                        for i in range(2):
                            c = (h + i) * P
                            ins = mv(e, par, ktm[:, b, c:c + P], bank[:, b * 256 + i * P:b * 256 + (i + 1) * P], scale=gcs[:, 2 + b, h + i:h + i + 1])
                    return ins
                items.append((four(k, h), ev))
            for t in range(0, 8, 2):
                items.append((four(v, t), lambda e, bank, par, t=t: mv(e, par, vtm[:, :, t * P:(t + 2) * P], bank.rearrange("p (b n) -> p b n", b=2))))
            for t0 in (0, 4):
                items.append(([(v[:, t, NP:T], P, NS, (t - t0) * P) for t in range(t0, t0 + 4)],
                              lambda e, bank, par, t0=t0: mv(e, par, vsr[:, t0 * P:(t0 + 4) * P], bank[0:NS, :])))
            items.append(([(nrow[:, :], 32, P, 0)], lambda e, bank, par: mv(e, par, nT[:, :, :], bank[:, 0:32].rearrange("p (b h) -> p b h", b=NS))))
            Turn(items, ready=at_least(n_in, 16), act_ready=g_ready, dve_ready=g_ready)
            t_ready = turned()

            class Prompt(Stage):
                def pe(S, e):
                    t_ready(e)
                    e.wait_ge(S_["sexp"], 1)
                    for h in range(MH):
                        if h >= 2:
                            e.wait_ge(S_["qkm"], h - 1)
                            e.wait_ge(S_["ebc"], h - 1)
                        e.matmul(psum[:, h % 2, 0:NP], k[:, h, 0:P], q[:, h, 0:NP], start=True, stop=True)
                        e.matmul(psum[:, h % 2, NP:384], k[:, h, P:NP], q[:, h, P:NP], start=True, stop=True).then_inc(S_["qk"], 1)
                        for j in range(2):
                            m = e.matmul(psum[:, 2 + h % 2, j * NP:(j + 1) * NP], ident[0:4, h:h + 1].to_broadcast([4, P]), gr[:, 6 + j, 0:NP], start=True, stop=True)
                        m.then_inc(S_["bc"], 1)
                    e.wait_ge(S_["qkm"], 4)
                    for h in range(MH):
                        e.wait_ge(S_["att"], h + 1)
                        if h >= 1:
                            e.wait_ge(S_["rden"], h)
                            e.wait_ge(S_["hh"], h)
                        e.matmul(psum[:, 4, 0:NP], ones[:, :], ee[:, h, 0:NP], start=True, stop=False)
                        e.matmul(psum[:, 4, P:NP], ones[:, :], ee[:, h, NP:384], start=False, stop=True).then_inc(S_["den"], 1)
                        for i in range(2):
                            c = h * MDV + i * P
                            o = psum[:, 5, i * NP:(i + 1) * NP]
                            e.matmul(o, vtm[:, 0, c:c + P], ee[:, h, 0:NP], start=True, stop=False)
                            m = e.matmul(o[:, P:NP], vtm[:, 1, c:c + P], ee[:, h, NP:384], start=False, stop=True)
                        m.then_inc(S_["num"], 1)
                    for h in range(MH):
                        if h >= 2:
                            e.wait_ge(S_["stc"], h - 1)
                        for b in range(2):
                            e.matmul(psum[:, h % 2, 0:256], ktm[:, b, h * P:(h + 1) * P], vtm[:, b, h * MDV:(h + 1) * MDV], start=b == 0, stop=b == 1)
                        for b in range(2):
                            m = e.matmul(psum[:, h % 2, 256:257], ktm[:, b, h * P:(h + 1) * P], ones[:, 0:1], start=b == 0, stop=b == 1)
                        m.then_inc(S_["st"], 1)
                    for h in range(MH):
                        m = e.matmul(psum[:, 2, h * 24:(h + 1) * 24], ident[0:4, h:h + 1].to_broadcast([4, P]), sm[:, 3:6, :].rearrange("h q b -> h (q b)"), start=True, stop=True)
                    m.then_inc(S_["fi"], 1)

                def dve(S, e):
                    t_ready(e)
                    for h in range(MH):
                        e.wait_ge(S_["qk"], h + 1)
                        e.tensor_tensor(qk[:, h, :], psum[:, h % 2, 0:384], mask[:, :], ALU.mult).then_inc(S_["qkm"], 1)
                        e.wait_ge(S_["bc"], h + 1)
                        e.tensor_scalar(ee[:, h, 0:NP], psum[:, 2 + h % 2, 0:NP], gcs[:, 0, h:h + 1], 0.0, ALU.add, ALU.min)
                        e.tensor_scalar(ee[:, h, NP:384], psum[:, 2 + h % 2, P:NP], gcs[:, 1, h:h + 1], 0.0, ALU.add, ALU.min).then_inc(S_["gap"], 1)
                    for h in range(MH):
                        e.wait_ge(S_["exp"], h + 1)
                        if h == 0:
                            e.wait_ge(S_["qkm"], 4)
                        e.tensor_tensor(ee[:, h, :], ee[:, h, :], qk[:, h, :], ALU.mult).then_inc(S_["att"], 1)
                    for h in range(MH):
                        e.wait_ge(S_["guard"], h + 1)
                        go = lambda ins: link(e, "dve", ins)
                        d = psum[:, 4, 0:NP]
                        go(e.tensor_tensor(ms[:, 0:NP], d, den[:, h, :], ALU.max))
                        e.scalar_tensor_tensor(out=den[:, h, :], in0=d, scalar=-1.0, in1=ms[:, 0:NP], op0=ALU.mult, op1=ALU.max).then_inc(S_["rden"], 1)
                        e.wait_ge(S_["rden"], h + 1)
                        go(e.reciprocal(den[:, h, :], den[:, h, :]))
                        e.wait_ge(S_["num"], h + 1)
                        e.tensor_tensor(v[:, 2 * h:2 * h + 2, 0:NP], psum[:, 5, :].rearrange("p (i n) -> p i n", i=2),
                                        den[:, h, :].unsqueeze(1).to_broadcast([P, 2, NP]), ALU.mult).then_inc(S_["hh"], 1)

                def act(S, e):
                    for h in range(MH):
                        e.wait_ge(S_["gap"], h + 1)
                        nc.scalar.activation(ee[:, h, :], ee[:, h, :], ACT.Exp).then_inc(S_["exp"], 1)
                        nc.scalar.activation(den[:, h, :], psum[:, 2 + h % 2, NP:512], ACT.Exp).then_inc(S_["ebc"], 1)
                    e.wait_ge(S_["ebc"], 4)
                    for h in range(MH):
                        e.wait_ge(S_["den"], h + 1)
                        nc.scalar.activation(nst[:, h:h + 1], ones[:, 0:1], ACT.Copy).then_inc(S_["guard"], 1)
                    for h in range(MH):
                        e.wait_ge(S_["st"], h + 1)
                        if h == 0:
                            e.wait_ge(S_["guard"], 4)
                        nc.scalar.activation(cst[:, h, :], psum[:, h % 2, 0:256], ACT.Copy)
                        nc.scalar.activation(nst[:, h:h + 1], psum[:, h % 2, 256:257], ACT.Copy).then_inc(S_["stc"], 1)
                    e.wait_ge(S_["fi"], 1)
                    nc.scalar.activation(fib[:, :, :], psum[:, 2, 0:96].rearrange("p (h q) -> p h q", h=4), ACT.Copy).then_inc(S_["bgd"], 1)

                def pool(S, e):
                    e.wait_ge(S_["stc"], 4)
                    store(e, "pool", O[10][0, 0].rearrange("h d e -> d h e"), cst[:, :, :])
                    with nc.allow_non_contiguous_dma(reason="the prompt's n: 512 numbers"):
                        store(e, "pool", O[12][0, 0].rearrange("h d -> d h"), nst[:, :])
            stages.append(Prompt())
            cin, cout, was = s_in[0:4], s_out[0:4], ret_moves
            cview = lambda t, b: t[0, b].rearrange("h d e -> d h e")
            tot["stores"] += 80
            pending.extend([(stored["pool"], tot["stores"])] + [(c, n + 32) for c, n in zip(cout, was)])

            class SampleN(Stage):
                def dve(S, e):
                    go = lambda ins: link(e, "dve", ins)
                    e.wait_ge(S_["bgd"], 1)
                    hb_ = lambda j: fib[:, :, j * NS:(j + 1) * NS]
                    go(e.tensor_tensor(ki[:, :, :], k[:, :, NP:T], hb_(1), ALU.mult))
                    go(e.tensor_tensor(nT[:, :, :], nT[:, :, :], hb_(0).rearrange("p h b -> p b h"), ALU.mult))
                    e.tensor_tensor(nT[:, :, :], nT[:, :, :], ki[:, :, :].rearrange("p h b -> p b h"), ALU.add).then_inc(S_["n_new"], 1)
                    e.wait_ge(S_["n_new"], 1)
                    e.tensor_tensor(qn[:, :, :], nT[:, :, :], q[:, :, NP:T].rearrange("p h b -> p b h"), ALU.mult).then_inc(S_["qn"], 1)
                    e.wait_ge(S_["dns"], 1)
                    d = psum[:, 2, 128:160].rearrange("p (b h) -> p b h", b=NS)
                    go(e.tensor_tensor(dn[:, :, :], d, hb_(2).rearrange("p h b -> p b h"), ALU.max))
                    go(e.scalar_tensor_tensor(out=dn[:, :, :], in0=d, scalar=-1.0, in1=dn[:, :, :], op0=ALU.mult, op1=ALU.max))
                    go(e.reciprocal(dn[:, :, :], dn[:, :, :]))

                def pe(S, e):
                    e.wait_ge(S_["qn"], 1)
                    e.wait_ge(S_["bgd"], 1)
                    e.matmul(psum[:, 2, 128:160], ones[:, :], qn[:, :, :].rearrange("p b h -> p (b h)"), start=True, stop=True).then_inc(S_["dns"], 1)

                def pool(S, e):
                    for b in range(4):
                        e.dma_start(cb[:, b, :, :], cview(A["state_mlstm_c"], b)).then_inc(cin[b], 16)
            stages.append(SampleN())
            Turn([([(nT[:, :, :].rearrange("p b h -> p (b h)"), P, 32, 0)], lambda e, bank, par: mv(e, par, nrow[:, :], bank[0:32, 0:P]))],
                 ready=at_least(S_["n_new"], 1))
            nr_ready = turned()

            class SampleC(Stage):
                def pool(S, e):
                    nr_ready(e)
                    store(e, "pool", O[13].rearrange("l b h d -> (l b h) d"), nrow[:, :])
                    for b in range(4, NS):
                        e.wait_ge(cout[b % 4], was[b % 4] + 16)
                        e.wait_ge(S_["cused"], b - 3)
                        e.dma_start(cb[:, b % 4, :, :], cview(A["state_mlstm_c"], b)).then_inc(cin[b % 4], 16)

                def act(S, e):
                    e.wait_ge(S_["bgd"], 1)
                    for b in range(NS):
                        e.wait_ge(cin[b % 4], was[b % 4] + 16 * (b // 4 + 1))
                        for h in range(MH):
                            c = cb[:, b % 4, h, :]
                            ins = nc.scalar.activation(c, c, ACT.Copy, scale=fib[:, h, b:b + 1])
                        ins.then_inc(S_["dec"], 1)
                        if b >= 1:
                            S.keep(e, b - 1)
                    S.keep(e, NS - 1)

                def keep(S, e, b):
                    e.wait_ge(S_["cnew"], b + 1)
                    e.dma_start(cview(O[11], b), cb[:, b % 4, :, :]).then_inc(cout[b % 4], 16)

                def bank(S, b):
                    return 4 * (b % 2)

                def pe(S, e):
                    e.wait_ge(S_["stc"], 4)
                    e.wait_ge(S_["hh"], 4)

                    def bc(b):
                        if b >= 2:
                            e.wait_ge(S_["cnew"], b - 1)
                        for j in range(2):
                            m = e.matmul(psum[:, S.bank(b) + j, :], ident[0:NS, b:b + 1].to_broadcast([NS, P]), vsr[:, j * 512:(j + 1) * 512], start=True, stop=True)
                        m.then_inc(S_["vb"], 1)
                    bc(0)
                    bc(1)
                    for b in range(NS):
                        e.wait_ge(S_["cnew"], b + 1)
                        for h in range(MH):
                            for i in range(2):
                                t = (2 * h + i) * NS + b
                                m = e.matmul(psum[:, 3, t:t + 1], cb[:, b % 4, h, i * P:(i + 1) * P], q[:, h, NP + b:NP + b + 1], start=True, stop=True)
                        m.then_inc(S_["cused"], 1)
                        if b + 2 < NS:
                            bc(b + 2)

                def dve(S, e):
                    for b in range(NS):
                        e.wait_ge(S_["dec"], b + 1)
                        e.wait_ge(S_["vb"], b + 1)
                        for h in range(MH):
                            c = cb[:, b % 4, h, :]
                            ins = e.scalar_tensor_tensor(out=c, in0=psum[:, S.bank(b) + h // 2, (h % 2) * 256:(h % 2 + 1) * 256],
                                                         scalar=ki[:, h, b:b + 1], in1=c, op0=ALU.mult, op1=ALU.add)
                        ins.then_inc(S_["cnew"], 1)
                    e.wait_ge(S_["cused"], NS)
                    for i in range(2):
                        ins = e.tensor_tensor(v[:, i:8:2, NP:T], psum[:, 3, 0:64].rearrange("p (h i b) -> p h i b", h=4, i=2)[:, :, i, :],
                                              dn[:, :, :].rearrange("p b h -> p h b"), ALU.mult)
                    ins.then_inc(S_["hs"], 1)
            stages.append(SampleC())
            Stat(v, 4, 2, rstd4, lambda e, t: e.wait_ge(S_["hs"], 1) if t == 0 else None)
            ao, do = gated(v, ACT.Sigmoid)
            Linear(W, 4, KD, 2, by_cols(W, 2056), (xnh, xnl), act=ao, dve=do)
            o_out = evicted()
            Apply(v, 4, 2, rstd4, G_M, xnh, xnl, wait=o_out)
            Wo = A["w_out_c"][0]
            residual(Wo, 4, KD, 2, by_cols(Wo, 0), (xnh, xnl), 1.0, ready=xn_wait())

        for layer in range(2):
            if layer == 0:
                u = None
                Stat(x, 1, KD, rstd1, lambda e, t: x_ready(e) if t == 0 else None)
                Apply(x, 1, KD, rstd1, G_FFN1, xnh, xnl)
            else:
                norm_x(G_FFN1 + 8 * layer)
            ffn(layer, A["w_ffn1_in"][layer], A["w_ffn1_out"][layer])
            norm_x(G_MIX + 8 * layer)
            (mixer_ab if layer == 0 else mixer_c)()
            cross(layer)
            norm_x(G_FFN2 + 8 * layer)
            ffn(layer, A["w_ffn2_in"][layer], A["w_ffn2_out"][layer])

        yT = place("yT", [P, KD, T], at=REG)
        ytok = place("ytok", [P, 2, D], at=REG + 8448)
        ystok = place("ystok", [NS, D], at=REG + 8448 + 8192)
        norm_x(G_FIN, hi=None, lo=None, out=yT)
        y_scaled = sem_of("y_scaled")

        class Mark(Stage):
            def dve(S, e):
                nc.vector.memset(ms[:, 0:1], 0.0).then_inc(y_scaled, 1)
        stages.append(Mark())
        src = yT
        items = []
        for b in range(2):
            for k0 in (0, 4):
                items.append(([(src[:, k, b * P:(b + 1) * P], P, P, (k - k0) * P) for k in range(k0, k0 + 4)],
                              lambda e, bank, par, b=b, k0=k0: mv(e, par, ytok[:, b, k0 * P:(k0 + 4) * P], bank)))
        for k0 in (0, 4):
            items.append(([(src[:, k, NP:T], P, NS, (k - k0) * P) for k in range(k0, k0 + 4)],
                          lambda e, bank, par, k0=k0: mv(e, par, ystok[:, k0 * P:(k0 + 4) * P], bank[0:NS, :])))
        Turn(items, ready=lambda e: e.wait_ge(y_scaled, 1))
        y_out = turned()

        class Final(Stage):
            def sp(S, e):
                y_out(e)
                store(e, "sp", O[0].rearrange("o (b p) d -> p (o b) d", p=P), ytok[:, :, :])
                store(e, "sp", O[1].rearrange("b o d -> (b o) d"), ystok[:, :])
        stages.append(Final())

        block = ctx.enter_context(nc.Block())

        @block.tensor
        def _(pe):
            for s in stages:
                s.pe(pe)

        @block.scalar
        def _(act):
            for s in stages:
                s.act(act)

        @block.vector
        def _(dve):
            for s in stages:
                s.dve(dve)

        @block.gpsimd
        def _(pool):
            for s in stages:
                s.pool(pool)

        @block.sync
        def _(sp):
            for s in stages:
                s.sp(sp)
            for q in stored:
                if stores[q]:
                    assert q == "sp" or stores[q] == tot["stores"]
                    sp.wait_ge(stored[q], stores[q])


OUTS = [(1, NP, D), (NS, 1, D), (2, 1, MEM, XH, XD), (2, 1, MEM, XH, XD), (1, 1, 3, CONV_CH), (1, NS, 3, CONV_CH),
        (1, 1, SSD_HEADS, SSD_P, SSD_N), (1, NS, SSD_HEADS, SSD_P, SSD_N), (1, 1, RH, RDK, RDV), (1, NS, RH, RDK, RDV),
        (1, 1, MH, MDK, MDV), (1, NS, MH, MDK, MDV), (1, 1, MH, MDK), (1, NS, MH, MDK), (1, 1, MH), (1, NS, MH)]
PAST_LEN = 2048


def constants():
    s, t = np.arange(P)[:, None], np.arange(P)[None, :]
    upper = (s <= t).astype(np.float32)
    mask = np.concatenate([upper, np.ones((P, P), np.float32), upper], 1)
    half = RDK // 2
    inv = np.exp(np.float32(-np.log(10000.0)) * np.arange(half, dtype=np.float32) / np.float32(half)).astype(np.float32)
    pos = np.concatenate([np.arange(NP), np.full(NS, PAST_LEN)]).astype(np.float32)
    ang = (inv[:, None] * pos[None, :]).astype(np.float64)
    c, sn = np.cos(ang), np.sin(ang)
    rot = np.stack([c, sn, c * RDK ** -0.5, sn * RDK ** -0.5], 1).astype(np.float32)
    lg = np.log1p(-np.exp2(-5.0 - np.arange(RH)))
    diff = np.arange(NP)[None, :] - np.arange(P)[:, None]
    dtab = np.stack([np.where(diff >= 0, np.exp(np.maximum(diff, 0) * g), 0.0) for g in lg], 1).astype(np.float32)
    end = np.stack([np.exp((NP - 1 - b * P - np.arange(P)) * g) for g in lg for b in range(2)], 1).astype(np.float32)
    return {"c_ident": np.eye(P, dtype=np.float32), "c_mask": mask, "c_rot": rot, "c_dtab": dtab, "c_tail": end}


def kernel(**inputs):
    import concourse.bacc as bacc
    from concourse.bass_utils import run_bass_kernel_spmd

    nc = bacc.Bacc("TRN2", target_bir_lowering=False, num_devices=1)
    arrays, A = {}, {}
    for name, a in {**inputs, **constants()}.items():
        a = np.ascontiguousarray(a)
        arrays[f"in_{name}"] = a
        A[name] = nc.dram_tensor(f"in_{name}", a.shape, mybir.dt.from_np(a.dtype), kind="ExternalInput").ap()
    O = [nc.dram_tensor(f"out_{i}", shape, F32, kind="ExternalOutput").ap() for i, shape in enumerate(OUTS)]
    build(nc, A, O)
    r = run_bass_kernel_spmd(nc, [arrays], core_ids=[0])
    return tuple(r.results[0][f"out_{i}"] for i in range(len(OUTS)))
```
